# Optimizing a Trainium2 kernel written in Bass

```python
import math
import jax
import jax.numpy as jnp
from jax import lax
import numpy as np

D_MODEL = 1024
BATCH = 1
SEQ = 512
DEPTH = 2

GRID_W = 64
CTX_LEN = 256
EPS = 1e-6

RET_HEADS = 8
RET_DV = D_MODEL // RET_HEADS
RET_DK = RET_DV // 2
RET_CHUNK = 128
ROPE_BASE = 10000.0

CONF_WIDTH = D_MODEL // 2
CONF_TAPS = 31

HY_WIDTH = D_MODEL // 2
HY_ORDER = 2
HY_SHORT_TAPS = 3
HY_BANDS = 16
HY_EMB = 2 * HY_BANDS + 1
HY_HIDDEN = 64
HY_DECAY_SHORT_PCT = 0.3
HY_DECAY_LONG_PCT = 1.5
HY_DECAY_TARGET = 1e-2

PEER_HEADS = 8
PEER_NKEYS = 128
PEER_EXPERTS = PEER_NKEYS * PEER_NKEYS
PEER_DKEY = D_MODEL // PEER_HEADS
PEER_TOPK = 16
PEER_TOKEN_BLOCK = 128

N_BRANCH = 3
OFF_Q = 0
OFF_K = OFF_Q + RET_HEADS * RET_DK
OFF_V = OFF_K + RET_HEADS * RET_DK
OFF_G = OFF_V + RET_HEADS * RET_DV
OFF_CONF = OFF_G + RET_HEADS * RET_DV
OFF_HY = OFF_CONF + 2 * CONF_WIDTH
OFF_GATE = OFF_HY + (HY_ORDER + 1) * HY_WIDTH
IN_COLS = OFF_GATE + N_BRANCH * D_MODEL

kernel_name = "hybrid_retention_conformer_hyena_peer_dit"

def rms_norm(x, gain):
    xf = x.astype(jnp.float32)
    y = xf * lax.rsqrt(jnp.mean(xf * xf, axis=-1, keepdims=True) + EPS)
    return (y * gain.astype(jnp.float32)).astype(x.dtype)

def modulate(h, shift, scale):
    return h * (1 + scale) + shift

def adaln(cvec, w, b):
    m = (jax.nn.silu(cvec) @ w + b)[:, None, :]
    return jnp.split(m, 6, axis=-1)

def depthwise_conv(x, w, b):
    taps = w.shape[0]
    left = (taps - 1) // 2
    y = lax.conv_general_dilated(
        x, w[:, None, :].astype(x.dtype), window_strides=(1,),
        padding=[(left, taps - 1 - left)],
        dimension_numbers=('NWC', 'WIO', 'NWC'),
        feature_group_count=x.shape[-1])
    return y + b.astype(x.dtype)

def split_heads(a, d):
    return a.astype(jnp.float32).reshape(a.shape[0], a.shape[1], -1, d)

def grid_rope_angles(rows):
    rr, cc = jnp.meshgrid(jnp.arange(rows, dtype=jnp.float32),
                          jnp.arange(GRID_W, dtype=jnp.float32), indexing='ij')
    row = rr.reshape(-1)
    col = cc.reshape(-1)
    n_freq = RET_DK // 4
    inv = ROPE_BASE ** (-jnp.arange(n_freq, dtype=jnp.float32) / n_freq)
    ang = jnp.concatenate([row[:, None] * inv, col[:, None] * inv], axis=-1)
    return jnp.cos(ang), jnp.sin(ang)

def apply_rope(x, cos, sin):
    xp = x.reshape(x.shape[:-1] + (-1, 2))
    x0, x1 = xp[..., 0], xp[..., 1]
    c = cos[None, :, None, :]
    s = sin[None, :, None, :]
    return jnp.stack([x0 * c - x1 * s, x0 * s + x1 * c], axis=-1).reshape(x.shape)

def retention_chunkwise(q, k, v, log_g, s0):
    B, L, H, dk = q.shape
    dv = v.shape[-1]
    C = RET_CHUNK
    n = L // C
    qc = q.reshape(B, n, C, H, dk)
    kc = k.reshape(B, n, C, H, dk)
    vc = v.reshape(B, n, C, H, dv)
    idx = jnp.arange(C, dtype=jnp.float32)
    diff = idx[:, None] - idx[None, :]
    dmask = jnp.where(diff[None] >= 0,
                      jnp.exp(jnp.maximum(diff, 0.0)[None] * log_g[:, None, None]), 0.0)
    scores = jnp.einsum('bnihd,bnjhd->bnhij', qc, kc) * dmask
    intra = jnp.einsum('bnhij,bnjhe->bnihe', scores, vc)
    k_dec = kc * jnp.exp((C - 1 - idx)[:, None] * log_g[None, :])[:, :, None]
    chunk_kv = jnp.einsum('bnjhd,bnjhe->nbhde', k_dec, vc)
    g_chunk = jnp.exp(C * log_g)[None, :, None, None]

    def step(s, kv):
        return g_chunk * s + kv, s

    _, s_before = lax.scan(step, s0, chunk_kv)
    q_dec = qc * jnp.exp((idx + 1)[:, None] * log_g[None, :])[:, :, None]
    cross = jnp.einsum('bnihd,nbhde->bnihe', q_dec, s_before)
    return (intra + cross).reshape(B, L, H, dv)

def retention_final_states(k, v, log_g):
    L = k.shape[1]
    t = jnp.arange(L, dtype=jnp.float32)
    wf = jnp.exp((L - 1 - t)[:, None] * log_g[0][None, :])
    wb = jnp.exp(t[:, None] * log_g[1][None, :])
    s_f = jnp.einsum('blhd,lh,blhe->bhde', k, wf, v)
    s_b = jnp.einsum('blhd,lh,blhe->bhde', k, wb, v)
    return s_f, s_b

def bidir_retention(q, k, v, log_g, s0_f, s0_b):
    o_f = retention_chunkwise(q, k, v, log_g[0], s0_f)
    fl = lambda a: jnp.flip(a, axis=1)
    o_b = fl(retention_chunkwise(fl(q), fl(k), fl(v), log_g[1], s0_b))
    return o_f + o_b

def retention_branch(q, k, v, g, s0_f, s0_b, lp):
    o = bidir_retention(q, k, v, lp['log_g'], s0_f, s0_b)
    mu = jnp.mean(o, axis=-1, keepdims=True)
    var = jnp.mean(jnp.square(o - mu), axis=-1, keepdims=True)
    o = (o - mu) * lax.rsqrt(var + EPS)
    o = o.reshape(o.shape[0], o.shape[1], -1) * lp['ret_gn_g'].astype(jnp.float32)
    return (o.astype(g.dtype) * jax.nn.silu(g)) @ lp['w_br_ret']

def conformer_branch(pc, lp):
    a, b = jnp.split(pc, 2, axis=-1)
    h = depthwise_conv(a * jax.nn.sigmoid(b), lp['conf_dw_w'], lp['conf_dw_b'])
    hf = h.astype(jnp.float32)
    mu = jnp.mean(hf, axis=-1, keepdims=True)
    var = jnp.mean(jnp.square(hf - mu), axis=-1, keepdims=True)
    hn = (hf - mu) * lax.rsqrt(var + EPS) * lp['conf_ln_g'].astype(jnp.float32) + lp['conf_ln_b'].astype(jnp.float32)
    return jax.nn.silu(hn).astype(pc.dtype) @ lp['w_br_conf']

def hyena_filters(L, lp):
    f32 = jnp.float32
    t = jnp.arange(L, dtype=f32)
    t_norm = t / max(L - 1, 1)
    w_ang = 2.0 * math.pi * t / L
    bands = jnp.linspace(1e-4, HY_BANDS - 1, HY_BANDS, dtype=f32)
    feat = jnp.concatenate([t_norm[:, None], jnp.cos(w_ang[:, None] * bands),
                            -jnp.sin(w_ang[:, None] * bands)], axis=-1)
    freq = lp['hy_freq'].astype(f32)
    h = jnp.sin(freq * (feat @ lp['hy_w1'].astype(f32) + lp['hy_b1'].astype(f32)))
    h = jnp.sin(freq * (h @ lp['hy_w2'].astype(f32) + lp['hy_b2'].astype(f32)))
    h = (h @ lp['hy_w3'].astype(f32) + lp['hy_b3'].astype(f32)).reshape(L, HY_ORDER, 2, HY_WIDTH)
    deltas = jnp.abs(jnp.linspace(math.log(HY_DECAY_TARGET) / HY_DECAY_LONG_PCT,
                                  math.log(HY_DECAY_TARGET) / HY_DECAY_SHORT_PCT, HY_WIDTH, dtype=f32))
    window = jnp.exp(-t_norm[:, None] * deltas[None, :])
    h = h * window[:, None, None, :]
    h_fwd = h[:, :, 0]
    h_bwd = h[:, :, 1]
    taps = jnp.concatenate([h_fwd, jnp.zeros_like(h_fwd[:1]), jnp.flip(h_bwd[1:], axis=0)], axis=0)
    taps = taps * lax.rsqrt(jnp.sum(taps * taps, axis=0, keepdims=True) + EPS)
    return jnp.fft.rfft(taps, axis=0)

def hyena_branch(ph, filt_fft, lp):
    L = ph.shape[1]
    ph = depthwise_conv(ph, lp['hy_short_w'], lp['hy_short_b'])
    v, x1, x2 = jnp.split(ph, 3, axis=-1)
    z = v.astype(jnp.float32)
    bias = lp['hy_bias'].astype(jnp.float32)
    for o, gate in enumerate((x1, x2)):
        zf = jnp.fft.rfft(z, n=2 * L, axis=1)
        y = jnp.fft.irfft(zf * filt_fft[None, :, o, :], n=2 * L, axis=1)[:, :L]
        z = gate.astype(jnp.float32) * (y + z * bias[o])
    return z.astype(ph.dtype) @ lp['w_br_hy']

def mixer_block(p, s0_f, s0_b, rope, filt_fft, lp):
    q = split_heads(p[..., OFF_Q:OFF_K], RET_DK)
    k = split_heads(p[..., OFF_K:OFF_V], RET_DK) * RET_DK ** -0.5
    v = split_heads(p[..., OFF_V:OFF_G], RET_DV)
    if rope is not None:
        q = apply_rope(q, rope[0], rope[1])
        k = apply_rope(k, rope[0], rope[1])
    b_ret = retention_branch(q, k, v, p[..., OFF_G:OFF_CONF], s0_f, s0_b, lp)
    b_conf = conformer_branch(p[..., OFF_CONF:OFF_HY], lp)
    b_hy = hyena_branch(p[..., OFF_HY:OFF_GATE], filt_fft, lp)
    g_ret, g_conf, g_hy = jnp.split(jax.nn.sigmoid(p[..., OFF_GATE:]), N_BRANCH, axis=-1)
    return (g_ret * b_ret + g_conf * b_conf + g_hy * b_hy) @ lp['w_out']

def peer_ffn(h, w_q, sub_keys, u_tab, v_tab):
    B, L, D = h.shape
    T = B * L
    ht = h.reshape(T, D)
    q = (ht @ w_q).astype(jnp.float32).reshape(T, PEER_HEADS, 2, PEER_DKEY // 2)
    s = jnp.einsum('thpd,hpkd->thpk', q, sub_keys.astype(jnp.float32))
    s_top, i_top = lax.top_k(s, PEER_TOPK)
    cand_s = s_top[:, :, 0, :, None] + s_top[:, :, 1, None, :]
    cand_i = i_top[:, :, 0, :, None] * PEER_NKEYS + i_top[:, :, 1, None, :]
    best_s, best_j = lax.top_k(cand_s.reshape(T, PEER_HEADS, -1), PEER_TOPK)
    experts = jnp.take_along_axis(cand_i.reshape(T, PEER_HEADS, -1), best_j, axis=-1)
    gates = jax.nn.softmax(best_s, axis=-1)
    n_blk = T // PEER_TOKEN_BLOCK

    def expert_block(args):
        hb, eb, gb = args
        a = jnp.einsum('tkd,td->tk', u_tab[eb], hb)
        w = (jax.nn.gelu(a.astype(jnp.float32)) * gb).astype(hb.dtype)
        return jnp.einsum('tk,tkd->td', w, v_tab[eb])

    out = lax.map(expert_block, (ht.reshape(n_blk, PEER_TOKEN_BLOCK, D),
                                 experts.reshape(n_blk, PEER_TOKEN_BLOCK, -1),
                                 gates.reshape(n_blk, PEER_TOKEN_BLOCK, -1)))
    return out.reshape(B, L, D)

def setup_inputs(seed: int = 0) -> dict:
    key = jax.random.key(seed)
    ks = iter(jax.random.split(key, 40))

    def nrm(shape, scale):
        return jax.random.normal(next(ks), shape, jnp.float32) * scale

    D = D_MODEL
    hh = np.arange(RET_HEADS, dtype=np.float64)
    gamma0 = 1.0 - 2.0 ** (-5.0 - hh)
    base_logit = jnp.asarray(np.log(gamma0) - np.log1p(-gamma0), dtype=jnp.float32)
    return {
        'x': nrm((BATCH, SEQ, D), 1.0),
        'c': nrm((BATCH, D), 1.0),
        'ctx': nrm((BATCH, CTX_LEN, D), 1.0),
        'c_ctx': nrm((D,), 1.0),
        'ada_w': nrm((DEPTH, D, 6 * D), 0.5 * D ** -0.5),
        'ada_b': nrm((DEPTH, 6 * D), 0.02),
        'norm1_g': 1.0 + nrm((DEPTH, D), 0.02),
        'norm2_g': 1.0 + nrm((DEPTH, D), 0.02),
        'w_in': nrm((DEPTH, D, IN_COLS), D ** -0.5),
        'ret_decay_logit': base_logit + nrm((DEPTH, 2, RET_HEADS), 0.05),
        'ret_gn_g': 1.0 + nrm((DEPTH, RET_HEADS * RET_DV), 0.02),
        'w_br_ret': nrm((DEPTH, RET_HEADS * RET_DV, D), (RET_HEADS * RET_DV) ** -0.5),
        'conf_dw_w': nrm((DEPTH, CONF_TAPS, CONF_WIDTH), CONF_TAPS ** -0.5),
        'conf_dw_b': nrm((DEPTH, CONF_WIDTH), 0.02),
        'conf_ln_g': 1.0 + nrm((DEPTH, CONF_WIDTH), 0.02),
        'conf_ln_b': nrm((DEPTH, CONF_WIDTH), 0.02),
        'w_br_conf': nrm((DEPTH, CONF_WIDTH, D), CONF_WIDTH ** -0.5),
        'hy_short_w': nrm((DEPTH, HY_SHORT_TAPS, (HY_ORDER + 1) * HY_WIDTH), HY_SHORT_TAPS ** -0.5),
        'hy_short_b': nrm((DEPTH, (HY_ORDER + 1) * HY_WIDTH), 0.02),
        'hy_w1': nrm((DEPTH, HY_EMB, HY_HIDDEN), HY_EMB ** -0.5),
        'hy_b1': nrm((DEPTH, HY_HIDDEN), 0.02),
        'hy_freq': 1.0 + nrm((DEPTH, HY_HIDDEN), 0.1),
        'hy_w2': nrm((DEPTH, HY_HIDDEN, HY_HIDDEN), HY_HIDDEN ** -0.5),
        'hy_b2': nrm((DEPTH, HY_HIDDEN), 0.02),
        'hy_w3': nrm((DEPTH, HY_HIDDEN, 2 * HY_ORDER * HY_WIDTH), HY_HIDDEN ** -0.5),
        'hy_b3': nrm((DEPTH, 2 * HY_ORDER * HY_WIDTH), 0.02),
        'hy_bias': nrm((DEPTH, HY_ORDER, HY_WIDTH), 0.5),
        'w_br_hy': nrm((DEPTH, HY_WIDTH, D), HY_WIDTH ** -0.5),
        'w_out': nrm((DEPTH, D, D), D ** -0.5),
        'peer_wq': nrm((DEPTH, D, PEER_HEADS * PEER_DKEY), D ** -0.5),
        'peer_keys': nrm((DEPTH, PEER_HEADS, 2, PEER_NKEYS, PEER_DKEY // 2), (PEER_DKEY // 2) ** -0.5),
        'peer_u': nrm((DEPTH, PEER_EXPERTS, D), D ** -0.5),
        'peer_v': nrm((DEPTH, PEER_EXPERTS, D), 1.0),
        'final_g': 1.0 + nrm((D,), 0.02),
    }

def reference(x, c, ctx, c_ctx, ada_w, ada_b, norm1_g, norm2_g, w_in, ret_decay_logit, ret_gn_g,
              w_br_ret, conf_dw_w, conf_dw_b, conf_ln_g, conf_ln_b, w_br_conf, hy_short_w, hy_short_b,
              hy_w1, hy_b1, hy_freq, hy_w2, hy_b2, hy_w3, hy_b3, hy_bias, w_br_hy, w_out, peer_wq,
              peer_keys, peer_u, peer_v, final_g):
    L = x.shape[1]
    Lc = ctx.shape[1]
    ROWS = L // GRID_W
    rope = grid_rope_angles(ROWS)
    for l in range(DEPTH):
        last = l == DEPTH - 1
        lp = {
            'log_g': jax.nn.log_sigmoid(ret_decay_logit[l].astype(jnp.float32)),
            'ret_gn_g': ret_gn_g[l], 'w_br_ret': w_br_ret[l],
            'conf_dw_w': conf_dw_w[l], 'conf_dw_b': conf_dw_b[l],
            'conf_ln_g': conf_ln_g[l], 'conf_ln_b': conf_ln_b[l], 'w_br_conf': w_br_conf[l],
            'hy_short_w': hy_short_w[l], 'hy_short_b': hy_short_b[l],
            'hy_w1': hy_w1[l], 'hy_b1': hy_b1[l], 'hy_freq': hy_freq[l],
            'hy_w2': hy_w2[l], 'hy_b2': hy_b2[l], 'hy_w3': hy_w3[l], 'hy_b3': hy_b3[l],
            'hy_bias': hy_bias[l], 'w_br_hy': w_br_hy[l], 'w_out': w_out[l],
        }
        mod = adaln(c, ada_w[l], ada_b[l])
        mod_c = adaln(c_ctx[None, :], ada_w[l], ada_b[l])

        u_c = modulate(rms_norm(ctx, norm1_g[l]), mod_c[0], mod_c[1])
        if last:
            pk_c = u_c @ w_in[l][:, OFF_K:OFF_V]
            pv_c = u_c @ w_in[l][:, OFF_V:OFF_G]
        else:
            p_c = u_c @ w_in[l]
            pk_c = p_c[..., OFF_K:OFF_V]
            pv_c = p_c[..., OFF_V:OFF_G]
        s_f, s_b = retention_final_states(split_heads(pk_c, RET_DK) * RET_DK ** -0.5,
                                          split_heads(pv_c, RET_DV), lp['log_g'])

        u = modulate(rms_norm(x, norm1_g[l]), mod[0], mod[1])
        p = u @ w_in[l]
        x = x + mod[2] * mixer_block(p, s_f, s_b, rope, hyena_filters(L, lp), lp)

        x = x + mod[5] * peer_ffn(modulate(rms_norm(x, norm2_g[l]), mod[3], mod[4]),
                                  peer_wq[l], peer_keys[l], peer_u[l], peer_v[l])

        if not last:
            zero = jnp.zeros_like(s_f)
            ctx = ctx + mod_c[2] * mixer_block(p_c, zero, zero, None, hyena_filters(Lc, lp), lp)
            ctx = ctx + mod_c[5] * peer_ffn(modulate(rms_norm(ctx, norm2_g[l]), mod_c[3], mod_c[4]),
                                            peer_wq[l], peer_keys[l], peer_u[l], peer_v[l])
    return rms_norm(x, final_g)


_drawn_inputs = setup_inputs


def setup_inputs(seed=0):
    import zlib

    import numpy as np

    out = dict(_drawn_inputs(seed))
    spreads = {}
    factors = {'ret_gn_g': 3.674,
     'conf_dw_b': 2.823,
     'conf_ln_g': 3.759,
     'conf_ln_b': 3.597,
     'final_g': 2.863}
    for name, (base, spread) in spreads.items():
        noise = np.random.default_rng([zlib.crc32(name.encode()), seed]).standard_normal(out[name].shape)
        drawn = base * np.exp(spread * noise) if base else spread * noise
        out[name] = jnp.asarray(drawn.astype(out[name].dtype))
    for name, factor in factors.items():
        out[name] = (out[name] * factor).astype(out[name].dtype)
    return out
```

```python
import math
from contextlib import ExitStack

import numpy as np
import concourse.bass as bass
from concourse import mybir

F32 = mybir.dt.float32
U32 = mybir.dt.uint32
F32R = mybir.dt.float32r
ALU = mybir.AluOpType
ACT = mybir.ActivationFunctionType
AX = mybir.AxisListType
ds = bass.ds

P = 128
D = 1024
KC = D // P
SEQ, CTX = 512, 256
DEPTH = 2
EPS = 1e-6
GRID_W = 64
HEADS, DK, DV = 8, 64, 128
TAPS, HALF = 31, 15
CW = HW = 512
CT4 = CW // P
EMB, HID = 33, 64
NK = 128
TOPK = 16
NMIX, NQ = 92, 8
LOW = -3.0e38

_cols = dict(n1=8, n2=8, ada_b=48, gn=8, cdw=CT4 * TAPS, cdb=4, clg=4, clb=4, hsw=36, hsb=12,
             hbias=8, logit=16, mlp=3)
PCOL, _at = {}, 0
for _n, _c in _cols.items():
    PCOL[_n] = (_at, _c)
    _at += _c
NPAR = _at


class Count:

    def __init__(self, nc, stack, name):
        self.sem = stack.enter_context(nc.semaphore(name))
        self.base = 0

    def at(self, n):
        return n + self.base

    def add(self, n):
        self.base += n


def build(nc, xT, cT, ctxT, final_g, ada, mix, peer_u, peer_v, par, hw1, hw2, hw3, keys, k_mats, k_rope,
          k_dec, k_decc, k_feat_x, k_feat_c, k_win_x, k_win_c, k_dft_x, k_dft_c, out):
    stack = ExitStack()
    with stack:
        M0 = -(-(14208 + NPAR + 265) // 8) * 8
        kept = stack.enter_context(nc.sbuf_tensor("kept", [P, M0], F32))
        sb_at = nc.sbuf_base - 4 * M0
        arena = stack.enter_context(nc.sbuf_tensor("arena", [P, 53200 - M0], F32))
        ps = stack.enter_context(nc.psum_tensor("psum", [P, 8, 512], F32))
        spec_d = nc.dram_tensor("spec_scratch", (2, 2, P, 4 * 2 * 512), F32, kind="Internal").ap()
        gate_d = nc.dram_tensor("gate_scratch", (NK, P, SEQ + CTX), F32, kind="Internal").ap()

        def new(name):
            return Count(nc, stack, name)

        loaded = [new(f"weights_loaded_{k}") for k in range(4)]
        blocks_done = new("blocks_done")
        bank_free = new("bank_free")
        gate_ready = new("gate_ready")
        consts_in = new("consts_loaded")
        store_done = new("store_done")
        pe_a, pe_b = new("pe_first"), new("pe_second")
        dve_a, dve_b, dve_c = new("dve_first"), new("dve_second"), new("dve_third")
        act_a, act_b = new("act_first"), new("act_second")
        pool_a = new("pool_first")
        u_hi, v_hi = new("u_rounded"), new("v_rounded")
        u_split, v_split = new("u_split"), new("v_split")
        w_ready = new("w_split")
        root_ready = new("root_ready")
        gates_in = [new("gates_loaded_0"), new("gates_loaded_1")]

        def flat(at, n):
            return kept[:, at:at + n] if at < M0 else arena[:, at - M0:at - M0 + n]

        def area(at, *shape):
            n = int(np.prod(shape))
            v = flat(at, n)
            if len(shape) == 2:
                v = v.rearrange("p (a b) -> p a b", b=shape[1])
            if len(shape) == 3:
                v = v.rearrange("p (a b c) -> p a b c", b=shape[1], c=shape[2])
            return v

        T_OF = {"X": SEQ, "C": CTX}
        res_flat = {"X": area(0, 4096), "C": area(4096, 2048)}
        res = {s: v.rearrange("p (a t) -> p a t", t=T_OF[s]) for s, v in res_flat.items()}
        ctx_k = area(6144, 4, 256)
        ctx_v = area(7168, 2, 1024)
        ring = area(9216, 4, 1024)
        mats = area(13312, 7, 128)
        ident, rotate, mean_d, mean_c, mean_h, ones, iota = (mats[:, n, :] for n in range(7))
        pars = area(14208, NPAR)
        o = 14208 + NPAR
        mod = area(o, 48, 2)
        amp = area(o + 96, 4, 8)
        cs = area(o + 128, 8, 2)
        cs_sig = area(o + 144, 8, 2)
        lg = area(o + 160, 16)
        lt = area(o + 176, 5, 16)
        fin_g = area(o + 256, 8)
        eps = area(o + 264, 1)
        SEG = {"X": 0, "C": 1}

        def par_of(name):
            a, n = PCOL[name]
            return pars[:, a:a + n]

        runs = []
        for l in range(DEPTH):
            runs.append(("ada", l, 0, 48))
            runs.append(("mix", l, 0, NMIX) if l == 0 else ("mix", l, 4, 12))
            runs.append(("mix", l, 0, NMIX))
            runs += [("mix", l, NMIX, NQ)] * (2 if l == 0 else 1)
            runs.append(("peer", l, 0, 4))
        tables = {"ada": ada, "mix": mix}
        order = [(r, l, n + k) for r, l, n, m in runs for k in range(m)]
        place = [0]

        def block_of(entry):
            kind, l, n = entry
            if kind == "peer":
                return (peer_u, peer_v)[n // 2][l, n % 2]
            return tables[kind][l, n]

        def load_ahead(eng, n):
            at, j = place[0] + 4, 0
            ahead = order[at:at + n]
            while j < len(ahead):
                kind, l, first = ahead[j]
                whole = 4
                while ahead[j + whole - 1:j + whole + 1][1:] == [(kind, l, first + whole)]:
                    whole += 4
                if kind != "peer" and whole > 4:
                    with eng.Fori(0, whole // 4) as i:
                        for k in range(4):
                            eng.wait_ge(blocks_done.sem, blocks_done.at(4 * i + (j + k + 1)))
                            eng.dma_start(ring[:, k, :], tables[kind][l, ds(4 * i + (first + k), 1)].rearrange("o p n -> p (o n)"))\
                               .then_inc(loaded[k].sem, 16)
                else:
                    for k in range(whole):
                        eng.wait_ge(blocks_done.sem, blocks_done.at(j + k + 1))
                        eng.dma_start(ring[:, k, :], block_of(ahead[j + k])).then_inc(loaded[k].sem, 16)
                j += whole

        def streamed(n, products):
            place[0] += n
            blocks_done.add(n)
            bank_free.add(products)
            for k in range(4):
                loaded[k].add(16 * n // 4)

        def pe_linear(pe, first, n, act, T):
            with pe.Fori(0, n // 4) as i:
                for k in range(4):
                    pe.wait_ge(loaded[k].sem, loaded[k].at(16 * i + (4 * first + 16)))
                    pe.wait_ge(bank_free.sem, bank_free.at(4 * i + (first + k + 1)))
                    for kc in range(KC):
                        last = pe.matmul(ps[:, k, 0:T], ring[:, k, kc * P:(kc + 1) * P], act[:, kc, :],
                                         start=kc == 0, stop=kc == KC - 1)
                    last.then_inc(blocks_done.sem, 1)

        with nc.Block() as block:
            @block.sync
            def _(sp):
                for k in range(4):
                    sp.dma_start(ring[:, k, :], ada[0, k]).then_inc(loaded[k].sem, 16)
                sp.dma_start(res_flat["X"], xT).then_inc(consts_in.sem, 16)
                sp.dma_start(res_flat["C"], ctxT).then_inc(consts_in.sem, 16)
                sp.dma_start(mats.rearrange("p a b -> p (a b)"), k_mats).then_inc(consts_in.sem, 16)
                sp.dma_start(cs.rearrange("p a b -> p (a b)"), cT).then_inc(consts_in.sem, 16)
                sp.dma_start(fin_g, final_g).then_inc(consts_in.sem, 16)
                sp.wait_ge(consts_in.sem, consts_in.at(80))

            @block.scalar
            def _(act):
                act.wait_ge(consts_in.sem, consts_in.at(80))
                act.activation(cs_sig, cs, ACT.Sigmoid).then_inc(act_a.sem, 1)

            @block.vector
            def _(dve):
                dve.memset(eps, EPS)
                dve.memset(lt[:, 0, :], 0.0).then_inc(bank_free.sem, 4)
                dve.wait_ge(act_a.sem, act_a.at(1))
                dve.tensor_tensor(cs, cs, cs_sig, ALU.mult)
        consts_in.add(80)
        act_a.add(1)

        def stage_ada(l):
            with nc.Block() as block:
                @block.sync
                def _(sp):
                    sp.dma_start(pars, par[l]).then_inc(consts_in.sem, 16)
                    load_ahead(sp, 48)

                @block.tensor
                def _(pe):
                    pm = ps[:, 4, 0:96]
                    with pe.Fori(0, 12) as i:
                        for k in range(4):
                            pe.wait_ge(loaded[k].sem, loaded[k].at(16 * i + 16))
                            for kc in range(KC):
                                last = pe.matmul(pm[:, ds(8 * i + 2 * k, 2)], ring[:, k, kc * P:(kc + 1) * P],
                                                 cs[:, kc, :], start=kc == 0, stop=kc == KC - 1)
                            last.then_inc(blocks_done.sem, 1)

                @block.scalar
                def _(act):
                    act.wait_ge(dve_a.sem, dve_a.at(1))
                    act.activation(lt[:, 1, :], lt[:, 0, :], ACT.Exp).then_inc(act_a.sem, 1)

                @block.vector
                def _(dve):
                    x, y, z, z2, r = (lt[:, n, :] for n in range(5))
                    logit = par_of("logit")
                    dve.wait_ge(consts_in.sem, consts_in.at(16))
                    dve.tensor_scalar(x, logit, -1.0, None, ALU.mult)
                    dve.drain()
                    dve.tensor_tensor(x, x, logit, ALU.min).then_inc(dve_a.sem, 1)
                    dve.wait_ge(act_a.sem, act_a.at(1))
                    dve.tensor_scalar(z2, y, 2.0, None, ALU.add)
                    dve.drain()
                    dve.reciprocal(z, z2)
                    dve.drain()
                    dve.tensor_tensor(z, z, y, ALU.mult)
                    dve.memset(r, 0.0)
                    dve.drain()
                    dve.tensor_tensor(z2, z, z, ALU.mult)
                    dve.drain()
                    for n in range(19, 1, -2):
                        dve.scalar_tensor_tensor(r, r, 1.0 / n, z2, ALU.add, ALU.mult)
                        dve.drain()
                    dve.scalar_tensor_tensor(r, r, 1.0, z, ALU.add, ALU.mult)
                    dve.tensor_scalar(x, logit, 0.0, None, ALU.min)
                    dve.drain()
                    dve.scalar_tensor_tensor(lg, r, -2.0, x, ALU.mult, ALU.add)
                    dve.wait_ge(blocks_done.sem, blocks_done.at(48))
                    b = par_of("ada_b").unsqueeze(2).broadcast_to([P, 48, 2])
                    dve.tensor_tensor(mod, ps[:, 4, 0:96].rearrange("p (a b) -> p a b", b=2), b, ALU.add)
                    dve.drain()
                    for norm in range(2):
                        g = par_of("n1" if norm == 0 else "n2")
                        for s in range(2):
                            j = 8 * (1 + 3 * norm)
                            dve.scalar_tensor_tensor(amp[:, 2 * norm + s, :], mod[:, j:j + 8, s], 1.0, g,
                                                     ALU.add, ALU.mult)
            consts_in.add(16)
            dve_a.add(1)
            act_a.add(1)
            streamed(48, 0)

        def stage_filters(l, s):
            L = T_OF[s]
            nt = L // P
            a = M0
            feat, h1, h2, rr = area(a, L), area(a + 512, L), area(a + 1024, L), area(a + 1536, L)
            w1, w2, w3 = area(a + 2048, HID), area(a + 2112, HID), area(a + 2176, 2048)
            a += 4224
            win = area(a, nt, 2, 512)
            a += 4096
            ab = flat(a, nt * 2048)
            ab = ab.rearrange("p (n d o c) -> p n d o c", d=2, o=2, c=512)
            a += 8192
            dft = area(a, nt, 2, L)
            a += 4096
            sq = area(a, 2, 512)
            hb = area(a + 1024, 2, 512)
            inv = area(a + 2048, 2, 512)
            stage = flat(a + 3072, nt * 2048).rearrange("p (o k r c) -> p o k r c", o=2, r=2, c=512)
            k_feat, k_win, k_dft = (k_feat_x, k_win_x, k_dft_x) if s == "X" else (k_feat_c, k_win_c, k_dft_c)
            mlp = par_of("mlp")
            MAGIC, TWO_PI = 12582912.0, 2.0 * math.pi
            HI = float(np.float32(6.28125))
            LO = TWO_PI - HI

            with nc.Block() as block:
                @block.sync
                def _(sp):
                    sp.dma_start(feat[0:EMB, :], k_feat).then_inc(consts_in.sem, 16)
                    sp.dma_start(w1[0:EMB, :], hw1[l]).then_inc(consts_in.sem, 16)
                    sp.dma_start(w2[0:HID, :], hw2[l]).then_inc(consts_in.sem, 16)
                    sp.dma_start(w3[0:HID + 1, :], hw3[l]).then_inc(consts_in.sem, 16)
                    sp.dma_start(win.rearrange("p a b c -> p (a b c)"), k_win).then_inc(consts_in.sem, 16)
                    sp.dma_start(dft.rearrange("p a b c -> p (a b c)"), k_dft[0]).then_inc(consts_in.sem, 16)
                    sp.wait_ge(dve_b.sem, dve_b.at(2 * nt * 2))
                    for o in range(2):
                        sp.dma_start(spec_d[SEG[s], o, :, 0:nt * 1024],
                                     stage[:, o].rearrange("p k r c -> p (k r c)")).then_inc(store_done.sem, 16)
                    sp.wait_ge(store_done.sem, store_done.at(32))

                @block.tensor
                def _(pe):
                    pe.wait_ge(consts_in.sem, consts_in.at(96))
                    pe.matmul(ps[0:HID, 4, 0:L], w1[0:EMB, :], feat[0:EMB, :], start=True, stop=True).then_inc(pe_a.sem, 1)
                    pe.wait_ge(act_a.sem, act_a.at(1))
                    pe.matmul(ps[0:HID, 5, 0:L], w2[0:HID, :], h1[0:HID, :], start=True, stop=True).then_inc(pe_a.sem, 1)
                    pe.wait_ge(act_a.sem, act_a.at(2))
                    for n in range(nt):
                        for q in range(4):
                            j = 4 * n + q
                            if j >= 4:
                                pe.wait_ge(dve_a.sem, dve_a.at(2 + j - 3))
                            pe.matmul(ps[:, q, :], h2[0:HID + 1, n * P:(n + 1) * P], w3[0:HID + 1, q * 512:(q + 1) * 512],
                                      start=True, stop=True).then_inc(pe_a.sem, 1)
                    for o in range(2):
                        for j in range(2 * nt):
                            pe.wait_ge(act_b.sem, act_b.at(2 * nt * o + j + 1))
                            pe.matmul(ps[:, 4 + o, :], ones, sq[:, j % 2, :], start=j == 0,
                                      stop=j == 2 * nt - 1).then_inc(pe_b.sem, 1)
                    j = 0
                    for o in range(2):
                        for kt in range(nt):
                            for r in range(2):
                                if j >= 4:
                                    pe.wait_ge(dve_b.sem, dve_b.at(j - 3))
                                for n in range(nt):
                                    last = pe.matmul(ps[:, j % 4, :], dft[:, n, r, kt * P:(kt + 1) * P],
                                                     ab[:, n, r, o, :], start=n == 0, stop=n == nt - 1)
                                last.then_inc(pe_a.sem, 1)
                                j += 1

                @block.scalar
                def _(act):
                    act.wait_ge(dve_a.sem, dve_a.at(1))
                    act.activation(h1[0:HID, :], h1[0:HID, :], ACT.Sin).then_inc(act_a.sem, 1)
                    act.wait_ge(dve_a.sem, dve_a.at(2))
                    act.activation(h2[0:HID, :], h2[0:HID, :], ACT.Sin).then_inc(act_a.sem, 1)
                    act.wait_ge(dve_c.sem, dve_c.at(1))
                    for o in range(2):
                        for n in range(nt):
                            for d in range(2):
                                j = 2 * nt * o + 2 * n + d
                                if j >= 2:
                                    act.wait_ge(pe_b.sem, pe_b.at(j - 1))
                                act.activation(sq[:, j % 2, :], ab[:, n, d, o, :], ACT.Square).then_inc(act_b.sem, 1)
                    for o in range(2):
                        act.wait_ge(pe_b.sem, pe_b.at(2 * nt * (o + 1)))
                        act.activation(inv[:, o, :], ps[:, 4 + o, :], ACT.Sqrt, scale=0.5, bias=eps).then_inc(root_ready.sem, 1)

                @block.vector
                def _(dve):
                    dve.memset(h2[64:65, :], 1.0)
                    dve.wait_ge(consts_in.sem, consts_in.at(96))
                    for layer, (bank, h, col) in enumerate(((4, h1, 0), (5, h2, 2))):
                        dve.wait_ge(pe_a.sem, pe_a.at(layer + 1))
                        hh, r = h[0:HID, :], rr[0:HID, :]
                        dve.tensor_scalar(hh, ps[0:HID, bank, 0:L], mlp[0:HID, col:col + 1], mlp[0:HID, 1:2], ALU.add, ALU.mult)
                        dve.drain()
                        dve.tensor_scalar(r, hh, 1.0 / TWO_PI, None, ALU.mult)
                        dve.drain()
                        dve.tensor_scalar(r, r, MAGIC, None, ALU.add)
                        dve.drain()
                        dve.tensor_scalar(r, r, -MAGIC, None, ALU.add)
                        dve.drain()
                        dve.scalar_tensor_tensor(hh, r, -HI, hh, ALU.mult, ALU.add)
                        dve.drain()
                        dve.scalar_tensor_tensor(hh, r, -LO, hh, ALU.mult, ALU.add)
                        dve.drain()
                        dve.tensor_scalar(hh, hh, 3.1415925, -3.1415925, ALU.min, ALU.max).then_inc(dve_a.sem, 1)
                    for n in range(nt):
                        for o in range(2):
                            for d in range(2):
                                j = 4 * n + 2 * o + d
                                dve.wait_ge(pe_a.sem, pe_a.at(2 + j + 1))
                                dve.tensor_tensor(hb[:, d, :], ps[:, 2 * o + d, :], win[:, n, d, :], ALU.mult)\
                                   .then_inc(dve_a.sem, 1)
                            dve.drain()
                            dve.tensor_tensor(ab[:, n, 0, o, :], hb[:, 0, :], hb[:, 1, :], ALU.add)
                            last = dve.tensor_tensor(ab[:, n, 1, o, :], hb[:, 0, :], hb[:, 1, :], ALU.subtract)
                            if n < nt - 1 or o == 0:
                                dve.drain()
                    last.then_inc(dve_c.sem, 1)
                    for o in range(2):
                        dve.wait_ge(root_ready.sem, root_ready.at(o + 1))
                        dve.reciprocal(inv[:, o, :], inv[:, o, :])
                    dve.drain()
                    j = 0
                    for o in range(2):
                        for kt in range(nt):
                            for r in range(2):
                                dve.wait_ge(pe_a.sem, pe_a.at(2 + 4 * nt + j + 1))
                                dve.scalar_tensor_tensor(stage[:, o, kt, r, :], ps[:, j % 4, :], 1.0 / L, inv[:, o, :],
                                                         ALU.mult, ALU.mult).then_inc(dve_b.sem, 1)
                                j += 1
            consts_in.add(96)
            store_done.add(32)
            pe_a.add(2 + 4 * nt + 4 * nt)
            pe_b.add(4 * nt)
            act_a.add(2)
            act_b.add(4 * nt)
            dve_a.add(2 + 4 * nt)
            root_ready.add(2)
            dve_b.add(4 * nt)
            dve_c.add(1)

        def stage_norm(s, norm, dst, rs):
            T = T_OF[s]
            with nc.Block() as block:
                @block.scalar
                def _(act):
                    act.activation(dst, res[s], ACT.Square).then_inc(act_a.sem, 1)
                    act.wait_ge(pe_a.sem, pe_a.at(1))
                    act.activation(rs, ps[:, 7, 0:T], ACT.Sqrt, bias=eps).then_inc(root_ready.sem, 1)
                    for kc in range(KC):
                        act.wait_ge(dve_a.sem, dve_a.at(1))
                        if norm < 2:
                            act.activation(dst[:, kc, :], dst[:, kc, :], ACT.Identity,
                                           scale=amp[:, 2 * norm + SEG[s], kc:kc + 1],
                                           bias=mod[:, 24 * norm + kc, SEG[s]:SEG[s] + 1])
                        else:
                            act.activation(dst[:, kc, :], dst[:, kc, :], ACT.Copy, scale=fin_g[:, kc:kc + 1])

                @block.tensor
                def _(pe):
                    pe.wait_ge(act_a.sem, act_a.at(1))
                    for kc in range(KC):
                        last = pe.matmul(ps[:, 7, 0:T], mean_d, dst[:, kc, :], start=kc == 0, stop=kc == KC - 1)
                    last.then_inc(pe_a.sem, 1)

                @block.vector
                def _(dve):
                    dve.wait_ge(root_ready.sem, root_ready.at(1))
                    dve.reciprocal(rs, rs)
                    dve.drain()
                    dve.tensor_tensor(dst, res[s], rs.unsqueeze(1).broadcast_to([P, KC, T]), ALU.mult).then_inc(dve_a.sem, 1)
            act_a.add(1)
            root_ready.add(1)
            pe_a.add(1)
            dve_a.add(1)

        def places(s):
            T = T_OF[s]
            m = {"T": T, "nt": T // P, "M": M0 - 14848}
            b = M0
            m["u"] = area(b, 8, T)
            m["qk"] = area(b + 4096, 8 * T)
            m["merged"] = area(b + 4096, 8, T)
            m["v"] = area(b + 8192, m["nt"], 1024)
            m["g"] = area(b + 12288, 8 * T)
            m["cp"] = area(b + 16384, 4, T + 2 * HALF)
            m["hc"] = area(b + 18552, 4, T)
            m["hp"] = area(b + 20600, 12, T + 2)
            m["hp_flat"] = flat(b + 20600, 6168)
            m["rest"] = b + 26768
            m["ret"] = b + 18552
            return m

        def stage_project(s, m, full):
            T, nt = m["T"], m["nt"]
            n_qk = 8 if full else 4
            total = 44 if full else 12
            off = 0 if full else 4
            tmp = area(m["rest"], 4, T)
            qk, v, g = m["qk"], m["v"], m["g"]

            with nc.Block() as block:
                @block.sync
                def _(sp):
                    load_ahead(sp, total)

                @block.tensor
                def _(pe):
                    pe_linear(pe, 0, n_qk, m["u"], T)
                    with pe.Fori(0, 2) as i:
                        for k in range(4):
                            pe.wait_ge(loaded[k].sem, loaded[k].at(16 * i + (4 * n_qk + 16)))
                            pe.wait_ge(bank_free.sem, bank_free.at(4 * i + (n_qk + k + 1)))
                            for tt in range(nt):
                                for kc in range(KC):
                                    last = pe.matmul(ps[:, k, tt * P:(tt + 1) * P], m["u"][:, kc, tt * P:(tt + 1) * P],
                                                     ring[:, k, kc * P:(kc + 1) * P], start=kc == 0, stop=kc == KC - 1)
                            last.then_inc(blocks_done.sem, 1)
                    if full:
                        pe_linear(pe, 16, 28, m["u"], T)

                @block.scalar
                def _(act):
                    if not full:
                        return
                    with act.Fori(0, 2) as i:
                        for k in range(4):
                            act.wait_ge(blocks_done.sem, blocks_done.at(4 * i + (16 + k + 1)))
                            act.wait_ge(bank_free.sem, bank_free.at(4 * i + (16 + k + 1)))
                            act.activation(tmp[:, k, :], ps[:, k, 0:T], ACT.Sigmoid).then_inc(gate_ready.sem, 1)
                    with act.Fori(0, 2) as i:
                        for k in (1, 3):
                            act.wait_ge(blocks_done.sem, blocks_done.at(4 * i + (24 + k + 1)))
                            act.wait_ge(bank_free.sem, bank_free.at(4 * i + (24 + k + 1)))
                            act.activation(tmp[:, k, :], ps[:, k, 0:T], ACT.Sigmoid).then_inc(gate_ready.sem, 1)

                @block.vector
                def _(dve):
                    if full:
                        dve.memset(m["cp"][:, :, 0:HALF], 0.0)
                        dve.memset(m["cp"][:, :, HALF + T:], 0.0)
                        dve.memset(m["hp"][:, :, 0:1], 0.0)
                        dve.memset(m["hp"][:, :, T + 1:], 0.0)
                    with dve.Fori(0, n_qk // 4) as i:
                        for k in range(4):
                            dve.wait_ge(blocks_done.sem, blocks_done.at(4 * i + (k + 1)))
                            dve.tensor_copy(qk[:, ds(4 * T * i + (off + k) * T, T)], ps[:, k, 0:T]).then_inc(bank_free.sem, 1)
                    with dve.Fori(0, 2) as i:
                        for k in range(4):
                            dve.wait_ge(blocks_done.sem, blocks_done.at(4 * i + (n_qk + k + 1)))
                            dve.tensor_copy(v[:, :, ds(4 * P * i + k * P, P)],
                                            ps[:, k, 0:T].rearrange("p (a b) -> p a b", b=P)).then_inc(bank_free.sem, 1)
                    if not full:
                        dve.drain()
                        dve.tensor_copy(ctx_k, qk[:, 4 * T:8 * T].rearrange("p (a b) -> p a b", b=T))
                        dve.tensor_copy(ctx_v, v)
                        return
                    with dve.Fori(0, 2) as i:
                        for k in range(4):
                            dve.wait_ge(gate_ready.sem, gate_ready.at(4 * i + (k + 1)))
                            dve.tensor_tensor(g[:, ds(4 * T * i + k * T, T)], ps[:, k, 0:T], tmp[:, k, :], ALU.mult)\
                               .then_inc(bank_free.sem, 1)
                    cp_flat = m["cp"].rearrange("p a b -> p (a b)")
                    cstep = T + 2 * HALF
                    with dve.Fori(0, 2) as i:
                        for k in (1, 3):
                            dve.wait_ge(gate_ready.sem, gate_ready.at(2 * i + (8 + (k + 1) // 2)))
                            dve.tensor_tensor(cp_flat[:, ds(2 * cstep * i + (k // 2) * cstep + HALF, T)],
                                              ps[:, k - 1, 0:T], tmp[:, k, :], ALU.mult).then_inc(bank_free.sem, 2)
                    hp_flat = m["hp"].rearrange("p a b -> p (a b)")
                    hstep = T + 2
                    with dve.Fori(0, 3) as i:
                        for k in range(4):
                            dve.wait_ge(blocks_done.sem, blocks_done.at(4 * i + (32 + k + 1)))
                            dve.tensor_copy(hp_flat[:, ds(4 * hstep * i + k * hstep + 1, T)], ps[:, k, 0:T])\
                               .then_inc(bank_free.sem, 1)
                    if s == "C":
                        dve.drain()
                        dve.tensor_copy(ctx_k, qk[:, 4 * T:8 * T].rearrange("p (a b) -> p a b", b=T))
                        dve.tensor_copy(ctx_v, v)
            if full:
                gate_ready.add(12)
            streamed(total, total)

        def stage_rope(m):
            a = m["rest"]
            cos, sin, t = area(a, 512), area(a + 512, 512), area(a + 1024, 2, 512)
            qk = m["qk"]
            with nc.Block() as block:
                @block.sync
                def _(sp):
                    sp.dma_start(cos, k_rope[0]).then_inc(consts_in.sem, 16)
                    sp.dma_start(sin, k_rope[1]).then_inc(consts_in.sem, 16)

                @block.tensor
                def _(pe):
                    for n in range(8):
                        if n >= 2:
                            pe.wait_ge(dve_a.sem, dve_a.at(n - 1))
                        pe.matmul(ps[:, n % 2, :], rotate, qk[:, n * 512:(n + 1) * 512], start=True, stop=True)\
                          .then_inc(pe_a.sem, 1)

                @block.vector
                def _(dve):
                    dve.wait_ge(consts_in.sem, consts_in.at(32))
                    for n in range(8):
                        x = qk[:, n * 512:(n + 1) * 512]
                        dve.wait_ge(pe_a.sem, pe_a.at(n + 1))
                        dve.tensor_tensor(t[:, n % 2, :], ps[:, n % 2, :], sin, ALU.mult).then_inc(dve_a.sem, 1)
                        dve.tensor_tensor(x, x, cos, ALU.mult)
                        dve.drain()
                        dve.tensor_tensor(x, x, t[:, n % 2, :], ALU.add)
            consts_in.add(32)
            pe_a.add(8)
            dve_a.add(8)

        def stage_retention(s, m):
            T, nt = m["T"], m["nt"]
            own = [("own", j) for j in range(nt)]
            tiles = own + ([("ctx", j) for j in range(2)] if s == "X" else [])
            NJ = len(tiles)
            a = m["rest"]
            dec = area(a, 3, 896)
            a += 2688
            decc = area(a, 2, 640)
            a += 1280
            e = area(a, 2, 896)
            a += 1792
            ec = area(a, 2, 640)
            a += 1280
            q_s, k_s, kc_s = area(a, T), area(a + 512, T), area(a + 1024, 256)
            a += 1280
            v_s = area(a, 6, 256)
            a += 1536
            prob = area(a, 2, 512)
            a += 1024
            o_s, o_c, o_q, rs = (area(m["ret"] + 512 * n, T) for n in range(4))
            qk, v, g = m["qk"], m["v"], m["g"]
            SC = DK ** -0.5
            gn = par_of("gn")

            with nc.Block() as block:
                @block.sync
                def _(sp):
                    sp.dma_start(dec.rearrange("p a b -> p (a b)"), k_dec).then_inc(consts_in.sem, 16)
                    sp.dma_start(decc.rearrange("p a b -> p (a b)"), k_decc).then_inc(consts_in.sem, 16)

                @block.scalar
                def _(act):
                    act.wait_ge(consts_in.sem, consts_in.at(32))
                    with act.Fori(0, 4) as hp:
                        for h in range(2):
                            for d in range(2):
                                act.activation(e[:, d, :], dec[:, d, :], ACT.Exp, scale=lg[:, ds(2 * hp + (8 * d + h), 1)])
                                last = act.activation(ec[:, d, :], decc[:, d, :], ACT.Exp,
                                                      scale=lg[:, ds(2 * hp + (8 * d + h), 1)])
                            last.then_inc(act_a.sem, 1)
                            act.wait_ge(pe_b.sem, pe_b.at(6 * hp + (3 * h + 1)))
                            act.activation(o_s, ps[:, 2, 0:T], ACT.Copy).then_inc(act_b.sem, 1)
                            act.wait_ge(dve_b.sem, dve_b.at(2 * hp + (h + 1)))
                            act.activation(o_q, o_c, ACT.Square).then_inc(act_b.sem, 1)
                            act.wait_ge(pe_b.sem, pe_b.at(6 * hp + (3 * h + 3)))
                            act.activation(rs, ps[:, 4, 0:T], ACT.Sqrt, bias=eps).then_inc(root_ready.sem, 1)

                @block.tensor
                def _(pe):
                    with pe.Fori(0, 4) as hp:
                        pe.wait_ge(dve_a.sem, dve_a.at(hp + 1))
                        for h in range(2):
                            b = h * DK
                            n0 = NJ * h

                            def score(j):
                                kind, jt = tiles[j]
                                k = k_s if kind == "own" else kc_s
                                pe.matmul(ps[:, j % 2, 0:T], k[b:b + DK, jt * P:(jt + 1) * P], q_s[b:b + DK, :],
                                          start=True, stop=True).then_inc(pe_a.sem, 1)

                            score(0)
                            for j in range(NJ):
                                if j + 1 < NJ:
                                    score(j + 1)
                                pe.wait_ge(dve_c.sem, dve_c.at(2 * NJ * hp + (n0 + j + 1)))
                                last = pe.matmul(ps[:, 2, 0:T], v_s[:, j, h * P:(h + 1) * P], prob[:, j % 2, 0:T],
                                                 start=j == 0, stop=j == NJ - 1)
                            last.then_inc(pe_b.sem, 1)
                            pe.wait_ge(act_b.sem, act_b.at(4 * hp + (2 * h + 1)))
                            pe.matmul(ps[:, 3, 0:T], mean_h, o_s, start=True, stop=True).then_inc(pe_b.sem, 1)
                            pe.wait_ge(act_b.sem, act_b.at(4 * hp + (2 * h + 2)))
                            pe.matmul(ps[:, 4, 0:T], mean_h, o_q, start=True, stop=True).then_inc(pe_b.sem, 1)

                @block.vector
                def _(dve):
                    dve.wait_ge(consts_in.sem, consts_in.at(32))
                    with dve.Fori(0, 4) as hp:
                        dve.tensor_copy(q_s, qk[:, ds(T * hp, T)])
                        dve.tensor_copy(k_s, qk[:, ds(T * hp + 4 * T, T)])
                        last = dve.tensor_copy(v_s[:, 0:nt, :], v[:, :, ds(256 * hp, 256)])
                        if s == "X":
                            dve.tensor_copy(kc_s, ctx_k.rearrange("p a b -> p (a b)")[:, ds(256 * hp, 256)])
                            last = dve.tensor_copy(v_s[:, nt:nt + 2, :], ctx_v[:, :, ds(256 * hp, 256)])
                        last.then_inc(dve_a.sem, 1)
                        for h in range(2):
                            n0 = NJ * h
                            dve.wait_ge(act_a.sem, act_a.at(2 * hp + h + 1))
                            dve.tensor_tensor(e[:, 0, :], e[:, 0, :], e[:, 1, :], ALU.mult)
                            dve.tensor_tensor(ec[:, 0, :], ec[:, 0, :], ec[:, 1, :], ALU.add)
                            dve.drain()
                            dve.tensor_tensor(e[:, 0, :], e[:, 0, :], dec[:, 2, :], ALU.add)
                            dve.drain()
                            for j, (kind, jt) in enumerate(tiles):
                                dve.wait_ge(pe_a.sem, pe_a.at(2 * NJ * hp + (n0 + j + 1)))
                                if kind == "own":
                                    w = e[:, 0, 384 - 128 * jt:384 - 128 * jt + T]
                                else:
                                    w = ec[:, 0, 128 - 128 * jt:128 - 128 * jt + T]
                                last = dve.scalar_tensor_tensor(prob[:, j % 2, 0:T], ps[:, j % 2, 0:T], SC, w, ALU.mult, ALU.mult)
                                last.then_inc(dve_c.sem, 1)
                            dve.wait_ge(pe_b.sem, pe_b.at(6 * hp + (3 * h + 2)))
                            dve.tensor_tensor(o_c, o_s, ps[:, 3, 0:T], ALU.subtract).then_inc(dve_b.sem, 1)
                            dve.wait_ge(root_ready.sem, root_ready.at(2 * hp + (h + 1)))
                            dve.reciprocal(rs, rs)
                            dve.drain()
                            dve.tensor_tensor(o_c, o_c, rs, ALU.mult)
                            dve.drain()
                            gh = g[:, ds(2 * T * hp + h * T, T)]
                            dve.scalar_tensor_tensor(gh, o_c, gn[:, ds(2 * hp + h, 1)], gh, ALU.mult, ALU.mult)
                            dve.drain()


            consts_in.add(32)
            act_a.add(8)
            act_b.add(16)
            root_ready.add(8)
            pe_a.add(8 * NJ)
            pe_b.add(24)
            dve_a.add(4)
            dve_b.add(8)
            dve_c.add(8 * NJ)

        def stage_conformer(m):
            T = m["T"]
            a = m["rest"]
            sq, rs, sg = area(a, 4, T), area(a + 2048, T), area(a + 2560, 4, T)
            hc = m["hc"]
            hc_all = hc.rearrange("p a t -> p (a t)")
            cp_flat = m["cp"].rearrange("p a b -> p (a b)")
            step = T + 2 * HALF
            w, b = par_of("cdw"), par_of("cdb")
            lng, lnb = par_of("clg"), par_of("clb")
            with nc.Block() as block:
                @block.vector
                def _(dve):
                    for c in range(CT4):
                        dve.tensor_scalar(hc[:, c, :], m["cp"][:, c, 0:T], w[:, c * TAPS:c * TAPS + 1], b[:, c:c + 1], ALU.mult, ALU.add)
                    dve.drain()
                    with dve.Fori(1, TAPS) as tap:
                        for c in range(CT4):
                            dve.scalar_tensor_tensor(hc[:, c, :], cp_flat[:, ds(tap + c * step, T)], w[:, ds(tap + c * TAPS, 1)],
                                                     hc[:, c, :], ALU.mult, ALU.add)
                        dve.drain()
                    dve.drain().then_inc(dve_a.sem, 1)
                    dve.wait_ge(pe_a.sem, pe_a.at(1))
                    dve.tensor_tensor(hc, hc, ps[:, 4, 0:T].unsqueeze(1).broadcast_to([P, 4, T]), ALU.subtract).then_inc(dve_a.sem, 1)
                    dve.wait_ge(root_ready.sem, root_ready.at(1))
                    dve.reciprocal(rs, rs)
                    dve.drain()
                    dve.tensor_tensor(hc, hc, rs.unsqueeze(1).broadcast_to([P, 4, T]), ALU.mult)
                    dve.drain()
                    for c in range(CT4):
                        last = dve.tensor_scalar(hc[:, c, :], hc[:, c, :], lng[:, c:c + 1], lnb[:, c:c + 1], ALU.mult, ALU.add)
                    last.then_inc(dve_a.sem, 1)
                    dve.wait_ge(act_a.sem, act_a.at(2))
                    dve.tensor_tensor(hc, hc, sg, ALU.mult)

                @block.scalar
                def _(act):
                    act.wait_ge(dve_a.sem, dve_a.at(2))
                    act.activation(sq, hc, ACT.Square).then_inc(act_a.sem, 1)
                    act.wait_ge(pe_a.sem, pe_a.at(2))
                    act.activation(rs, ps[:, 5, 0:T], ACT.Sqrt, bias=eps).then_inc(root_ready.sem, 1)
                    act.wait_ge(dve_a.sem, dve_a.at(3))
                    act.activation(sg, hc, ACT.Sigmoid).then_inc(act_a.sem, 1)

                @block.tensor
                def _(pe):
                    pe.wait_ge(dve_a.sem, dve_a.at(1))
                    for c in range(CT4):
                        last = pe.matmul(ps[:, 4, 0:T], mean_c, hc[:, c, :], start=c == 0, stop=c == CT4 - 1)
                    last.then_inc(pe_a.sem, 1)
                    pe.wait_ge(act_a.sem, act_a.at(1))
                    for c in range(CT4):
                        last = pe.matmul(ps[:, 5, 0:T], mean_c, sq[:, c, :], start=c == 0, stop=c == CT4 - 1)
                    last.then_inc(pe_a.sem, 1)
            pe_a.add(2)
            root_ready.add(1)
            act_a.add(2)
            dve_a.add(3)

        def stage_hyena(s, m):
            T, nt = m["T"], m["nt"]
            a = m["rest"]
            hs = area(a, 12, T)
            hs_flat = area(a, 12 * T)
            y = area(a + 6144, nt, 2, 512)
            tmp = area(a + 10240, 2, 512)
            spec = m["hp_flat"][:, 0:nt * 1024].rearrange("p (k r c) -> p k r c", r=2, c=512)
            ztm = m["hp_flat"][:, 4096:4096 + nt * 512].rearrange("p (a b) -> p a b", b=512)
            fwd = area(M0 + 4096, nt, 2, T)
            inv = area(M0 + 8192, nt, 2, T)
            k_dft = k_dft_x if s == "X" else k_dft_c
            w, b, bias = par_of("hsw"), par_of("hsb"), par_of("hbias")
            z = hs[:, 0:4, :]
            with nc.Block() as block:
                @block.sync
                def _(sp):
                    sp.dma_start(fwd.rearrange("p a b c -> p (a b c)"), k_dft[0]).then_inc(consts_in.sem, 16)
                    sp.dma_start(inv.rearrange("p a b c -> p (a b c)"), k_dft[1]).then_inc(consts_in.sem, 16)
                    with sp.Fori(0, 2) as o:
                        sp.wait_ge(dve_a.sem, dve_a.at(o + 1))
                        sp.dma_start(spec.rearrange("p k r c -> p (k r c)"),
                                     spec_d[SEG[s], ds(o, 1), :, 0:nt * 1024].rearrange("o p n -> p (o n)")).then_inc(gates_in[0].sem, 16)

                @block.vector
                def _(dve):
                    for c in range(12):
                        dve.tensor_scalar(hs[:, c, :], m["hp"][:, c, 0:T], w[:, c:c + 1], b[:, c:c + 1], ALU.mult, ALU.add)
                    dve.drain()
                    for tap in (1, 2):
                        for c in range(12):
                            last = dve.scalar_tensor_tensor(hs[:, c, :], m["hp"][:, c, tap:tap + T], w[:, tap * 12 + c:tap * 12 + c + 1],
                                                            hs[:, c, :], ALU.mult, ALU.add)
                        if tap == 1:
                            dve.drain()
                    last.then_inc(dve_a.sem, 1)
                    dve.drain().then_inc(dve_c.sem, 1)
                    with dve.Fori(0, 2) as o:
                        for n in range(nt):
                            dve.wait_ge(pe_a.sem, pe_a.at(nt * o + (n + 1)))
                            dve.tensor_copy(ztm[:, n, :], ps[:, n % 4, :]).then_inc(dve_b.sem, 1)
                        dve.wait_ge(gates_in[0].sem, gates_in[0].at(16 * o + 16))
                        for k in range(nt):
                            dve.wait_ge(pe_b.sem, pe_b.at((nt + 4) * o + (k + 1)))
                            zr, zi = ps[:, 4 + 2 * (k % 2), :], ps[:, 5 + 2 * (k % 2), :]
                            dve.tensor_tensor(y[:, k, 0, :], zr, spec[:, k, 0, :], ALU.mult)
                            dve.tensor_tensor(tmp[:, 0, :], zi, spec[:, k, 1, :], ALU.mult)
                            dve.tensor_tensor(y[:, k, 1, :], zr, spec[:, k, 1, :], ALU.mult)
                            dve.tensor_tensor(tmp[:, 1, :], zi, spec[:, k, 0, :], ALU.mult)
                            dve.drain()
                            dve.tensor_tensor(y[:, k, 0, :], y[:, k, 0, :], tmp[:, 0, :], ALU.subtract)
                            last = dve.tensor_tensor(y[:, k, 1, :], y[:, k, 1, :], tmp[:, 1, :], ALU.add)
                            last.then_inc(dve_b.sem, 1)
                            dve.drain()
                        dve.drain().then_inc(dve_a.sem, 1)
                        for c in range(4):
                            dve.wait_ge(pe_b.sem, pe_b.at((nt + 4) * o + (nt + c + 1)))
                            zc = z[:, c, :]
                            dve.scalar_tensor_tensor(zc, zc, bias[:, ds(4 * o + c, 1)], ps[:, c, 0:T], ALU.mult, ALU.add)
                            dve.drain()
                            dve.tensor_tensor(zc, zc, hs_flat[:, ds(4 * T * o + (4 + c) * T, T)], ALU.mult).then_inc(dve_c.sem, 1)

                @block.tensor
                def _(pe):
                    pe.wait_ge(consts_in.sem, consts_in.at(32))
                    with pe.Fori(0, 2) as o:
                        pe.wait_ge(dve_c.sem, dve_c.at(4 * o + 1))
                        for n in range(nt):
                            for c in range(4):
                                last = pe.transpose(ps[:, n % 4, c * P:(c + 1) * P], z[:, c, n * P:(n + 1) * P], ident)
                            last.then_inc(pe_a.sem, 1)
                        pe.wait_ge(dve_b.sem, dve_b.at(2 * nt * o + nt))
                        for k in range(nt):
                            if k >= 2:
                                pe.wait_ge(dve_b.sem, dve_b.at(2 * nt * o + (nt + k - 1)))
                            for r in range(2):
                                for n in range(nt):
                                    last = pe.matmul(ps[:, 4 + 2 * (k % 2) + r, :], fwd[:, n, r, k * P:(k + 1) * P], ztm[:, n, :],
                                                     start=n == 0, stop=n == nt - 1)
                            last.then_inc(pe_b.sem, 1)
                        pe.wait_ge(dve_b.sem, dve_b.at(2 * nt * o + 2 * nt))
                        for c in range(4):
                            for k in range(nt):
                                for r in range(2):
                                    last = pe.matmul(ps[:, c, 0:T], y[:, k, r, c * P:(c + 1) * P], inv[:, k, r, :],
                                                     start=k == r == 0, stop=(k, r) == (nt - 1, 1))
                            last.then_inc(pe_b.sem, 1)
            consts_in.add(32)
            gates_in[0].add(32)
            pe_a.add(2 * nt)
            pe_b.add(2 * (nt + 4))
            dve_a.add(3)
            dve_b.add(4 * nt)
            dve_c.add(9)

        def stage_merge_retention(s, m):
            T = m["T"]
            tmp = area(m["rest"] + 6144, 4, T)
            g = m["g"].rearrange("p (a t) -> p a t", t=T)
            mg = m["merged"].rearrange("p a t -> p (a t)")
            with nc.Block() as block:
                @block.sync
                def _(sp):
                    load_ahead(sp, 16)

                @block.tensor
                def _(pe):
                    with pe.Fori(0, 4) as i:
                        for k in range(4):
                            pe.wait_ge(loaded[k].sem, loaded[k].at(16 * i + 16))
                            pe.wait_ge(bank_free.sem, bank_free.at(4 * i + (k + 1)))
                            x = m["u"] if k % 2 == 0 else g
                            for kc in range(KC):
                                last = pe.matmul(ps[:, k, 0:T], ring[:, k, kc * P:(kc + 1) * P], x[:, kc, :],
                                                 start=kc == 0, stop=kc == KC - 1)
                            last.then_inc(blocks_done.sem, 1)

                @block.scalar
                def _(act):
                    with act.Fori(0, 4) as i:
                        for k in (0, 2):
                            act.wait_ge(blocks_done.sem, blocks_done.at(4 * i + (k + 1)))
                            act.wait_ge(bank_free.sem, bank_free.at(4 * i + (k + 1)))
                            act.activation(tmp[:, k, :], ps[:, k, 0:T], ACT.Sigmoid).then_inc(gate_ready.sem, 1)

                @block.vector
                def _(dve):
                    with dve.Fori(0, 4) as i:
                        for k in (1, 3):
                            dve.wait_ge(blocks_done.sem, blocks_done.at(4 * i + (k + 1)))
                            dve.wait_ge(gate_ready.sem, gate_ready.at(2 * i + (k + 1) // 2))
                            dve.tensor_tensor(mg[:, ds(2 * T * i + (k // 2) * T, T)], ps[:, k, 0:T], tmp[:, k - 1, :], ALU.mult)\
                               .then_inc(bank_free.sem, 2)
            gate_ready.add(8)
            streamed(16, 16)

        def stage_merge_others(s, m):
            T = m["T"]
            z = area(m["rest"], 12, T)[:, 0:4, :]
            tmp = area(m["rest"] + 6144, 4, T)
            part = area(m["rest"] + 8192, 4, T)
            mg = m["merged"].rearrange("p a t -> p (a t)")
            with nc.Block() as block:
                @block.sync
                def _(sp):
                    load_ahead(sp, 24)

                @block.tensor
                def _(pe):
                    with pe.Fori(0, 2) as i:
                        for n in range(12):
                            k, c, kind = n % 4, n // 3, n % 3
                            pe.wait_ge(loaded[k].sem, loaded[k].at(48 * i + (16 * (n // 4) + 16)))
                            if kind < 2:
                                bank = 2 * (c % 2) + kind
                                pe.wait_ge(bank_free.sem, bank_free.at(12 * i + (3 * c + 1)))
                                for kc in range(KC):
                                    last = pe.matmul(ps[:, bank, 0:T], ring[:, k, kc * P:(kc + 1) * P], m["u"][:, kc, :],
                                                     start=kc == 0, stop=kc == KC - 1)
                            else:
                                bank = 4 + 2 * (c % 2)
                                for kc in range(4):
                                    pe.matmul(ps[:, bank, 0:T], ring[:, k, kc * P:(kc + 1) * P], m["hc"][:, kc, :],
                                              start=kc == 0, stop=kc == 3)
                                for kc in range(4):
                                    last = pe.matmul(ps[:, bank + 1, 0:T], ring[:, k, (4 + kc) * P:(5 + kc) * P], z[:, kc, :],
                                                     start=kc == 0, stop=kc == 3)
                            last.then_inc(blocks_done.sem, 1)

                @block.scalar
                def _(act):
                    with act.Fori(0, 2) as i:
                        for n in range(12):
                            c, kind = n // 3, n % 3
                            if kind == 2:
                                continue
                            act.wait_ge(blocks_done.sem, blocks_done.at(12 * i + (n + 1)))
                            act.activation(tmp[:, 2 * (c % 2) + kind, :], ps[:, 2 * (c % 2) + kind, 0:T], ACT.Sigmoid)\
                               .then_inc(gate_ready.sem, 1)

                @block.vector
                def _(dve):
                    with dve.Fori(0, 2) as i:
                        for c in range(4):
                            dve.wait_ge(gate_ready.sem, gate_ready.at(8 * i + (2 * c + 2)))
                            dve.wait_ge(blocks_done.sem, blocks_done.at(12 * i + (3 * c + 3)))
                            for r in range(2):
                                dve.tensor_tensor(part[:, 2 * (c % 2) + r, :], ps[:, 4 + 2 * (c % 2) + r, 0:T], tmp[:, 2 * (c % 2) + r, :], ALU.mult)
                            dve.drain()
                            dve.tensor_tensor(part[:, 2 * (c % 2), :], part[:, 2 * (c % 2), :], part[:, 2 * (c % 2) + 1, :], ALU.add)
                            dve.drain()
                            x = mg[:, ds(4 * T * i + c * T, T)]
                            dve.tensor_tensor(x, x, part[:, 2 * (c % 2), :], ALU.add).then_inc(bank_free.sem, 3)
            gate_ready.add(16)
            streamed(24, 24)

        def stage_linear(s, x, evacuate):
            T = T_OF[s]
            with nc.Block() as block:
                @block.sync
                def _(sp):
                    load_ahead(sp, 8)

                @block.tensor
                def _(pe):
                    pe_linear(pe, 0, 8, x, T)

                @block.vector
                def _(dve):
                    with dve.Fori(0, 2) as i:
                        for k in range(4):
                            dve.wait_ge(blocks_done.sem, blocks_done.at(4 * i + (k + 1)))
                            evacuate(dve, i, k).then_inc(bank_free.sem, 1)
            streamed(8, 8)

        mod_flat = mod.rearrange("p a b -> p (a b)")

        def stage_out(s, m):
            T = T_OF[s]

            def add(dve, i, k):
                x = res_flat[s][:, ds(4 * T * i + k * T, T)]
                gate = mod_flat[:, ds(8 * i + (2 * (16 + k) + SEG[s]), 1)]
                return dve.scalar_tensor_tensor(x, ps[:, k, 0:T], gate, x, ALU.mult, ALU.add)

            stage_linear(s, m["merged"], add)

        def mixer(l, s):
            m = places(s)
            stage_norm(s, 0, m["u"], area(m["rest"], T_OF[s]))
            stage_project(s, m, True)
            if s == "X":
                stage_rope(m)
            stage_retention(s, m)
            stage_conformer(m)
            stage_hyena(s, m)
            stage_merge_retention(s, m)
            stage_merge_others(s, m)
            stage_out(s, m)

        TOK = SEQ + CTX
        off = {"X": 0, "C": SEQ}
        ht = area(M0, KC, TOK)
        acc = area(M0 + 6144, KC, TOK)
        acc_flat = area(M0 + 6144, KC * TOK)
        gate_block = area(M0 + 12288, NK, P)
        qp = area(M0 + 28672, 8 * SEQ)
        keys_sb = area(M0 + 32768, 8, 256)
        small = M0 + 34816

        def stage_select(l, s):
            T = T_OF[s]
            nt = T // P
            q_s = area(small, 8, P)
            top = area(small + 1024, 8, 2, TOPK)
            top_i = area(small + 1280, 8, 2, TOPK)
            top_u = top_i.bitcast(U32)
            top_f = area(small + 1536, 8, 2, TOPK)
            best = area(small + 1792, 8, TOPK)
            best_u = area(small + 1920, 8, TOPK).bitcast(U32)
            half_u = area(small + 2048, 2, 128).bitcast(U32)
            half_f = area(small + 2304, 2, 8, TOPK)
            picked = area(small + 2560, 3, 128)
            picked_t = area(small + 2944, 3, 128)
            total = area(small + 3328, 8)
            a = M0 + 6144
            sc, sc2, cand = area(a, 8, 2, NK), area(a + 2048, 8, 2, NK), area(a + 4096, 8, 256)
            cand2 = area(M0 + 12288, 8, 256)
            hot = area(a, 8, 2, NK)
            match = area(a, 8, TOPK, TOPK)
            q3 = qp[:, 0:8 * T].rearrange("p (h t) -> p h t", t=T)
            iota16 = iota[:, 0:TOPK].unsqueeze(1).unsqueeze(1).broadcast_to([P, 8, TOPK, TOPK])

            with nc.Block() as block:
                @block.sync
                def _(sp):
                    sp.dma_start(keys_sb.rearrange("p a b -> p (a b)"), keys[l]).then_inc(consts_in.sem, 16)
                    with sp.Fori(0, nt) as tt:
                        sp.wait_ge(act_b.sem, act_b.at(32 * tt + 32))
                        sp.dma_start(gate_d[:, :, ds(P * tt + off[s], P)].rearrange("i p t -> p i t"), gate_block)\
                          .then_inc(store_done.sem, 16)
                    sp.wait_ge(store_done.sem, store_done.at(16 * nt))

                @block.tensor
                def _(pe):
                    pe.wait_ge(consts_in.sem, consts_in.at(16))
                    with pe.Fori(0, nt) as tt:
                        pe.wait_ge(dve_a.sem, dve_a.at(2 * tt + 1))
                        for h in range(8):
                            last = pe.matmul(ps[:, h // 2, (h % 2) * 256:(h % 2) * 256 + 256], q_s[:, h, :], keys_sb[:, h, :],
                                             start=True, stop=True)
                        last.then_inc(pe_a.sem, 1)
                        pe.wait_ge(dve_a.sem, dve_a.at(2 * tt + 2))
                        for n in range(3):
                            last = pe.transpose(ps[:, 4, n * P:(n + 1) * P], picked[:, n, :], ident)
                        last.then_inc(pe_a.sem, 1)
                        with pe.Fori(0, P // 8) as tg:
                            for q in range(8):
                                if q % 4 == 0:
                                    pe.wait_ge(act_b.sem, act_b.at(32 * tt + 2 * tg + (q // 4 - 1)))
                                pe.wait_ge(dve_b.sem, dve_b.at(P * tt + 8 * tg + (q + 1)))
                                pe.matmul(ps[:, 5 + q // 4, (q % 4) * P:(q % 4 + 1) * P], hot[:, q, 1, :], hot[:, q, 0, :],
                                          start=True, stop=True).then_inc(pe_b.sem, 1)

                @block.scalar
                def _(act):
                    with act.Fori(0, nt) as tt:
                        act.wait_ge(pe_a.sem, pe_a.at(2 * tt + 1))
                        act.activation(sc.rearrange("p a b c -> p (a b c)"), ps[:, 0:4, :].rearrange("p a b -> p (a b)"), ACT.Copy)\
                           .then_inc(act_a.sem, 1)
                        act.wait_ge(dve_c.sem, dve_c.at(tt + 1))
                        act.activation(best, best, ACT.Exp).then_inc(act_a.sem, 1)
                        act.wait_ge(store_done.sem, store_done.at(16 * tt))
                        with act.Fori(0, P // 8) as tg:
                            for q in range(2):
                                act.wait_ge(pe_b.sem, pe_b.at(P * tt + 8 * tg + (4 * q + 4)))
                                act.activation(gate_block[:, :, ds(8 * tg + 4 * q, 4)],
                                               ps[:, 5 + q, :].rearrange("p (t i) -> p i t", t=4), ACT.Copy).then_inc(act_b.sem, 1)

                @block.vector
                def _(dve):
                    with dve.Fori(0, nt) as tt:
                        dve.tensor_copy(q_s, q3[:, :, ds(P * tt, P)]).then_inc(dve_a.sem, 1)
                        dve.wait_ge(act_a.sem, act_a.at(2 * tt + 1))
                        dve.memset(total, 0.0)
                        for h in range(8):
                            for r in range(2):
                                dve.max(top[:, h, r, 0:8], sc[:, h, r, :])
                        dve.drain()
                        for h in range(8):
                            for r in range(2):
                                dve.match_replace(sc2[:, h, r, :], top[:, h, r, 0:8], sc[:, h, r, :], LOW)
                                dve.max_index(top_u[:, h, r, 0:8], top[:, h, r, 0:8], sc[:, h, r, :])
                        dve.drain()
                        for h in range(8):
                            for r in range(2):
                                dve.max(top[:, h, r, 8:16], sc2[:, h, r, :])
                        dve.drain()
                        for h in range(8):
                            for r in range(2):
                                dve.max_index(top_u[:, h, r, 8:16], top[:, h, r, 8:16], sc2[:, h, r, :])
                        dve.tensor_tensor(cand.rearrange("p h (a b) -> p h a b", b=TOPK),
                                          top[:, :, 0, :].unsqueeze(3).broadcast_to([P, 8, TOPK, TOPK]),
                                          top[:, :, 1, :].unsqueeze(2).broadcast_to([P, 8, TOPK, TOPK]), ALU.add)
                        dve.drain()
                        dve.wait_ge(store_done.sem, store_done.at(16 * tt))
                        dve.tensor_copy(top_f, top_u)
                        for h in range(8):
                            dve.max(best[:, h, 0:8], cand[:, h, :])
                        dve.drain()
                        for h in range(8):
                            dve.match_replace(cand2[:, h, :], best[:, h, 0:8], cand[:, h, :], LOW)
                            dve.max_index(best_u[:, h, 0:8], best[:, h, 0:8], cand[:, h, :])
                        dve.drain()
                        for h in range(8):
                            dve.max(best[:, h, 8:16], cand2[:, h, :])
                        dve.drain()
                        for h in range(8):
                            dve.max_index(best_u[:, h, 8:16], best[:, h, 8:16], cand2[:, h, :])
                        dve.tensor_copy(total, best[:, :, 0])
                        dve.drain()
                        dve.tensor_tensor(best, best, total.unsqueeze(2).broadcast_to([P, 8, TOPK]), ALU.subtract)\
                           .then_inc(dve_c.sem, 1)
                        flat_u = best_u.rearrange("p h k -> p (h k)")
                        dve.tensor_scalar(half_u[:, 0, :], flat_u, 4, None, ALU.logical_shift_right)
                        dve.tensor_scalar(half_u[:, 1, :], flat_u, 15, None, ALU.bitwise_and)
                        dve.drain()
                        dve.tensor_copy(half_f.rearrange("p r h k -> p r (h k)"), half_u)
                        dve.drain()
                        for r in range(2):
                            dve.tensor_tensor(match, half_f[:, r].unsqueeze(3).broadcast_to([P, 8, TOPK, TOPK]), iota16, ALU.is_equal)
                            dve.drain()
                            dve.tensor_tensor(match, match, top_f[:, :, r, :].unsqueeze(2).broadcast_to([P, 8, TOPK, TOPK]), ALU.mult)
                            dve.drain()
                            dve.tensor_reduce(picked[:, r, :].rearrange("p (h k) -> p h k", k=TOPK), match, AX.X, ALU.add)
                            dve.drain()
                        dve.wait_ge(act_a.sem, act_a.at(2 * tt + 2))
                        dve.tensor_reduce(total, best, AX.X, ALU.add)
                        dve.drain()
                        dve.reciprocal(total, total)
                        dve.drain()
                        dve.tensor_tensor(picked[:, 2, :].rearrange("p (h k) -> p h k", k=TOPK), best,
                                          total.unsqueeze(2).broadcast_to([P, 8, TOPK]), ALU.mult).then_inc(dve_a.sem, 1)
                        dve.wait_ge(pe_a.sem, pe_a.at(2 * tt + 2))
                        dve.tensor_copy(picked_t.rearrange("p a b -> p (a b)"), ps[:, 4, 0:384])
                        dve.drain()
                        pick_i, pick_j, pick_g = (picked_t[:, n, :] for n in range(3))
                        with dve.Fori(0, P // 8) as tg:
                            for q in range(8):
                                dve.wait_ge(pe_b.sem, pe_b.at(P * tt + 8 * tg + (q - 7)))
                                dve.tensor_scalar(hot[:, q, 0, :], iota, pick_i[:, ds(8 * tg + q, 1)], pick_g[:, ds(8 * tg + q, 1)],
                                                  ALU.is_equal, ALU.mult)
                                dve.tensor_scalar(hot[:, q, 1, :], iota, pick_j[:, ds(8 * tg + q, 1)], None, ALU.is_equal)\
                                   .then_inc(dve_b.sem, 1)
                        dve.wait_ge(pe_b.sem, pe_b.at(P * tt + P))
            consts_in.add(16)
            store_done.add(16 * nt)
            pe_a.add(2 * nt)
            pe_b.add(P * nt)
            act_a.add(2 * nt)
            act_b.add(32 * nt)
            dve_a.add(2 * nt)
            dve_b.add(P * nt)
            dve_c.add(nt)

        def split_tensor(name, at, *shape):
            return nc.alloc_sbuf_tensor_at(name, [P] + list(shape), F32R, offset=sb_at + 4 * at)

        F0 = M0 + 12288
        h_hi = split_tensor("h_hi", F0, KC, TOK)
        h_lo = split_tensor("h_lo", F0 + 6144, KC, TOK)
        ring_hi = split_tensor("ring_hi", F0 + 12288, 4, 1024)
        w_hi = split_tensor("w_hi", F0 + 16384, 2, TOK)
        w_lo = split_tensor("w_lo", F0 + 17920, 2, TOK)
        ring_lo = split_tensor("ring_lo", 9216, 4, 1024)

        def stage_split(T):
            with nc.Block() as block:
                @block.scalar
                def _(act):
                    for kc in range(KC):
                        act.activation(h_hi[:, kc, 0:T], ht[:, kc, 0:T], ACT.Copy).then_inc(act_a.sem, 1)

                @block.vector
                def _(dve):
                    for kc in range(KC):
                        dve.wait_ge(act_a.sem, act_a.at(kc + 1))
                        dve.tensor_tensor(h_lo[:, kc, 0:T], ht[:, kc, 0:T], h_hi[:, kc, 0:T].bitcast(F32), ALU.subtract)
            act_a.add(KC)

        def stage_experts(l, segs):
            T = sum(T_OF[s] for s in segs)
            halves = [(0, T // 2), (T // 2, T // 2)]
            a = M0
            gt = area(a, 2, 2, TOK)
            w = area(a + 3072, 2, TOK)
            N = NK // 2
            kinds = order[place[0] + 4:place[0] + 8]

            with nc.Block() as block:
                @block.sync
                def _(sp):
                    def load_u(n, k):
                        for r in range(2):
                            sp.wait_ge(pe_a.sem, pe_a.at(2 * n + (2 * k + r - 1)))
                            sp.dma_start(ring[:, r, :], peer_u[l, ds(2 * n + (2 * k + r), 1)].rearrange("o p n -> p (o n)"))\
                              .then_inc(loaded[r].sem, 16)

                    def load_v(n, k):
                        sp.wait_ge(pe_b.sem, pe_b.at(8 * n + 8 * k))
                        for r in range(2):
                            sp.dma_start(ring[:, 2 + r, :], peer_v[l, ds(2 * n + (2 * k + r), 1)].rearrange("o p n -> p (o n)"))\
                              .then_inc(loaded[2 + r].sem, 16)

                    def load_gates(n, k):
                        sp.dma_start(gt[:, k % 2, :, 0:T], gate_d[ds(2 * n + 2 * k, 2), :, 0:T].rearrange("i p t -> p i t"))\
                          .then_inc(gates_in[k % 2].sem, 16)

                    load_gates(0, 0)
                    load_gates(0, 1)
                    load_u(0, 1)
                    with sp.Fori(0, (N - 2) // 2) as pair:
                        n = 2 * pair
                        for k in range(2):
                            load_u(n, k + 2)
                            sp.wait_ge(w_ready.sem, w_ready.at(2 * n + (2 * k + 2)))
                            load_gates(n, k + 2)
                            load_v(n, k + 1)
                    load_v(N - 2, 1)
                    for k, entry in enumerate(kinds):
                        if k < 2:
                            sp.wait_ge(pe_a.sem, pe_a.at(2 * N - 1 + k))
                        else:
                            sp.wait_ge(pe_b.sem, pe_b.at(8 * N))
                        sp.dma_start(ring[:, k, :], block_of(entry)).then_inc(loaded[k].sem, 16)

                @block.tensor
                def _(pe):
                    def products(out, lhs, rhs, first, last):
                        for j, (x, y) in enumerate(((0, 0), (0, 1), (1, 0))):
                            done = pe.matmul(out, lhs[x], rhs[y], start=first and j == 0, stop=last and j == 2)
                        return done

                    def a_of(n, k):
                        for r in range(2):
                            pe.wait_ge(u_split.sem, u_split.at(2 * n + (2 * k + r + 1)))
                            pe.wait_ge(act_a.sem, act_a.at(2 * n + (2 * k + r - 1)))
                            for p, (t0, t) in enumerate(halves):
                                for kc in range(KC):
                                    c = slice(kc * P, (kc + 1) * P)
                                    last = products(ps[:, 2 * r + p, 0:t], (ring_hi[:, r, c], ring_lo[:, r, c]),
                                                    (h_hi[:, kc, t0:t0 + t], h_lo[:, kc, t0:t0 + t]), kc == 0, kc == KC - 1)
                            last.then_inc(pe_a.sem, 1)

                    def o_of(n, k):
                        pe.wait_ge(v_split.sem, v_split.at(2 * n + (2 * k + 2)))
                        pe.wait_ge(w_ready.sem, w_ready.at(2 * n + (2 * k + 2)))
                        for dc in range(KC):
                            pe.wait_ge(dve_c.sem, dve_c.at(8 * n + (8 * k + dc - 1)))
                            c = slice(dc * P, (dc + 1) * P)
                            for p, (t0, t) in enumerate(halves):
                                for r in range(2):
                                    last = products(ps[:, 4 + 2 * (dc % 2) + p, 0:t], (ring_hi[:, 2 + r, c], ring_lo[:, 2 + r, c]),
                                                    (w_hi[:, r, t0:t0 + t], w_lo[:, r, t0:t0 + t]), r == 0, r == 1)
                            last.then_inc(pe_b.sem, 1)

                    a_of(0, 0)
                    with pe.Fori(0, (N - 2) // 2) as pair:
                        n = 2 * pair
                        for k in range(2):
                            a_of(n, k + 1)
                            o_of(n, k)
                    a_of(N - 2, 1)
                    o_of(N - 2, 0)
                    o_of(N - 2, 1)

                @block.scalar
                def _(act):
                    def round_block(n, k, first):
                        for r in range(2):
                            slot = first + r
                            act.wait_ge(loaded[slot].sem, loaded[slot].at(16 * n + (16 * k + 16)))
                            act.activation(ring_hi[:, slot, :], ring[:, slot, :], ACT.Copy)\
                               .then_inc((u_hi if first == 0 else v_hi).sem, 1)

                    def gelu(n, k):
                        for r in range(2):
                            act.wait_ge(pe_a.sem, pe_a.at(2 * n + (2 * k + r + 1)))
                            act.wait_ge(w_ready.sem, w_ready.at(2 * n + 2 * k))
                            act.activation(w[:, r, 0:T].rearrange("p (a b) -> p a b", a=2), ps[:, 2 * r:2 * r + 2, 0:T // 2],
                                           ACT.Gelu_apprx_tanh).then_inc(act_a.sem, 1)

                    round_block(0, 0, 0)
                    round_block(0, 0, 2)
                    gelu(0, 0)
                    round_block(0, 1, 0)
                    with act.Fori(0, (N - 2) // 2) as pair:
                        n = 2 * pair
                        for k in range(2):
                            gelu(n, k + 1)
                            round_block(n, k + 2, 0)
                            round_block(n, k + 1, 2)
                    gelu(N - 2, 1)
                    round_block(N - 2, 1, 2)

                @block.vector
                def _(dve):
                    def rest_of_block(n, k, first, r):
                        hi, done = (u_hi, u_split) if first == 0 else (v_hi, v_split)
                        slot = first + r
                        dve.wait_ge(hi.sem, hi.at(2 * n + (2 * k + r + 1)))
                        dve.tensor_tensor(ring_lo[:, slot, :], ring[:, slot, :], ring_hi[:, slot, :].bitcast(F32), ALU.subtract)\
                           .then_inc(done.sem, 1)

                    def weigh(n, k):
                        dve.wait_ge(gates_in[k % 2].sem, gates_in[k % 2].at(8 * n + (16 * (k // 2) + 16)))
                        for r in range(2):
                            dve.wait_ge(act_a.sem, act_a.at(2 * n + (2 * k + r + 1)))
                            dve.tensor_tensor(w[:, r, 0:T], w[:, r, 0:T], gt[:, k % 2, r, 0:T], ALU.mult)
                        dve.drain()
                        for r in range(2):
                            dve.tensor_copy(w_hi[:, r, 0:T], w[:, r, 0:T])
                        dve.drain()
                        for r in range(2):
                            dve.tensor_tensor(w_lo[:, r, 0:T], w[:, r, 0:T], w_hi[:, r, 0:T].bitcast(F32), ALU.subtract)\
                               .then_inc(w_ready.sem, 1)

                    def gather(n, k, dc):
                        dve.wait_ge(pe_b.sem, pe_b.at(8 * n + (8 * k + dc + 1)))
                        x = acc[:, dc, 0:T].rearrange("p (a b) -> p a b", a=2)
                        b = 4 + 2 * (dc % 2)
                        dve.tensor_tensor(x, x, ps[:, b:b + 2, 0:T // 2], ALU.add).then_inc(dve_c.sem, 1)

                    def step(n, k, more):
                        for dc in range(KC):
                            gather(n, k, dc)
                            if more and dc in (4, 5):
                                rest_of_block(n, k + 2, 0, dc - 4)
                        weigh(n, k + 1)
                        for r in range(2):
                            rest_of_block(n, k + 1, 2, r)

                    dve.memset(acc_flat, 0.0)
                    for first in (0, 2):
                        for r in range(2):
                            rest_of_block(0, 0, first, r)
                    weigh(0, 0)
                    for r in range(2):
                        rest_of_block(0, 1, 0, r)
                    with dve.Fori(0, (N - 2) // 2) as pair:
                        n = 2 * pair
                        for k in range(2):
                            step(n, k, True)
                    step(N - 2, 0, False)
                    for dc in range(KC):
                        gather(N - 2, 1, dc)
                    dve.drain()
                    for s in segs:
                        for kc in range(KC):
                            x = res[s][:, kc, :]
                            dve.scalar_tensor_tensor(x, acc[:, kc, off[s]:off[s] + T_OF[s]], mod[:, 40 + kc, SEG[s]:SEG[s] + 1], x,
                                                     ALU.mult, ALU.add)
            for k in range(4):
                loaded[k].add(16 * N)
            place[0] += 4
            for c in (pe_a, act_a, u_hi, v_hi, u_split, v_split, w_ready):
                c.add(2 * N)
            pe_b.add(8 * N)
            dve_c.add(8 * N)
            for g in gates_in:
                g.add(16 * N // 2)

        def peer(l, segs):
            for s in segs:
                x = ht[:, :, off[s]:off[s] + T_OF[s]]
                stage_norm(s, 1, x, area(small, T_OF[s]))

                def keep(dve, i, k, T=T_OF[s]):
                    return dve.tensor_copy(qp[:, ds(4 * T * i + k * T, T)], ps[:, k, 0:T])

                stage_linear(s, x, keep)
                stage_select(l, s)
            T = sum(T_OF[s] for s in segs)
            stage_split(T)
            stage_experts(l, segs)

        for l in range(DEPTH):
            last = l == DEPTH - 1
            stage_ada(l)
            if not last:
                stage_filters(l, "C")
            stage_filters(l, "X")
            if not last:
                mixer(l, "C")
            else:
                m = places("C")
                stage_norm("C", 0, m["u"], area(m["rest"], CTX))
                stage_project("C", m, False)
            mixer(l, "X")
            peer(l, ("X",) if last else ("X", "C"))
        m = places("X")
        stage_norm("X", 2, m["u"], area(m["rest"], SEQ))
        with nc.Block() as block:
            @block.sync
            def _(sp):
                sp.dma_start(out, m["u"].rearrange("p a b -> p (a b)")).then_inc(store_done.sem, 16)
                sp.wait_ge(store_done.sem, store_done.at(16))


def _chunks(a):
    a = np.asarray(a)
    return np.swapaxes(a.reshape(a.shape[:-1] + (a.shape[-1] // P, P)), -1, -2)


def _tokens(a):
    return np.ascontiguousarray(np.asarray(a).T.reshape(KC, P, -1).transpose(1, 0, 2).reshape(P, -1))


def _blocks(w):
    w = np.asarray(w)
    n = w.shape[1] // P
    return w.reshape(KC, P, n, P).transpose(2, 1, 0, 3).reshape(n, P, KC * P)


def _constants():
    f = np.float32
    mats = np.zeros((P, 7, P), f)
    mats[:, 0] = np.eye(P)
    for m in range(0, P, 2):
        mats[m + 1, 1, m] = -1.0
        mats[m, 1, m + 1] = 1.0
    mats[:, 2], mats[:, 3], mats[:, 4], mats[:, 5] = 1.0 / D, 1.0 / CW, 1.0 / DV, 1.0
    mats[:, 6] = np.arange(P)
    t = np.arange(SEQ)
    nf = DK // 4
    inv = (10000.0 ** (-np.arange(nf, dtype=f) / f(nf))).astype(f)
    ang = np.concatenate([(t // GRID_W).astype(f)[:, None] * inv, (t % GRID_W).astype(f)[:, None] * inv], 1)
    pair = (np.arange(P) % DK) // 2
    rope = np.stack([np.cos(ang)[:, pair].T, np.sin(ang)[:, pair].T]).astype(f)
    lag = np.arange(896)[None, :] - 384 - np.arange(P)[:, None]
    dec = np.stack([np.maximum(lag, 0), np.maximum(-lag, 0), lag == 0], 1).astype(f)
    c, p = np.arange(640)[None, :], np.arange(P)[:, None]
    decc = np.stack([c - p + CTX - 128, SEQ + 128 - c + p], 1).astype(f)
    got = dict(mats=mats.reshape(P, -1), rope=rope, dec=dec.reshape(P, -1), decc=decc.reshape(P, -1))
    for s, L in (("x", SEQ), ("c", CTX)):
        tt = np.arange(L, dtype=f)
        tn = tt / f(L - 1)
        w = f(2.0 * math.pi) * tt / f(L)
        bands = np.linspace(1e-4, 15, 16, dtype=f)
        feat = np.concatenate([tn[:, None], np.cos(w[:, None] * bands), -np.sin(w[:, None] * bands)], 1)
        got["feat_" + s] = np.ascontiguousarray(feat.T.astype(f))
        deltas = np.abs(np.linspace(math.log(1e-2) / 1.5, math.log(1e-2) / 0.3, HW, dtype=f))
        win = np.exp(-tn[:, None] * deltas[None, :]).astype(f)
        win2 = np.stack([win, win], 1)
        win2[0, 1] = 0.0
        got["win_" + s] = np.ascontiguousarray(win2.reshape(L // P, P, 2 * HW).transpose(1, 0, 2).reshape(P, -1))
        ph = np.pi * np.outer(np.arange(L), np.arange(L) + 0.5) / L
        tab = np.stack([np.cos(ph), -np.sin(ph)], 1)
        back = np.stack([np.cos(ph).T, -np.sin(ph).T], 1)
        got["dft_" + s] = np.stack([x.reshape(L // P, P, 2 * L).transpose(1, 0, 2).reshape(P, -1) for x in (tab, back)]).astype(f)
    return got


def kernel(x, c, ctx, c_ctx, ada_w, ada_b, norm1_g, norm2_g, w_in, ret_decay_logit, ret_gn_g, w_br_ret, conf_dw_w,
           conf_dw_b, conf_ln_g, conf_ln_b, w_br_conf, hy_short_w, hy_short_b, hy_w1, hy_b1, hy_freq, hy_w2, hy_b2,
           hy_w3, hy_b3, hy_bias, w_br_hy, w_out, peer_wq, peer_keys, peer_u, peer_v, final_g):
    import concourse.bacc as bacc
    from concourse.bass_utils import run_bass_kernel_spmd

    A = np.asarray
    x, c, ctx, c_ctx, w_in = A(x), A(c), A(ctx), A(c_ctx), A(w_in)
    mix, par, keys = [], [], []
    for l in range(DEPTH):
        wb = _blocks(w_in[l])
        ret, conf_hy = _blocks(w_br_ret[l]), _blocks(np.concatenate([A(w_br_conf[l]), A(w_br_hy[l])], 0))
        conf, hy, gate = wb[24:32], wb[32:44], wb[44:68]
        order = list(wb[0:24])
        for n in range(4):
            order += [conf[n], conf[4 + n]]
        order += list(hy)
        for n in range(8):
            order += [gate[n], ret[n]]
        for n in range(8):
            order += [gate[8 + n], gate[16 + n], conf_hy[n]]
        order += list(_blocks(w_out[l])) + list(_blocks(peer_wq[l]))
        mix.append(np.stack(order))
        mlp = np.zeros((P, 3), np.float32)
        mlp[0:HID, 0], mlp[0:HID, 1], mlp[0:HID, 2] = A(hy_b1[l]), A(hy_freq[l]), A(hy_b2[l])
        logit = np.broadcast_to(A(ret_decay_logit[l]).reshape(1, 16), (P, 16))
        cdw = _chunks(conf_dw_w[l]).transpose(1, 2, 0).reshape(P, -1)
        hsw = _chunks(hy_short_w[l]).transpose(1, 0, 2).reshape(P, -1)
        hb = _chunks(hy_bias[l]).transpose(1, 0, 2).reshape(P, -1)
        parts = dict(n1=_chunks(norm1_g[l]), n2=_chunks(norm2_g[l]), ada_b=_chunks(ada_b[l]), gn=_chunks(ret_gn_g[l]),
                     cdw=cdw, cdb=_chunks(conf_dw_b[l]), clg=_chunks(conf_ln_g[l]), clb=_chunks(conf_ln_b[l]),
                     hsw=hsw, hsb=_chunks(hy_short_b[l]), hbias=hb, logit=logit, mlp=mlp)
        par.append(np.concatenate([parts[n] for n in _cols], 1))
        kk = np.zeros((P, 8, 256), np.float32)
        for r in range(2):
            kk[64 * r:64 * r + 64, :, 128 * r:128 * r + 128] = A(peer_keys[l])[:, r].transpose(2, 0, 1)
        keys.append(kk.reshape(P, -1))
    k = _constants()
    arrays = {
        "xT": _tokens(x[0]), "cT": np.stack([_chunks(c[0]), _chunks(c_ctx)], 2).reshape(P, 16),
        "ctxT": _tokens(ctx[0]), "final_g": _chunks(final_g),
        "ada": np.stack([_blocks(ada_w[l]) for l in range(DEPTH)]), "mix": np.stack(mix),
        "peer_u": A(peer_u).reshape(DEPTH, NK, P, KC, P).transpose(0, 1, 4, 3, 2).reshape(DEPTH, NK, P, D),
        "peer_v": A(peer_v).reshape(DEPTH, NK, P, D), "par": np.stack(par),
        "hw1": A(hy_w1), "hw2": A(hy_w2),
        "hw3": np.concatenate([A(hy_w3), A(hy_b3)[:, None, :]], 1), "keys": np.stack(keys),
        "k_mats": k["mats"], "k_rope": k["rope"], "k_dec": k["dec"], "k_decc": k["decc"],
        "k_feat_x": k["feat_x"], "k_feat_c": k["feat_c"], "k_win_x": k["win_x"], "k_win_c": k["win_c"],
        "k_dft_x": k["dft_x"], "k_dft_c": k["dft_c"],
    }
    arrays = {n: np.ascontiguousarray(a) for n, a in arrays.items()}
    nc = bacc.Bacc("TRN2", target_bir_lowering=False, num_devices=1)
    args = {n: nc.dram_tensor("in_" + n, a.shape, mybir.dt.from_np(a.dtype), kind="ExternalInput").ap()
            for n, a in arrays.items()}
    out = nc.dram_tensor("out_0", (P, KC * SEQ), F32, kind="ExternalOutput").ap()
    build(nc, out=out, **args)
    r = run_bass_kernel_spmd(nc, [{"in_" + n: a for n, a in arrays.items()}], core_ids=[0])
    got = np.asarray(r.results[0]["out_0"])
    return np.ascontiguousarray(got.reshape(P, KC, SEQ).transpose(2, 1, 0).reshape(1, SEQ, D))
```

```python
import math
from contextlib import ExitStack

import numpy as np
import concourse.bass as bass
from concourse import mybir

F32 = mybir.dt.float32
U32 = mybir.dt.uint32
F32R = mybir.dt.float32r
ALU = mybir.AluOpType
ACT = mybir.ActivationFunctionType
AX = mybir.AxisListType
ds = bass.ds

P = 128
D = 1024
KC = D // P
SEQ, CTX = 512, 256
DEPTH = 2
EPS = 1e-6
GRID_W = 64
HEADS, DK, DV = 8, 64, 128
TAPS, HALF = 31, 15
CW = HW = 512
CT4 = CW // P
EMB, HID = 33, 64
NK = 128
TOPK = 16
NMIX, NQ = 92, 8
LOW = -3.0e38

_cols = dict(n1=8, n2=8, ada_b=48, gn=8, cdw=CT4 * TAPS, cdb=4, clg=4, clb=4, hsw=36, hsb=12,
             hbias=8, logit=16, mlp=3)
PCOL, _at = {}, 0
for _n, _c in _cols.items():
    PCOL[_n] = (_at, _c)
    _at += _c
NPAR = _at


class Count:

    def __init__(self, nc, stack, name):
        self.sem = stack.enter_context(nc.semaphore(name))
        self.base = 0

    def at(self, n):
        return n + self.base

    def add(self, n):
        self.base += n


def build(nc, xT, cT, ctxT, final_g, ada, mix, peer_u, peer_v, par, hw1, hw2, hw3, keys, k_mats, k_rope,
          k_dec, k_decc, k_feat_x, k_feat_c, k_win_x, k_win_c, k_dft_x, k_dft_c, out):
    stack = ExitStack()
    with stack:
        M0 = -(-(14208 + NPAR + 265) // 8) * 8
        kept = stack.enter_context(nc.sbuf_tensor("kept", [P, M0], F32))
        sb_at = nc.sbuf_base - 4 * M0
        arena = stack.enter_context(nc.sbuf_tensor("arena", [P, 53200 - M0], F32))
        ps = stack.enter_context(nc.psum_tensor("psum", [P, 8, 512], F32))
        spec_d = nc.dram_tensor("spec_scratch", (2, 2, P, 4 * 2 * 512), F32, kind="Internal").ap()
        gate_d = nc.dram_tensor("gate_scratch", (NK, P, SEQ + CTX), F32, kind="Internal").ap()

        def new(name):
            return Count(nc, stack, name)

        loaded = [new(f"weights_loaded_{k}") for k in range(4)]
        blocks_done = new("blocks_done")
        bank_free = new("bank_free")
        gate_ready = new("gate_ready")
        consts_in = new("consts_loaded")
        store_done = new("store_done")
        pe_a, pe_b = new("pe_first"), new("pe_second")
        dve_a, dve_b, dve_c = new("dve_first"), new("dve_second"), new("dve_third")
        act_a, act_b = new("act_first"), new("act_second")
        pool_a = new("pool_first")
        tables_used, staged = new("tables_used"), new("pair_staged")
        mean_ready, var_ready, squared = new("mean_ready"), new("variance_ready"), new("squares_ready")
        u_hi, v_hi = new("u_rounded"), new("v_rounded")
        u_split, v_split = new("u_split"), new("v_split")
        block_hi, block_lo = new("block_rounded"), new("block_split")
        w_ready = new("w_split")
        root_ready = new("root_ready")
        gates_in = [new("gates_loaded_0"), new("gates_loaded_1")]

        def flat(at, n):
            return kept[:, at:at + n] if at < M0 else arena[:, at - M0:at - M0 + n]

        def area(at, *shape):
            n = int(np.prod(shape))
            v = flat(at, n)
            if len(shape) == 2:
                v = v.rearrange("p (a b) -> p a b", b=shape[1])
            if len(shape) == 3:
                v = v.rearrange("p (a b c) -> p a b c", b=shape[1], c=shape[2])
            return v

        T_OF = {"X": SEQ, "C": CTX}
        res_flat = {"X": area(0, 4096), "C": area(4096, 2048)}
        res = {s: v.rearrange("p (a t) -> p a t", t=T_OF[s]) for s, v in res_flat.items()}
        ctx_k = area(6144, 4, 256)
        ctx_v = area(7168, 2, 1024)
        ring = area(9216, 4, 1024)
        mats = area(13312, 7, 128)
        ident, rotate, mean_d, mean_c, mean_h, ones, iota = (mats[:, n, :] for n in range(7))
        pars = area(14208, NPAR)
        o = 14208 + NPAR
        mod = area(o, 48, 2)
        amp = area(o + 96, 4, 8)
        cs = area(o + 128, 8, 2)
        cs_sig = area(o + 144, 8, 2)
        lg = area(o + 160, 16)
        lt = area(o + 176, 5, 16)
        fin_g = area(o + 256, 8)
        eps = area(o + 264, 1)
        SEG = {"X": 0, "C": 1}

        def par_of(name):
            a, n = PCOL[name]
            return pars[:, a:a + n]

        runs = []
        for l in range(DEPTH):
            runs.append(("ada", l, 0, 48))
            runs.append(("mix", l, 0, NMIX) if l == 0 else ("mix", l, 4, 12))
            runs.append(("mix", l, 0, NMIX))
            runs += [("mix", l, NMIX, NQ)] * (2 if l == 0 else 1)
            runs.append(("peer", l, 0, 4))
        tables = {"ada": ada, "mix": mix}
        order = [(r, l, n + k) for r, l, n, m in runs for k in range(m)]
        place = [0]

        def block_of(entry):
            kind, l, n = entry
            if kind == "peer":
                return (peer_u, peer_v)[n // 2][l, n % 2]
            return tables[kind][l, n]

        def load_ahead(eng, n):
            at, j = place[0] + 4, 0
            ahead = order[at:at + n]
            while j < len(ahead):
                kind, l, first = ahead[j]
                whole = 4
                while ahead[j + whole - 1:j + whole + 1][1:] == [(kind, l, first + whole)]:
                    whole += 4
                if kind != "peer" and whole > 4:
                    with eng.Fori(0, whole // 4) as i:
                        for k in range(4):
                            eng.wait_ge(blocks_done.sem, blocks_done.at(4 * i + (j + k + 1)))
                            eng.dma_start(ring[:, k, :], tables[kind][l, ds(4 * i + (first + k), 1)].rearrange("o p n -> p (o n)"))\
                               .then_inc(loaded[k].sem, 16)
                else:
                    for k in range(whole):
                        eng.wait_ge(blocks_done.sem, blocks_done.at(j + k + 1))
                        eng.dma_start(ring[:, k, :], block_of(ahead[j + k])).then_inc(loaded[k].sem, 16)
                j += whole

        def streamed(n, products):
            place[0] += n
            blocks_done.add(n)
            bank_free.add(products)
            for k in range(4):
                loaded[k].add(16 * n // 4)

        def pe_linear(pe, first, n, act, T):
            with pe.Fori(0, n // 4) as i:
                for k in range(4):
                    pe.wait_ge(loaded[k].sem, loaded[k].at(16 * i + (4 * first + 16)))
                    pe.wait_ge(bank_free.sem, bank_free.at(4 * i + (first + k + 1)))
                    for kc in range(KC):
                        last = pe.matmul(ps[:, k, 0:T], ring[:, k, kc * P:(kc + 1) * P], act[:, kc, :],
                                         start=kc == 0, stop=kc == KC - 1)
                    last.then_inc(blocks_done.sem, 1)

        def split_tensor(name, at, *shape):
            return nc.alloc_sbuf_tensor_at(name, [P] + list(shape), F32R, offset=sb_at + 4 * at)

        ring_lo = split_tensor("ring_lo", 9216, 4, 1024)

        def pe_products(pe, out, lhs, rhs, first, last):
            for j, (x, y) in enumerate(((0, 0), (0, 1), (1, 0))):
                done = pe.matmul(out, lhs[x], rhs[y], start=first and j == 0, stop=last and j == 2)
            return done

        def act_round(act, x, hi):
            for kc in range(x.shape[1]):
                act.activation(hi[:, kc, :], x[:, kc, :], ACT.Copy).then_inc(act_a.sem, 1)

        def dve_rest(dve, x, hi, lo, n):
            for kc in range(x.shape[1]):
                dve.wait_ge(act_a.sem, act_a.at(n + kc + 1))
                last = dve.tensor_tensor(lo[:, kc, :], x[:, kc, :], hi[:, kc, :].bitcast(F32), ALU.subtract)
            last.then_inc(dve_a.sem, 1)

        def act_round_block(act, hi2, j, n, k):
            act.wait_ge(loaded[k % 4].sem, loaded[k % 4].at(4 * j + (16 * (k // 4) + 16)))
            act.wait_ge(blocks_done.sem, blocks_done.at(j + (k - 1)))
            act.activation(hi2[:, k % 2, :], ring[:, k % 4, :], ACT.Copy).then_inc(block_hi.sem, 1)

        def dve_rest_block(dve, hi2, n, k):
            dve.wait_ge(block_hi.sem, block_hi.at(n + (k + 1)))
            dve.tensor_tensor(ring_lo[:, k % 4, :], ring[:, k % 4, :], hi2[:, k % 2, :].bitcast(F32), ALU.subtract)\
               .then_inc(block_lo.sem, 1)

        def skewed(eng, n, prepare, finish, begun, more):
            if not begun:
                prepare(0, 0)
            if n > 4:
                with eng.Fori(0, n // 4 - 1) as i:
                    for k in range(4):
                        prepare(4 * i, k + 1)
                        finish(i, k)
            for k in range(4):
                if k < 3 or more:
                    prepare(n - 4, k + 1)
                finish(n // 4 - 1, k)

        def pe_split_linear(pe, hi2, first, n0, n, x, T):
            with pe.Fori(0, n // 4) as i:
                for k in range(4):
                    pe.wait_ge(block_lo.sem, block_lo.at(4 * i + (n0 + k + 1)))
                    pe.wait_ge(bank_free.sem, bank_free.at(4 * i + (first + k + 1)))
                    for kc in range(KC):
                        c = slice(kc * P, (kc + 1) * P)
                        last = pe_products(pe, ps[:, k, 0:T], (hi2[:, k % 2, c], ring_lo[:, k, c]),
                                           (x[0][:, kc, :], x[1][:, kc, :]), kc == 0, kc == KC - 1)
                    last.then_inc(blocks_done.sem, 1)

        with nc.Block() as block:
            @block.sync
            def _(sp):
                for k in range(4):
                    sp.dma_start(ring[:, k, :], ada[0, k]).then_inc(loaded[k].sem, 16)
                sp.dma_start(res_flat["X"], xT).then_inc(consts_in.sem, 16)
                sp.dma_start(res_flat["C"], ctxT).then_inc(consts_in.sem, 16)
                sp.dma_start(mats.rearrange("p a b -> p (a b)"), k_mats).then_inc(consts_in.sem, 16)
                sp.dma_start(cs.rearrange("p a b -> p (a b)"), cT).then_inc(consts_in.sem, 16)
                sp.dma_start(fin_g, final_g).then_inc(consts_in.sem, 16)
                sp.wait_ge(consts_in.sem, consts_in.at(80))

            @block.scalar
            def _(act):
                act.wait_ge(consts_in.sem, consts_in.at(80))
                act.activation(cs_sig, cs, ACT.Sigmoid).then_inc(act_a.sem, 1)

            @block.vector
            def _(dve):
                dve.memset(eps, EPS)
                dve.memset(lt[:, 0, :], 0.0).then_inc(bank_free.sem, 4)
                dve.wait_ge(act_a.sem, act_a.at(1))
                dve.tensor_tensor(cs, cs, cs_sig, ALU.mult)
        consts_in.add(80)
        act_a.add(1)

        def stage_ada(l):
            rows = area(M0, 2, 512)
            with nc.Block() as block:
                @block.sync
                def _(sp):
                    sp.dma_start(pars, par[l]).then_inc(consts_in.sem, 16)
                    load_ahead(sp, 48)

                @block.tensor
                def _(pe):
                    columns = ps[:, 6, 0:96]
                    with pe.Fori(0, 6) as i:
                        for q in range(2):
                            for k in range(4):
                                pe.wait_ge(loaded[k].sem, loaded[k].at(32 * i + (16 * q + 16)))
                                for kc in range(KC):
                                    last = pe.matmul(ps[0:2, 4 + q, k * P:(k + 1) * P], cs[:, kc, :],
                                                     ring[:, k, kc * P:(kc + 1) * P], start=kc == 0, stop=kc == KC - 1)
                                last.then_inc(blocks_done.sem, 1)
                        for q in range(2):
                            pe.wait_ge(dve_b.sem, dve_b.at(2 * i + (q + 1)))
                            for k in range(4):
                                last = pe.matmul(columns[:, ds(16 * i + (8 * q + 2 * k), 2)],
                                                 rows[0:2, q, k * P:(k + 1) * P], ident[0:2, 0:2], start=True, stop=True)
                            last.then_inc(pe_b.sem, 1)

                @block.scalar
                def _(act):
                    act.wait_ge(dve_a.sem, dve_a.at(1))
                    act.activation(lt[:, 1, :], lt[:, 0, :], ACT.Exp).then_inc(act_a.sem, 1)

                @block.vector
                def _(dve):
                    x, y, z, z2, r = (lt[:, n, :] for n in range(5))
                    logit = par_of("logit")
                    dve.wait_ge(consts_in.sem, consts_in.at(16))
                    dve.tensor_scalar(x, logit, -1.0, None, ALU.mult)
                    dve.drain()
                    dve.tensor_tensor(x, x, logit, ALU.min).then_inc(dve_a.sem, 1)
                    dve.wait_ge(act_a.sem, act_a.at(1))
                    dve.tensor_scalar(z2, y, 2.0, None, ALU.add)
                    dve.drain()
                    dve.reciprocal(z, z2)
                    dve.drain()
                    dve.tensor_tensor(z, z, y, ALU.mult)
                    dve.memset(r, 0.0)
                    dve.drain()
                    dve.tensor_tensor(z2, z, z, ALU.mult)
                    dve.drain()
                    for n in range(19, 1, -2):
                        dve.scalar_tensor_tensor(r, r, 1.0 / n, z2, ALU.add, ALU.mult)
                        dve.drain()
                    dve.scalar_tensor_tensor(r, r, 1.0, z, ALU.add, ALU.mult)
                    dve.tensor_scalar(x, logit, 0.0, None, ALU.min)
                    dve.drain()
                    dve.scalar_tensor_tensor(lg, r, -2.0, x, ALU.mult, ALU.add)
                    with dve.Fori(0, 6) as i:
                        for q in range(2):
                            dve.wait_ge(blocks_done.sem, blocks_done.at(8 * i + (4 * q + 4)))
                            dve.tensor_copy(rows[0:2, q, :], ps[0:2, 4 + q, :]).then_inc(dve_b.sem, 1)
                    dve.wait_ge(pe_b.sem, pe_b.at(12))
                    b = par_of("ada_b").unsqueeze(2).broadcast_to([P, 48, 2])
                    dve.tensor_tensor(mod, ps[:, 6, 0:96].rearrange("p (a b) -> p a b", b=2), b, ALU.add)
                    dve.drain()
                    for norm in range(2):
                        g = par_of("n1" if norm == 0 else "n2")
                        for s in range(2):
                            j = 8 * (1 + 3 * norm)
                            dve.scalar_tensor_tensor(amp[:, 2 * norm + s, :], mod[:, j:j + 8, s], 1.0, g,
                                                     ALU.add, ALU.mult)
            consts_in.add(16)
            dve_a.add(1)
            dve_b.add(12)
            pe_b.add(12)
            act_a.add(1)
            streamed(48, 0)

        def stage_filters(l, s):
            L = T_OF[s]
            nt = L // P
            a = M0
            feat, h1, h2, rr = area(a, L), area(a + 512, L), area(a + 1024, L), area(a + 1536, L)
            w1, w2, w3 = area(a + 2048, HID), area(a + 2112, HID), area(a + 2176, 2048)
            a += 4224
            win = area(a, nt, 2, 512)
            a += 4096
            ab = flat(a, nt * 2048)
            ab = ab.rearrange("p (n d o c) -> p n d o c", d=2, o=2, c=512)
            a += 8192
            dft = area(a, nt, 2, L)
            a += 4096
            sq = area(a, 2, 512)
            hb = area(a + 1024, 2, 512)
            inv = area(a + 2048, 2, 512)
            stage = flat(a + 3072, nt * 2048).rearrange("p (o k r c) -> p o k r c", o=2, r=2, c=512)
            k_feat, k_win, k_dft = (k_feat_x, k_win_x, k_dft_x) if s == "X" else (k_feat_c, k_win_c, k_dft_c)
            mlp = par_of("mlp")
            MAGIC, TWO_PI = 12582912.0, 2.0 * math.pi
            HI = float(np.float32(6.28125))
            LO = TWO_PI - HI

            with nc.Block() as block:
                @block.sync
                def _(sp):
                    sp.dma_start(feat[0:EMB, :], k_feat).then_inc(consts_in.sem, 16)
                    sp.dma_start(w1[0:EMB, :], hw1[l]).then_inc(consts_in.sem, 16)
                    sp.dma_start(w2[0:HID, :], hw2[l]).then_inc(consts_in.sem, 16)
                    sp.dma_start(w3[0:HID + 1, :], hw3[l]).then_inc(consts_in.sem, 16)
                    sp.dma_start(win.rearrange("p a b c -> p (a b c)"), k_win).then_inc(consts_in.sem, 16)
                    sp.dma_start(dft.rearrange("p a b c -> p (a b c)"), k_dft[0]).then_inc(consts_in.sem, 16)
                    sp.wait_ge(dve_b.sem, dve_b.at(2 * nt * 2))
                    for o in range(2):
                        sp.dma_start(spec_d[SEG[s], o, :, 0:nt * 1024],
                                     stage[:, o].rearrange("p k r c -> p (k r c)")).then_inc(store_done.sem, 16)
                    sp.wait_ge(store_done.sem, store_done.at(32))

                @block.tensor
                def _(pe):
                    pe.wait_ge(consts_in.sem, consts_in.at(96))
                    pe.matmul(ps[0:HID, 4, 0:L], w1[0:EMB, :], feat[0:EMB, :], start=True, stop=True).then_inc(pe_a.sem, 1)
                    pe.wait_ge(act_a.sem, act_a.at(1))
                    pe.matmul(ps[0:HID, 5, 0:L], w2[0:HID, :], h1[0:HID, :], start=True, stop=True).then_inc(pe_a.sem, 1)
                    pe.wait_ge(act_a.sem, act_a.at(2))
                    for n in range(nt):
                        for q in range(4):
                            j = 4 * n + q
                            if j >= 4:
                                pe.wait_ge(dve_a.sem, dve_a.at(2 + j - 3))
                            pe.matmul(ps[:, q, :], h2[0:HID + 1, n * P:(n + 1) * P], w3[0:HID + 1, q * 512:(q + 1) * 512],
                                      start=True, stop=True).then_inc(pe_a.sem, 1)
                    for o in range(2):
                        for j in range(2 * nt):
                            pe.wait_ge(act_b.sem, act_b.at(2 * nt * o + j + 1))
                            pe.matmul(ps[:, 4 + o, :], ones, sq[:, j % 2, :], start=j == 0,
                                      stop=j == 2 * nt - 1).then_inc(pe_b.sem, 1)
                    j = 0
                    for o in range(2):
                        for kt in range(nt):
                            for r in range(2):
                                if j >= 4:
                                    pe.wait_ge(dve_b.sem, dve_b.at(j - 3))
                                for n in range(nt):
                                    last = pe.matmul(ps[:, j % 4, :], dft[:, n, r, kt * P:(kt + 1) * P],
                                                     ab[:, n, r, o, :], start=n == 0, stop=n == nt - 1)
                                last.then_inc(pe_a.sem, 1)
                                j += 1

                @block.scalar
                def _(act):
                    act.wait_ge(dve_a.sem, dve_a.at(1))
                    act.activation(h1[0:HID, :], h1[0:HID, :], ACT.Sin).then_inc(act_a.sem, 1)
                    act.wait_ge(dve_a.sem, dve_a.at(2))
                    act.activation(h2[0:HID, :], h2[0:HID, :], ACT.Sin).then_inc(act_a.sem, 1)
                    act.wait_ge(dve_c.sem, dve_c.at(1))
                    for o in range(2):
                        for n in range(nt):
                            for d in range(2):
                                j = 2 * nt * o + 2 * n + d
                                if j >= 2:
                                    act.wait_ge(pe_b.sem, pe_b.at(j - 1))
                                act.activation(sq[:, j % 2, :], ab[:, n, d, o, :], ACT.Square).then_inc(act_b.sem, 1)
                    for o in range(2):
                        act.wait_ge(pe_b.sem, pe_b.at(2 * nt * (o + 1)))
                        act.activation(inv[:, o, :], ps[:, 4 + o, :], ACT.Sqrt, scale=0.5, bias=eps).then_inc(root_ready.sem, 1)

                @block.vector
                def _(dve):
                    dve.memset(h2[64:65, :], 1.0)
                    dve.wait_ge(consts_in.sem, consts_in.at(96))
                    for layer, (bank, h, col) in enumerate(((4, h1, 0), (5, h2, 2))):
                        dve.wait_ge(pe_a.sem, pe_a.at(layer + 1))
                        hh, r = h[0:HID, :], rr[0:HID, :]
                        dve.tensor_scalar(hh, ps[0:HID, bank, 0:L], mlp[0:HID, col:col + 1], mlp[0:HID, 1:2], ALU.add, ALU.mult)
                        dve.drain()
                        dve.tensor_scalar(r, hh, 1.0 / TWO_PI, None, ALU.mult)
                        dve.drain()
                        dve.tensor_scalar(r, r, MAGIC, None, ALU.add)
                        dve.drain()
                        dve.tensor_scalar(r, r, -MAGIC, None, ALU.add)
                        dve.drain()
                        dve.scalar_tensor_tensor(hh, r, -HI, hh, ALU.mult, ALU.add)
                        dve.drain()
                        dve.scalar_tensor_tensor(hh, r, -LO, hh, ALU.mult, ALU.add)
                        dve.drain()
                        dve.tensor_scalar(hh, hh, 3.1415925, -3.1415925, ALU.min, ALU.max).then_inc(dve_a.sem, 1)
                    for n in range(nt):
                        for o in range(2):
                            for d in range(2):
                                j = 4 * n + 2 * o + d
                                dve.wait_ge(pe_a.sem, pe_a.at(2 + j + 1))
                                dve.tensor_tensor(hb[:, d, :], ps[:, 2 * o + d, :], win[:, n, d, :], ALU.mult)\
                                   .then_inc(dve_a.sem, 1)
                            dve.drain()
                            dve.tensor_tensor(ab[:, n, 0, o, :], hb[:, 0, :], hb[:, 1, :], ALU.add)
                            last = dve.tensor_tensor(ab[:, n, 1, o, :], hb[:, 0, :], hb[:, 1, :], ALU.subtract)
                            if n < nt - 1 or o == 0:
                                dve.drain()
                    last.then_inc(dve_c.sem, 1)
                    for o in range(2):
                        dve.wait_ge(root_ready.sem, root_ready.at(o + 1))
                        dve.reciprocal(inv[:, o, :], inv[:, o, :])
                    dve.drain()
                    j = 0
                    for o in range(2):
                        for kt in range(nt):
                            for r in range(2):
                                dve.wait_ge(pe_a.sem, pe_a.at(2 + 4 * nt + j + 1))
                                dve.scalar_tensor_tensor(stage[:, o, kt, r, :], ps[:, j % 4, :], 1.0 / L, inv[:, o, :],
                                                         ALU.mult, ALU.mult).then_inc(dve_b.sem, 1)
                                j += 1
            consts_in.add(96)
            store_done.add(32)
            pe_a.add(2 + 4 * nt + 4 * nt)
            pe_b.add(4 * nt)
            act_a.add(2)
            act_b.add(4 * nt)
            dve_a.add(2 + 4 * nt)
            root_ready.add(2)
            dve_b.add(4 * nt)
            dve_c.add(1)

        def stage_norm(s, norm, dst, rs):
            T = T_OF[s]
            with nc.Block() as block:
                @block.scalar
                def _(act):
                    act.activation(dst, res[s], ACT.Square).then_inc(act_a.sem, 1)
                    act.wait_ge(pe_a.sem, pe_a.at(1))
                    act.activation(rs, ps[:, 7, 0:T], ACT.Sqrt, bias=eps).then_inc(root_ready.sem, 1)
                    for kc in range(KC):
                        act.wait_ge(dve_a.sem, dve_a.at(1))
                        if norm < 2:
                            act.activation(dst[:, kc, :], dst[:, kc, :], ACT.Identity,
                                           scale=amp[:, 2 * norm + SEG[s], kc:kc + 1],
                                           bias=mod[:, 24 * norm + kc, SEG[s]:SEG[s] + 1])
                        else:
                            act.activation(dst[:, kc, :], dst[:, kc, :], ACT.Copy, scale=fin_g[:, kc:kc + 1])

                @block.tensor
                def _(pe):
                    pe.wait_ge(act_a.sem, act_a.at(1))
                    for kc in range(KC):
                        last = pe.matmul(ps[:, 7, 0:T], mean_d, dst[:, kc, :], start=kc == 0, stop=kc == KC - 1)
                    last.then_inc(pe_a.sem, 1)

                @block.vector
                def _(dve):
                    dve.wait_ge(root_ready.sem, root_ready.at(1))
                    dve.reciprocal(rs, rs)
                    dve.drain()
                    dve.tensor_tensor(dst, res[s], rs.unsqueeze(1).broadcast_to([P, KC, T]), ALU.mult).then_inc(dve_a.sem, 1)
            act_a.add(1)
            root_ready.add(1)
            pe_a.add(1)
            dve_a.add(1)

        def places(s):
            T = T_OF[s]
            m = {"T": T, "nt": T // P, "M": M0 - 14848}
            b = M0
            m["u"] = area(b, 8, T)
            m["qk"] = area(b + 4096, 8 * T)
            m["merged"] = area(b + 4096, 8, T)
            m["v"] = area(b + 8192, m["nt"], 1024)
            m["g"] = area(b + 12288, 8 * T)
            m["cp"] = area(b + 16384, 4, T + 2 * HALF)
            m["hc"] = area(b + 18552, 4, T)
            m["hp"] = area(b + 20600, 12, T + 2)
            m["hp_flat"] = flat(b + 20600, 6168)
            m["rest"] = r = b + 26768
            m["ret"] = b + 18552
            m["project_split"] = (split_tensor("pu_hi" + s, r, KC, T), split_tensor("pu_lo" + s, r + 4096, KC, T),
                                  split_tensor("p_ring_hi" + s, r + 8192, 2, 1024))
            m["merge_split"] = (split_tensor("mu_hi" + s, b + 8192, KC, T), split_tensor("mu_lo" + s, b + 12288, KC, T),
                                split_tensor("m_ring_hi" + s, b + 16384, 2, 1024))
            m["branch_split"] = (split_tensor("hc_hi" + s, r + 2048, 4, T), split_tensor("hc_lo" + s, b + 20600, 4, T),
                                 split_tensor("z_hi" + s, r + 4096, 4, T), split_tensor("z_lo" + s, b + 22648, 4, T))
            return m

        both = {s: places(s) for s in ("C", "X")}

        def stage_project(s, m, full):
            T, nt = m["T"], m["nt"]
            n_qk = 8 if full else 4
            total = 44 if full else 12
            off = 0 if full else 4
            tmp = area(m["ret"], 4, T)
            qk, v, g = m["qk"], m["v"], m["g"]
            u_hi, u_lo, hi2 = m["project_split"]

            with nc.Block() as block:
                @block.sync
                def _(sp):
                    load_ahead(sp, total)

                @block.tensor
                def _(pe):
                    pe.wait_ge(dve_a.sem, dve_a.at(1))
                    pe_split_linear(pe, hi2, 0, 0, n_qk, (u_hi, u_lo), T)
                    with pe.Fori(0, 2) as i:
                        for k in range(4):
                            pe.wait_ge(loaded[k].sem, loaded[k].at(16 * i + (4 * n_qk + 16)))
                            pe.wait_ge(bank_free.sem, bank_free.at(4 * i + (n_qk + k + 1)))
                            for tt in range(nt):
                                for kc in range(KC):
                                    last = pe.matmul(ps[:, k, tt * P:(tt + 1) * P], m["u"][:, kc, tt * P:(tt + 1) * P],
                                                     ring[:, k, kc * P:(kc + 1) * P], start=kc == 0, stop=kc == KC - 1)
                            last.then_inc(blocks_done.sem, 1)
                    if full:
                        pe_split_linear(pe, hi2, 16, 8, 28, (u_hi, u_lo), T)

                @block.scalar
                def _(act):
                    def rounder(first, n0):
                        return lambda j, k: act_round_block(act, hi2, j + first, n0, k)

                    def sigmoid(first):
                        def finish(i, k):
                            act.wait_ge(blocks_done.sem, blocks_done.at(4 * i + (first + k + 1)))
                            act.wait_ge(bank_free.sem, bank_free.at(4 * i + (first + k + 1)))
                            act.activation(tmp[:, k, :], ps[:, k, 0:T], ACT.Sigmoid).then_inc(gate_ready.sem, 1)
                        return finish

                    def nothing(i, k):
                        pass

                    act_round(act, m["u"], u_hi)
                    skewed(act, n_qk, rounder(0, 0), nothing, False, False)
                    if full:
                        skewed(act, 8, rounder(16, 8), sigmoid(16), False, True)
                        glu = sigmoid(24)
                        skewed(act, 8, rounder(24, 16), lambda i, k: glu(i, k) if k % 2 else None, True, True)
                        skewed(act, 12, rounder(32, 24), nothing, True, False)

                @block.vector
                def _(dve):
                    def rest(n0):
                        return lambda j, k: dve_rest_block(dve, hi2, j + n0, k)

                    def keep_qk(i, k):
                        dve.wait_ge(blocks_done.sem, blocks_done.at(4 * i + (k + 1)))
                        dve.tensor_copy(qk[:, ds(4 * T * i + (off + k) * T, T)], ps[:, k, 0:T]).then_inc(bank_free.sem, 1)

                    def keep_v(i, k):
                        dve.wait_ge(blocks_done.sem, blocks_done.at(4 * i + (n_qk + k + 1)))
                        dve.tensor_copy(v[:, :, ds(4 * P * i + k * P, P)],
                                        ps[:, k, 0:T].rearrange("p (a b) -> p a b", b=P)).then_inc(bank_free.sem, 1)

                    def keep_g(i, k):
                        dve.wait_ge(gate_ready.sem, gate_ready.at(4 * i + (k + 1)))
                        dve.tensor_tensor(g[:, ds(4 * T * i + k * T, T)], ps[:, k, 0:T], tmp[:, k, :], ALU.mult)\
                           .then_inc(bank_free.sem, 1)

                    cp_flat = m["cp"].rearrange("p a b -> p (a b)")
                    cstep = T + 2 * HALF

                    def keep_glu(i, k):
                        if k % 2:
                            dve.wait_ge(gate_ready.sem, gate_ready.at(2 * i + (8 + (k + 1) // 2)))
                            dve.tensor_tensor(cp_flat[:, ds(2 * cstep * i + (k // 2) * cstep + HALF, T)],
                                              ps[:, k - 1, 0:T], tmp[:, k, :], ALU.mult).then_inc(bank_free.sem, 2)

                    hp_flat = m["hp"].rearrange("p a b -> p (a b)")
                    hstep = T + 2

                    def keep_hp(i, k):
                        dve.wait_ge(blocks_done.sem, blocks_done.at(4 * i + (32 + k + 1)))
                        dve.tensor_copy(hp_flat[:, ds(4 * hstep * i + k * hstep + 1, T)], ps[:, k, 0:T]).then_inc(bank_free.sem, 1)

                    dve_rest(dve, m["u"], u_hi, u_lo, 0)
                    skewed(dve, n_qk, rest(0), keep_qk, False, False)
                    with dve.Fori(0, 2) as i:
                        for k in range(4):
                            keep_v(i, k)
                    if full:
                        dve.memset(m["cp"][:, :, 0:HALF], 0.0)
                        dve.memset(m["cp"][:, :, HALF + T:], 0.0)
                        dve.memset(m["hp"][:, :, 0:1], 0.0)
                        dve.memset(m["hp"][:, :, T + 1:], 0.0)
                        skewed(dve, 8, rest(8), keep_g, False, True)
                        skewed(dve, 8, rest(16), keep_glu, True, True)
                        skewed(dve, 12, rest(24), keep_hp, True, False)
                    if s == "C":
                        dve.drain()
                        dve.tensor_copy(ctx_k, qk[:, 4 * T:8 * T].rearrange("p (a b) -> p a b", b=T))
                        dve.tensor_copy(ctx_v, v)
            if full:
                gate_ready.add(12)
            act_a.add(KC)
            dve_a.add(1)
            block_hi.add(total - 8)
            block_lo.add(total - 8)
            streamed(total, total)

        def stage_rope(m):
            a = m["rest"]
            cos, sin, t = area(a, 512), area(a + 512, 512), area(a + 1024, 2, 512)
            qk = m["qk"]
            with nc.Block() as block:
                @block.sync
                def _(sp):
                    sp.dma_start(cos, k_rope[0]).then_inc(consts_in.sem, 16)
                    sp.dma_start(sin, k_rope[1]).then_inc(consts_in.sem, 16)

                @block.tensor
                def _(pe):
                    for n in range(8):
                        if n >= 2:
                            pe.wait_ge(dve_a.sem, dve_a.at(n - 1))
                        pe.matmul(ps[:, n % 2, :], rotate, qk[:, n * 512:(n + 1) * 512], start=True, stop=True)\
                          .then_inc(pe_a.sem, 1)

                @block.vector
                def _(dve):
                    dve.wait_ge(consts_in.sem, consts_in.at(32))
                    for n in range(8):
                        x = qk[:, n * 512:(n + 1) * 512]
                        dve.wait_ge(pe_a.sem, pe_a.at(n + 1))
                        dve.tensor_tensor(t[:, n % 2, :], ps[:, n % 2, :], sin, ALU.mult).then_inc(dve_a.sem, 1)
                        dve.tensor_tensor(x, x, cos, ALU.mult)
                        dve.drain()
                        dve.tensor_tensor(x, x, t[:, n % 2, :], ALU.add)
            consts_in.add(32)
            pe_a.add(8)
            dve_a.add(8)

        def stage_retention(s, m):
            T, nt = m["T"], m["nt"]
            own = [("own", j) for j in range(nt)]
            tiles = own + ([("ctx", j) for j in range(2)] if s == "X" else [])
            NJ = len(tiles)
            J_MEAN, J_VAR, J_END = (0, 3, 4) if s == "X" else (0, 1, 1)
            a = m["rest"]
            dec = area(a, 2, 896)
            a += 1792
            decc = area(a, 2, 640)
            a += 1280
            e = area(a, 2, 896)
            a += 1792
            ec = area(a, 2, 640)
            a += 1280
            table, table_c = area(a, 896), area(a + 896, 640)
            a += 1536
            q_s, k_s = area(a, T), area(a + 512, T)
            a += 1024
            v_s = area(a, 6, 256)
            a += 1536
            prob = area(a, 2, 512)
            o_s, o_c, rs = (area(m["ret"] + 512 * n, T) for n in range(3))
            kc_s = area(m["ret"] + 1536, 256)
            qk, v, g = m["qk"], m["v"], m["g"]
            SC = DK ** -0.5
            gn = par_of("gn")

            def over_heads(eng, step):
                step(0, 0, False)
                with eng.Fori(0, 3) as i:
                    step(2 * i, 1, True)
                    step(2 * i, 2, True)
                step(0, 7, True)

            with nc.Block() as block:
                @block.sync
                def _(sp):
                    sp.dma_start(dec.rearrange("p a b -> p (a b)"), k_dec).then_inc(consts_in.sem, 16)
                    sp.dma_start(decc.rearrange("p a b -> p (a b)"), k_decc).then_inc(consts_in.sem, 16)

                @block.scalar
                def _(act):
                    def exponentials(x, c):
                        for d in range(2):
                            act.activation(e[:, d, :], dec[:, d, :], ACT.Exp, scale=lg[:, ds(x + (8 * d + c), 1)])
                            last = act.activation(ec[:, d, :], decc[:, d, :], ACT.Exp, scale=lg[:, ds(x + (8 * d + c), 1)])
                        last.then_inc(act_a.sem, 1)

                    def end(x, c):
                        act.wait_ge(dve_b.sem, dve_b.at(x + (c + 1)))
                        act.activation(o_s, o_c, ACT.Square).then_inc(squared.sem, 1)
                        act.wait_ge(var_ready.sem, var_ready.at(x + (c + 1)))
                        act.activation(rs, ps[:, 4, 0:T], ACT.Sqrt, bias=eps).then_inc(root_ready.sem, 1)

                    def step(x, c, after):
                        if c < 7:
                            act.wait_ge(tables_used.sem, tables_used.at(x + (c + 1)))
                            exponentials(x, c + 1)
                        if after:
                            end(x, c - 1)
                        act.wait_ge(pe_b.sem, pe_b.at(x + (c + 1)))
                        act.activation(o_s, ps[:, 2 + 3 * (c % 2), 0:T], ACT.Copy).then_inc(act_b.sem, 1)

                    act.wait_ge(consts_in.sem, consts_in.at(32))
                    exponentials(0, 0)
                    over_heads(act, step)
                    end(0, 7)

                @block.tensor
                def _(pe):
                    def mean(x, c):
                        pe.wait_ge(act_b.sem, act_b.at(x + (c + 1)))
                        pe.matmul(ps[:, 3, 0:T], mean_h, o_s, start=True, stop=True).then_inc(mean_ready.sem, 1)

                    def variance(x, c):
                        pe.wait_ge(squared.sem, squared.at(x + (c + 1)))
                        pe.matmul(ps[:, 4, 0:T], mean_h, o_s, start=True, stop=True).then_inc(var_ready.sem, 1)

                    def step(x, c, after):
                        h = c % 2
                        b = h * DK
                        if h == 0:
                            pe.wait_ge(staged.sem, staged.at(x + (c + 1)))

                        def score(j):
                            kind, jt = tiles[j]
                            k = k_s if kind == "own" else kc_s
                            pe.matmul(ps[:, j % 2, 0:T], k[b:b + DK, jt * P:(jt + 1) * P], q_s[b:b + DK, :],
                                      start=True, stop=True).then_inc(pe_a.sem, 1)

                        score(0)
                        for j in range(NJ):
                            if j + 1 < NJ:
                                score(j + 1)
                            if after and j == J_MEAN:
                                mean(x, c - 1)
                            if after and j == J_VAR:
                                variance(x, c - 1)
                            pe.wait_ge(dve_c.sem, dve_c.at(NJ * x + (NJ * c + j + 1)))
                            last = pe.matmul(ps[:, 2 + 3 * h, 0:T], v_s[:, j, h * P:(h + 1) * P], prob[:, j % 2, 0:T],
                                             start=j == 0, stop=j == NJ - 1)
                        last.then_inc(pe_b.sem, 1)

                    over_heads(pe, step)
                    mean(0, 7)
                    variance(0, 7)

                @block.vector
                def _(dve):
                    def stage_pair(x, c):
                        if c > 0:
                            dve.wait_ge(pe_b.sem, pe_b.at(x + c))
                        at = (T // 2) * x + T * (c // 2)
                        at_v = 128 * x + 128 * c
                        dve.tensor_copy(q_s, qk[:, ds(at, T)])
                        dve.tensor_copy(k_s, qk[:, ds(at + 4 * T, T)])
                        last = dve.tensor_copy(v_s[:, 0:nt, :], v[:, :, ds(at_v, 256)])
                        if s == "X":
                            dve.tensor_copy(kc_s, ctx_k.rearrange("p a b -> p (a b)")[:, ds(at_v, 256)])
                            last = dve.tensor_copy(v_s[:, nt:nt + 2, :], ctx_v[:, :, ds(at_v, 256)])
                        last.then_inc(staged.sem, 2)

                    def centre(x, c):
                        dve.wait_ge(mean_ready.sem, mean_ready.at(x + (c + 1)))
                        dve.tensor_tensor(o_c, o_s, ps[:, 3, 0:T], ALU.subtract).then_inc(dve_b.sem, 1)

                    def end(x, c):
                        dve.wait_ge(root_ready.sem, root_ready.at(x + (c + 1)))
                        dve.reciprocal(rs, rs)
                        dve.drain()
                        dve.tensor_tensor(o_c, o_c, rs, ALU.mult)
                        dve.drain()
                        gh = g[:, ds(T * x + T * c, T)]
                        dve.scalar_tensor_tensor(gh, o_c, gn[:, ds(x + c, 1)], gh, ALU.mult, ALU.mult)
                        dve.drain()

                    def step(x, c, after):
                        if c % 2 == 0:
                            stage_pair(x, c)
                        dve.drain()
                        dve.wait_ge(act_a.sem, act_a.at(x + (c + 1)))
                        dve.tensor_tensor(table, e[:, 0, :], e[:, 1, :], ALU.mult)
                        dve.tensor_tensor(table_c, ec[:, 0, :], ec[:, 1, :], ALU.add).then_inc(tables_used.sem, 1)
                        dve.drain()
                        dve.tensor_tensor(table[:, 384:512], table[:, 384:512], ident, ALU.add)
                        dve.drain()
                        for j, (kind, jt) in enumerate(tiles):
                            dve.wait_ge(pe_a.sem, pe_a.at(NJ * x + (NJ * c + j + 1)))
                            if kind == "own":
                                w = table[:, 384 - 128 * jt:384 - 128 * jt + T]
                            else:
                                w = table_c[:, 128 - 128 * jt:128 - 128 * jt + T]
                            dve.scalar_tensor_tensor(prob[:, j % 2, 0:T], ps[:, j % 2, 0:T], SC, w, ALU.mult, ALU.mult)\
                               .then_inc(dve_c.sem, 1)
                            if after and j == J_MEAN:
                                centre(x, c - 1)
                            if after and j == J_END:
                                end(x, c - 1)

                    dve.wait_ge(consts_in.sem, consts_in.at(32))
                    over_heads(dve, step)
                    centre(0, 7)
                    end(0, 7)
            consts_in.add(32)
            for c in (act_a, act_b, root_ready, pe_b, dve_b, mean_ready, var_ready, squared, tables_used, staged):
                c.add(HEADS)
            pe_a.add(8 * NJ)
            dve_c.add(8 * NJ)

        def stage_conformer(m):
            T = m["T"]
            a = m["rest"]
            sq, rs, sg = area(a, 4, T), area(a + 2048, T), area(a + 2560, 4, T)
            tmp = area(a + 6144, 4, T)
            g = m["g"].rearrange("p (a t) -> p a t", t=T)
            mg = m["merged"].rearrange("p a t -> p (a t)")
            hc = m["hc"]
            cp_flat = m["cp"].rearrange("p a b -> p (a b)")
            step = T + 2 * HALF
            w, b = par_of("cdw"), par_of("cdb")
            lng, lnb = par_of("clg"), par_of("clb")

            with nc.Block() as block:
                @block.sync
                def _(sp):
                    load_ahead(sp, 16)

                @block.tensor
                def _(pe):
                    def merge_block(i, k):
                        pe.wait_ge(loaded[k].sem, loaded[k].at(16 * i + 16))
                        pe.wait_ge(bank_free.sem, bank_free.at(4 * i + (k + 1)))
                        x = m["u"] if k % 2 == 0 else g
                        for kc in range(KC):
                            last = pe.matmul(ps[:, k, 0:T], ring[:, k, kc * P:(kc + 1) * P], x[:, kc, :],
                                             start=kc == 0, stop=kc == KC - 1)
                        last.then_inc(blocks_done.sem, 1)

                    def mean_of(bank, x):
                        for c in range(CT4):
                            last = pe.matmul(ps[:, bank, 0:T], mean_c, x[:, c, :], start=c == 0, stop=c == CT4 - 1)
                        last.then_inc(pe_a.sem, 1)

                    with pe.Fori(0, 3) as i:
                        for k in range(4):
                            merge_block(i, k)
                    merge_block(3, 0)
                    merge_block(3, 1)
                    pe.wait_ge(dve_a.sem, dve_a.at(1))
                    mean_of(4, hc)
                    merge_block(3, 2)
                    pe.wait_ge(act_a.sem, act_a.at(1))
                    mean_of(5, sq)
                    merge_block(3, 3)

                @block.scalar
                def _(act):
                    def gate(i, k):
                        act.wait_ge(blocks_done.sem, blocks_done.at(4 * i + (k + 1)))
                        act.wait_ge(bank_free.sem, bank_free.at(4 * i + (k + 1)))
                        act.activation(tmp[:, k, :], ps[:, k, 0:T], ACT.Sigmoid).then_inc(gate_ready.sem, 1)

                    with act.Fori(0, 3) as i:
                        for k in (0, 2):
                            gate(i, k)
                    gate(3, 0)
                    act.wait_ge(dve_a.sem, dve_a.at(2))
                    act.activation(sq, hc, ACT.Square).then_inc(act_a.sem, 1)
                    act.wait_ge(pe_a.sem, pe_a.at(2))
                    act.activation(rs, ps[:, 5, 0:T], ACT.Sqrt, bias=eps).then_inc(root_ready.sem, 1)
                    gate(3, 2)
                    act.wait_ge(dve_a.sem, dve_a.at(3))
                    act.activation(sg, hc, ACT.Sigmoid).then_inc(act_a.sem, 1)

                @block.vector
                def _(dve):
                    def merge(i, k):
                        dve.wait_ge(blocks_done.sem, blocks_done.at(4 * i + (k + 1)))
                        dve.wait_ge(gate_ready.sem, gate_ready.at(2 * i + (k + 1) // 2))
                        dve.tensor_tensor(mg[:, ds(2 * T * i + (k // 2) * T, T)], ps[:, k, 0:T], tmp[:, k - 1, :], ALU.mult)\
                           .then_inc(bank_free.sem, 2)

                    def taps(first, n):
                        for tap in range(n):
                            dve.drain()
                            for c in range(CT4):
                                dve.scalar_tensor_tensor(hc[:, c, :], cp_flat[:, ds(first + (tap + c * step), T)],
                                                         w[:, ds(first + (tap + c * TAPS), 1)], hc[:, c, :], ALU.mult, ALU.add)

                    for c in range(CT4):
                        dve.tensor_scalar(hc[:, c, :], m["cp"][:, c, 0:T], w[:, c * TAPS:c * TAPS + 1], b[:, c:c + 1], ALU.mult, ALU.add)
                    taps(1, 3)
                    with dve.Fori(0, 3) as i:
                        taps(9 * i + 4, 5)
                        merge(i, 1)
                        taps(9 * i + 9, 4)
                        merge(i, 3)
                    dve.drain().then_inc(dve_a.sem, 1)
                    merge(3, 1)
                    dve.wait_ge(pe_a.sem, pe_a.at(1))
                    dve.tensor_tensor(hc, hc, ps[:, 4, 0:T].unsqueeze(1).broadcast_to([P, 4, T]), ALU.subtract).then_inc(dve_a.sem, 1)
                    dve.wait_ge(root_ready.sem, root_ready.at(1))
                    dve.reciprocal(rs, rs)
                    dve.drain()
                    dve.tensor_tensor(hc, hc, rs.unsqueeze(1).broadcast_to([P, 4, T]), ALU.mult)
                    dve.drain()
                    for c in range(CT4):
                        last = dve.tensor_scalar(hc[:, c, :], hc[:, c, :], lng[:, c:c + 1], lnb[:, c:c + 1], ALU.mult, ALU.add)
                    last.then_inc(dve_a.sem, 1)
                    merge(3, 3)
                    dve.wait_ge(act_a.sem, act_a.at(2))
                    dve.tensor_tensor(hc, hc, sg, ALU.mult)
            pe_a.add(2)
            root_ready.add(1)
            act_a.add(2)
            dve_a.add(3)
            gate_ready.add(8)
            streamed(16, 16)

        def stage_hyena(s, m):
            T, nt = m["T"], m["nt"]
            a = m["rest"]
            hs = area(a, 12, T)
            hs_flat = area(a, 12 * T)
            y = area(a + 6144, nt, 2, 512)
            tmp = area(a + 10240, 2, 512)
            spec = m["hp_flat"][:, 0:nt * 1024].rearrange("p (k r c) -> p k r c", r=2, c=512)
            ztm = m["hp_flat"][:, 4096:4096 + nt * 512].rearrange("p (a b) -> p a b", b=512)
            fwd = area(M0 + 12288, nt, 2, T)
            inv = area(M0 + 8192, nt, 2, T)
            k_dft = k_dft_x if s == "X" else k_dft_c
            w, b, bias = par_of("hsw"), par_of("hsb"), par_of("hbias")
            z = hs[:, 0:4, :]
            with nc.Block() as block:
                @block.sync
                def _(sp):
                    sp.dma_start(fwd.rearrange("p a b c -> p (a b c)"), k_dft[0]).then_inc(consts_in.sem, 16)
                    sp.dma_start(inv.rearrange("p a b c -> p (a b c)"), k_dft[1]).then_inc(consts_in.sem, 16)
                    with sp.Fori(0, 2) as o:
                        sp.wait_ge(dve_a.sem, dve_a.at(o + 1))
                        sp.dma_start(spec.rearrange("p k r c -> p (k r c)"),
                                     spec_d[SEG[s], ds(o, 1), :, 0:nt * 1024].rearrange("o p n -> p (o n)")).then_inc(gates_in[0].sem, 16)

                @block.vector
                def _(dve):
                    for c in range(12):
                        dve.tensor_scalar(hs[:, c, :], m["hp"][:, c, 0:T], w[:, c:c + 1], b[:, c:c + 1], ALU.mult, ALU.add)
                    dve.drain()
                    for tap in (1, 2):
                        for c in range(12):
                            last = dve.scalar_tensor_tensor(hs[:, c, :], m["hp"][:, c, tap:tap + T], w[:, tap * 12 + c:tap * 12 + c + 1],
                                                            hs[:, c, :], ALU.mult, ALU.add)
                        if tap == 1:
                            dve.drain()
                    last.then_inc(dve_a.sem, 1)
                    dve.drain().then_inc(dve_c.sem, 1)
                    with dve.Fori(0, 2) as o:
                        for n in range(nt):
                            dve.wait_ge(pe_a.sem, pe_a.at(nt * o + (n + 1)))
                            dve.tensor_copy(ztm[:, n, :], ps[:, n % 4, :]).then_inc(dve_b.sem, 1)
                        dve.wait_ge(gates_in[0].sem, gates_in[0].at(16 * o + 16))
                        for k in range(nt):
                            dve.wait_ge(pe_b.sem, pe_b.at((nt + 4) * o + (k + 1)))
                            zr, zi = ps[:, 4 + 2 * (k % 2), :], ps[:, 5 + 2 * (k % 2), :]
                            dve.tensor_tensor(y[:, k, 0, :], zr, spec[:, k, 0, :], ALU.mult)
                            dve.tensor_tensor(tmp[:, 0, :], zi, spec[:, k, 1, :], ALU.mult)
                            dve.tensor_tensor(y[:, k, 1, :], zr, spec[:, k, 1, :], ALU.mult)
                            dve.tensor_tensor(tmp[:, 1, :], zi, spec[:, k, 0, :], ALU.mult)
                            dve.drain()
                            dve.tensor_tensor(y[:, k, 0, :], y[:, k, 0, :], tmp[:, 0, :], ALU.subtract)
                            last = dve.tensor_tensor(y[:, k, 1, :], y[:, k, 1, :], tmp[:, 1, :], ALU.add)
                            last.then_inc(dve_b.sem, 1)
                            dve.drain()
                        dve.drain().then_inc(dve_a.sem, 1)
                        for c in range(4):
                            dve.wait_ge(pe_b.sem, pe_b.at((nt + 4) * o + (nt + c + 1)))
                            zc = z[:, c, :]
                            dve.scalar_tensor_tensor(zc, zc, bias[:, ds(4 * o + c, 1)], ps[:, c, 0:T], ALU.mult, ALU.add)
                            dve.drain()
                            dve.tensor_tensor(zc, zc, hs_flat[:, ds(4 * T * o + (4 + c) * T, T)], ALU.mult).then_inc(dve_c.sem, 1)

                @block.tensor
                def _(pe):
                    pe.wait_ge(consts_in.sem, consts_in.at(32))
                    with pe.Fori(0, 2) as o:
                        pe.wait_ge(dve_c.sem, dve_c.at(4 * o + 1))
                        for n in range(nt):
                            for c in range(4):
                                last = pe.transpose(ps[:, n % 4, c * P:(c + 1) * P], z[:, c, n * P:(n + 1) * P], ident)
                            last.then_inc(pe_a.sem, 1)
                        pe.wait_ge(dve_b.sem, dve_b.at(2 * nt * o + nt))
                        for k in range(nt):
                            if k >= 2:
                                pe.wait_ge(dve_b.sem, dve_b.at(2 * nt * o + (nt + k - 1)))
                            for r in range(2):
                                for n in range(nt):
                                    last = pe.matmul(ps[:, 4 + 2 * (k % 2) + r, :], fwd[:, n, r, k * P:(k + 1) * P], ztm[:, n, :],
                                                     start=n == 0, stop=n == nt - 1)
                            last.then_inc(pe_b.sem, 1)
                        pe.wait_ge(dve_b.sem, dve_b.at(2 * nt * o + 2 * nt))
                        for c in range(4):
                            for k in range(nt):
                                for r in range(2):
                                    last = pe.matmul(ps[:, c, 0:T], y[:, k, r, c * P:(c + 1) * P], inv[:, k, r, :],
                                                     start=k == r == 0, stop=(k, r) == (nt - 1, 1))
                            last.then_inc(pe_b.sem, 1)
            consts_in.add(32)
            gates_in[0].add(32)
            pe_a.add(2 * nt)
            pe_b.add(2 * (nt + 4))
            dve_a.add(3)
            dve_b.add(4 * nt)
            dve_c.add(9)

        def stage_merge_others(s, m):
            T = m["T"]
            z = area(m["rest"], 12, T)[:, 0:4, :]
            tmp = area(m["rest"] + 6144, 4, T)
            part = area(m["rest"] + 8192, 4, T)
            mg = m["merged"].rearrange("p a t -> p (a t)")
            u_hi, u_lo, hi2 = m["merge_split"]
            hc_hi, hc_lo, z_hi, z_lo = m["branch_split"]
            with nc.Block() as block:
                @block.sync
                def _(sp):
                    load_ahead(sp, 24)

                @block.tensor
                def _(pe):
                    def merge_block(i, n):
                        k, c, kind = n % 4, n // 3, n % 3
                        pe.wait_ge(block_lo.sem, block_lo.at(12 * i + (n + 1)))
                        w = (hi2[:, k % 2, :], ring_lo[:, k, :])

                        def product(bank, x, first):
                            for j in range(len(x[0])):
                                at = slice((first + j) * P, (first + j + 1) * P)
                                last = pe_products(pe, ps[:, bank, 0:T], [v[:, at] for v in w], [v[j] for v in x],
                                                   j == 0, j == len(x[0]) - 1)
                            return last

                        def chunks(hi, lo):
                            return [[v[:, j, :] for j in range(v.shape[1])] for v in (hi, lo)]

                        if kind < 2:
                            pe.wait_ge(bank_free.sem, bank_free.at(12 * i + (3 * c + 1)))
                            last = product(2 * (c % 2) + kind, chunks(u_hi, u_lo), 0)
                        else:
                            if c == 0 and n == 2:
                                pe.wait_ge(dve_a.sem, dve_a.at(3))
                            product(4 + 2 * (c % 2), chunks(hc_hi, hc_lo), 0)
                            last = product(5 + 2 * (c % 2), chunks(z_hi, z_lo), 4)
                        last.then_inc(blocks_done.sem, 1)

                    pe.wait_ge(dve_a.sem, dve_a.at(1))
                    with pe.Fori(0, 2) as i:
                        for n in range(12):
                            merge_block(i, n)

                @block.scalar
                def _(act):
                    def gate(i, n):
                        if n % 3 < 2:
                            c, kind = n // 3, n % 3
                            act.wait_ge(blocks_done.sem, blocks_done.at(12 * i + (n + 1)))
                            act.activation(tmp[:, 2 * (c % 2) + kind, :], ps[:, 2 * (c % 2) + kind, 0:T], ACT.Sigmoid)\
                               .then_inc(gate_ready.sem, 1)

                    act_round(act, m["u"], u_hi)
                    act_round_block(act, hi2, 0, 0, 0)
                    act_round(act, m["hc"], hc_hi)
                    act_round(act, z, z_hi)
                    for i in range(2):
                        for n in range(12):
                            if 12 * i + n < 23:
                                act_round_block(act, hi2, 12 * i, 0, n + 1)
                            gate(i, n)

                @block.vector
                def _(dve):
                    def merge(i, c):
                        dve.wait_ge(gate_ready.sem, gate_ready.at(8 * i + (2 * c + 2)))
                        dve.wait_ge(blocks_done.sem, blocks_done.at(12 * i + (3 * c + 3)))
                        for r in range(2):
                            dve.tensor_tensor(part[:, 2 * (c % 2) + r, :], ps[:, 4 + 2 * (c % 2) + r, 0:T], tmp[:, 2 * (c % 2) + r, :], ALU.mult)
                        dve.drain()
                        dve.tensor_tensor(part[:, 2 * (c % 2), :], part[:, 2 * (c % 2), :], part[:, 2 * (c % 2) + 1, :], ALU.add)
                        dve.drain()
                        x = mg[:, ds(4 * T * i + c * T, T)]
                        dve.tensor_tensor(x, x, part[:, 2 * (c % 2), :], ALU.add).then_inc(bank_free.sem, 3)

                    dve_rest(dve, m["u"], u_hi, u_lo, 0)
                    dve_rest_block(dve, hi2, 0, 0)
                    dve_rest(dve, m["hc"], hc_hi, hc_lo, 8)
                    dve_rest(dve, z, z_hi, z_lo, 12)
                    for i in range(2):
                        for n in range(12):
                            if 12 * i + n < 23:
                                dve_rest_block(dve, hi2, 12 * i, n + 1)
                            if n % 3 == 2:
                                merge(i, n // 3)
            gate_ready.add(16)
            act_a.add(16)
            dve_a.add(3)
            block_hi.add(24)
            block_lo.add(24)
            streamed(24, 24)

        def stage_linear(s, x, evacuate):
            T = T_OF[s]
            with nc.Block() as block:
                @block.sync
                def _(sp):
                    load_ahead(sp, 8)

                @block.tensor
                def _(pe):
                    pe_linear(pe, 0, 8, x, T)

                @block.vector
                def _(dve):
                    with dve.Fori(0, 2) as i:
                        for k in range(4):
                            dve.wait_ge(blocks_done.sem, blocks_done.at(4 * i + (k + 1)))
                            evacuate(dve, i, k).then_inc(bank_free.sem, 1)
            streamed(8, 8)

        mod_flat = mod.rearrange("p a b -> p (a b)")

        def stage_out(s, m):
            T = T_OF[s]

            def add(dve, i, k):
                x = res_flat[s][:, ds(4 * T * i + k * T, T)]
                gate = mod_flat[:, ds(8 * i + (2 * (16 + k) + SEG[s]), 1)]
                return dve.scalar_tensor_tensor(x, ps[:, k, 0:T], gate, x, ALU.mult, ALU.add)

            stage_linear(s, m["merged"], add)

        def mixer(l, s):
            m = both[s]
            stage_norm(s, 0, m["u"], area(m["rest"], T_OF[s]))
            stage_project(s, m, True)
            if s == "X":
                stage_rope(m)
            stage_retention(s, m)
            stage_conformer(m)
            stage_hyena(s, m)
            stage_merge_others(s, m)
            stage_out(s, m)

        TOK = SEQ + CTX
        off = {"X": 0, "C": SEQ}
        ht = area(M0, KC, TOK)
        acc = area(M0 + 6144, KC, TOK)
        acc_flat = area(M0 + 6144, KC * TOK)
        gate_block = area(M0 + 12288, NK, P)
        qp = area(M0 + 28672, 8 * SEQ)
        keys_sb = area(M0 + 32768, 8, 256)
        small = M0 + 34816

        def stage_select(l, s, last_segment):
            T = T_OF[s]
            nt = T // P
            q_s = area(small, 8, P)
            top = area(small + 1024, 8, 2, TOPK)
            top_i = area(small + 1280, 8, 2, TOPK)
            top_u = top_i.bitcast(U32)
            top_f = area(small + 1536, 8, 2, TOPK)
            best = area(small + 1792, 8, TOPK)
            best_u = area(small + 1920, 8, TOPK).bitcast(U32)
            half_u = area(small + 2048, 2, 128).bitcast(U32)
            half_f = area(small + 2304, 2, 8, TOPK)
            picked = area(small + 2560, 3, 128)
            picked_t = area(small + 2944, 3, 128)
            total = area(small + 3328, 8)
            a = M0 + 6144
            sc, sc2, cand = area(a, 8, 2, NK), area(a + 2048, 8, 2, NK), area(a + 4096, 8, 256)
            cand2 = area(M0 + 12288, 8, 256)
            hot_i, hot_j = (area(a + 2048 * n, 2, 8 * NK) for n in range(2))
            hot_i, hot_j = (v.rearrange("p g (t n) -> p g t n", n=NK) for v in (hot_i, hot_j))
            match = area(a, 8, TOPK, TOPK)
            q3 = qp[:, 0:8 * T].rearrange("p (h t) -> p h t", t=T)
            iota16 = iota[:, 0:TOPK].unsqueeze(1).unsqueeze(1).broadcast_to([P, 8, TOPK, TOPK])

            with nc.Block() as block:
                @block.sync
                def _(sp):
                    sp.dma_start(keys_sb.rearrange("p a b -> p (a b)"), keys[l]).then_inc(consts_in.sem, 16)
                    with sp.Fori(0, nt) as tt:
                        sp.wait_ge(act_b.sem, act_b.at(32 * tt + 32))
                        sp.dma_start(gate_d[:, :, ds(P * tt + off[s], P)].rearrange("i p t -> p i t"), gate_block)\
                          .then_inc(store_done.sem, 16)
                    if last_segment:
                        sp.wait_ge(store_done.sem, store_done.at(16 * nt))

                @block.tensor
                def _(pe):
                    pe.wait_ge(consts_in.sem, consts_in.at(16))
                    with pe.Fori(0, nt) as tt:
                        pe.wait_ge(dve_a.sem, dve_a.at(2 * tt + 1))
                        pe.wait_ge(act_b.sem, act_b.at(32 * tt))
                        for h in range(8):
                            last = pe.matmul(ps[:, h // 2, (h % 2) * 256:(h % 2) * 256 + 256], q_s[:, h, :], keys_sb[:, h, :],
                                             start=True, stop=True)
                        last.then_inc(pe_a.sem, 1)
                        pe.wait_ge(dve_a.sem, dve_a.at(2 * tt + 2))
                        for n in range(3):
                            last = pe.transpose(ps[:, 4, n * P:(n + 1) * P], picked[:, n, :], ident)
                        last.then_inc(pe_a.sem, 1)
                        with pe.Fori(0, P // 16) as pair:
                            for g in range(2):
                                pe.wait_ge(dve_b.sem, dve_b.at(32 * tt + 4 * pair + (2 * g + 2)))
                                pe.wait_ge(pool_a.sem, pool_a.at(16 * tt + 2 * pair + (g + 1)))
                                for q in range(8):
                                    if q % 4 == 0:
                                        pe.wait_ge(act_b.sem, act_b.at(32 * tt + 4 * pair + (2 * g + q // 4 - 3)))
                                    pe.matmul(ps[:, 2 * g + q // 4, (q % 4) * P:(q % 4 + 1) * P], hot_j[:, g, q, :],
                                              hot_i[:, g, q, :], start=True, stop=True).then_inc(pe_b.sem, 1)

                @block.scalar
                def _(act):
                    with act.Fori(0, nt) as tt:
                        act.wait_ge(pe_a.sem, pe_a.at(2 * tt + 1))
                        act.activation(sc.rearrange("p a b c -> p (a b c)"), ps[:, 0:4, :].rearrange("p a b -> p (a b)"), ACT.Copy)\
                           .then_inc(act_a.sem, 1)
                        act.wait_ge(dve_c.sem, dve_c.at(tt + 1))
                        act.activation(best, best, ACT.Exp).then_inc(act_a.sem, 1)
                        act.wait_ge(store_done.sem, store_done.at(16 * tt))
                        with act.Fori(0, P // 16) as pair:
                            for q in range(4):
                                act.wait_ge(pe_b.sem, pe_b.at(P * tt + 16 * pair + (4 * q + 4)))
                                act.activation(gate_block[:, :, ds(16 * pair + 4 * q, 4)],
                                               ps[:, q, :].rearrange("p (t i) -> p i t", t=4), ACT.Copy).then_inc(act_b.sem, 1)

                @block.vector
                def _(dve):
                    with dve.Fori(0, nt) as tt:
                        dve.tensor_copy(q_s, q3[:, :, ds(P * tt, P)]).then_inc(dve_a.sem, 1)
                        dve.wait_ge(act_a.sem, act_a.at(2 * tt + 1))
                        dve.memset(total, 0.0)
                        for h in range(8):
                            for r in range(2):
                                dve.max(top[:, h, r, 0:8], sc[:, h, r, :])
                        dve.drain()
                        for h in range(8):
                            for r in range(2):
                                dve.match_replace(sc2[:, h, r, :], top[:, h, r, 0:8], sc[:, h, r, :], LOW)
                                dve.max_index(top_u[:, h, r, 0:8], top[:, h, r, 0:8], sc[:, h, r, :])
                        dve.drain()
                        for h in range(8):
                            for r in range(2):
                                dve.max(top[:, h, r, 8:16], sc2[:, h, r, :])
                        dve.drain()
                        for h in range(8):
                            for r in range(2):
                                dve.max_index(top_u[:, h, r, 8:16], top[:, h, r, 8:16], sc2[:, h, r, :])
                        dve.tensor_tensor(cand.rearrange("p h (a b) -> p h a b", b=TOPK),
                                          top[:, :, 0, :].unsqueeze(3).broadcast_to([P, 8, TOPK, TOPK]),
                                          top[:, :, 1, :].unsqueeze(2).broadcast_to([P, 8, TOPK, TOPK]), ALU.add)
                        dve.drain()
                        dve.wait_ge(store_done.sem, store_done.at(16 * tt))
                        dve.tensor_copy(top_f, top_u)
                        for h in range(8):
                            dve.max(best[:, h, 0:8], cand[:, h, :])
                        dve.drain()
                        for h in range(8):
                            dve.match_replace(cand2[:, h, :], best[:, h, 0:8], cand[:, h, :], LOW)
                            dve.max_index(best_u[:, h, 0:8], best[:, h, 0:8], cand[:, h, :])
                        dve.drain()
                        for h in range(8):
                            dve.max(best[:, h, 8:16], cand2[:, h, :])
                        dve.drain()
                        for h in range(8):
                            dve.max_index(best_u[:, h, 8:16], best[:, h, 8:16], cand2[:, h, :])
                        dve.tensor_copy(total, best[:, :, 0])
                        dve.drain()
                        dve.tensor_tensor(best, best, total.unsqueeze(2).broadcast_to([P, 8, TOPK]), ALU.subtract)\
                           .then_inc(dve_c.sem, 1)
                        flat_u = best_u.rearrange("p h k -> p (h k)")
                        dve.tensor_scalar(half_u[:, 0, :], flat_u, 4, None, ALU.logical_shift_right)
                        dve.tensor_scalar(half_u[:, 1, :], flat_u, 15, None, ALU.bitwise_and)
                        dve.drain()
                        dve.tensor_copy(half_f.rearrange("p r h k -> p r (h k)"), half_u)
                        dve.drain()
                        for r in range(2):
                            dve.tensor_tensor(match, half_f[:, r].unsqueeze(3).broadcast_to([P, 8, TOPK, TOPK]), iota16, ALU.is_equal)
                            dve.drain()
                            dve.tensor_tensor(match, match, top_f[:, :, r, :].unsqueeze(2).broadcast_to([P, 8, TOPK, TOPK]), ALU.mult)
                            dve.drain()
                            dve.tensor_reduce(picked[:, r, :].rearrange("p (h k) -> p h k", k=TOPK), match, AX.X, ALU.add)
                            dve.drain()
                        dve.wait_ge(act_a.sem, act_a.at(2 * tt + 2))
                        dve.tensor_reduce(total, best, AX.X, ALU.add)
                        dve.drain()
                        dve.reciprocal(total, total)
                        dve.drain()
                        dve.tensor_tensor(picked[:, 2, :].rearrange("p (h k) -> p h k", k=TOPK), best,
                                          total.unsqueeze(2).broadcast_to([P, 8, TOPK]), ALU.mult).then_inc(dve_a.sem, 1)
                        dve.wait_ge(pe_a.sem, pe_a.at(2 * tt + 2))
                        dve.tensor_copy(picked_t.rearrange("p a b -> p (a b)"), ps[:, 4, 0:384])
                        dve.drain()
                        pick_i, pick_j, pick_g = (picked_t[:, n, :] for n in range(3))
                        iota8 = iota.unsqueeze(1).broadcast_to([P, 8, NK])
                        with dve.Fori(0, P // 16) as pair:
                            for g in range(2):
                                dve.wait_ge(pe_b.sem, pe_b.at(P * tt + 16 * pair + (8 * g - 8)))
                                for hot, pick in ((hot_i, pick_i), (hot_j, pick_j)):
                                    dve.tensor_tensor(hot[:, g], iota8, pick[:, ds(16 * pair + 8 * g, 8)].unsqueeze(2).broadcast_to([P, 8, NK]),
                                                      ALU.is_equal).then_inc(dve_b.sem, 1)
                        dve.wait_ge(pe_b.sem, pe_b.at(P * tt + P))

                @block.gpsimd
                def _(pool):
                    with pool.Fori(0, nt) as tt:
                        with pool.Fori(0, P // 16) as pair:
                            for g in range(2):
                                pool.wait_ge(dve_b.sem, dve_b.at(32 * tt + 4 * pair + (2 * g + 1)))
                                pool.tensor_tensor(hot_i[:, g], hot_i[:, g],
                                                   picked_t[:, 2, ds(16 * pair + 8 * g, 8)].unsqueeze(2).broadcast_to([P, 8, NK]),
                                                   ALU.mult).then_inc(pool_a.sem, 1)
            consts_in.add(16)
            store_done.add(16 * nt)
            pe_a.add(2 * nt)
            pe_b.add(P * nt)
            act_a.add(2 * nt)
            act_b.add(32 * nt)
            dve_a.add(2 * nt)
            dve_b.add(32 * nt)
            pool_a.add(16 * nt)
            dve_c.add(nt)

        F0 = M0 + 12288
        h_hi = split_tensor("h_hi", F0, KC, TOK)
        h_lo = split_tensor("h_lo", F0 + 6144, KC, TOK)
        ring_hi = split_tensor("ring_hi", F0 + 12288, 4, 1024)
        w_hi = split_tensor("w_hi", F0 + 16384, 2, TOK)
        w_lo = split_tensor("w_lo", F0 + 17920, 2, TOK)

        def stage_split(T):
            with nc.Block() as block:
                @block.scalar
                def _(act):
                    for kc in range(KC):
                        act.activation(h_hi[:, kc, 0:T], ht[:, kc, 0:T], ACT.Copy).then_inc(act_a.sem, 1)

                @block.vector
                def _(dve):
                    for kc in range(KC):
                        dve.wait_ge(act_a.sem, act_a.at(kc + 1))
                        dve.tensor_tensor(h_lo[:, kc, 0:T], ht[:, kc, 0:T], h_hi[:, kc, 0:T].bitcast(F32), ALU.subtract)
            act_a.add(KC)

        def stage_experts(l, segs):
            T = sum(T_OF[s] for s in segs)
            halves = [(0, T // 2), (T // 2, T // 2)]
            a = M0
            gt = area(a, 2, 2, TOK)
            w = area(a + 3072, 2, TOK)
            N = NK // 2
            kinds = order[place[0] + 4:place[0] + 8]

            with nc.Block() as block:
                @block.sync
                def _(sp):
                    def load_u(n, k):
                        for r in range(2):
                            sp.wait_ge(pe_a.sem, pe_a.at(2 * n + (2 * k + r - 1)))
                            sp.dma_start(ring[:, r, :], peer_u[l, ds(2 * n + (2 * k + r), 1)].rearrange("o p n -> p (o n)"))\
                              .then_inc(loaded[r].sem, 16)

                    def load_v(n, k):
                        sp.wait_ge(pe_b.sem, pe_b.at(8 * n + 8 * k))
                        for r in range(2):
                            sp.dma_start(ring[:, 2 + r, :], peer_v[l, ds(2 * n + (2 * k + r), 1)].rearrange("o p n -> p (o n)"))\
                              .then_inc(loaded[2 + r].sem, 16)

                    def load_gates(n, k):
                        sp.dma_start(gt[:, k % 2, :, 0:T], gate_d[ds(2 * n + 2 * k, 2), :, 0:T].rearrange("i p t -> p i t"))\
                          .then_inc(gates_in[k % 2].sem, 16)

                    load_gates(0, 0)
                    load_gates(0, 1)
                    load_u(0, 1)
                    with sp.Fori(0, (N - 2) // 2) as pair:
                        n = 2 * pair
                        for k in range(2):
                            load_u(n, k + 2)
                            sp.wait_ge(w_ready.sem, w_ready.at(2 * n + (2 * k + 2)))
                            load_gates(n, k + 2)
                            load_v(n, k + 1)
                    load_v(N - 2, 1)
                    for k, entry in enumerate(kinds):
                        if k < 2:
                            sp.wait_ge(pe_a.sem, pe_a.at(2 * N - 1 + k))
                        else:
                            sp.wait_ge(pe_b.sem, pe_b.at(8 * N))
                        sp.dma_start(ring[:, k, :], block_of(entry)).then_inc(loaded[k].sem, 16)

                @block.tensor
                def _(pe):
                    def a_of(n, k):
                        for r in range(2):
                            pe.wait_ge(u_split.sem, u_split.at(2 * n + (2 * k + r + 1)))
                            pe.wait_ge(act_a.sem, act_a.at(2 * n + (2 * k + r - 1)))
                            for p, (t0, t) in enumerate(halves):
                                for kc in range(KC):
                                    c = slice(kc * P, (kc + 1) * P)
                                    last = pe_products(pe, ps[:, 2 * r + p, 0:t], (ring_hi[:, r, c], ring_lo[:, r, c]),
                                                    (h_hi[:, kc, t0:t0 + t], h_lo[:, kc, t0:t0 + t]), kc == 0, kc == KC - 1)
                            last.then_inc(pe_a.sem, 1)

                    def o_of(n, k):
                        pe.wait_ge(v_split.sem, v_split.at(2 * n + (2 * k + 2)))
                        pe.wait_ge(w_ready.sem, w_ready.at(2 * n + (2 * k + 2)))
                        for dc in range(KC):
                            pe.wait_ge(dve_c.sem, dve_c.at(8 * n + (8 * k + dc - 1)))
                            c = slice(dc * P, (dc + 1) * P)
                            for p, (t0, t) in enumerate(halves):
                                for r in range(2):
                                    last = pe_products(pe, ps[:, 4 + 2 * (dc % 2) + p, 0:t], (ring_hi[:, 2 + r, c], ring_lo[:, 2 + r, c]),
                                                    (w_hi[:, r, t0:t0 + t], w_lo[:, r, t0:t0 + t]), r == 0, r == 1)
                            last.then_inc(pe_b.sem, 1)

                    a_of(0, 0)
                    with pe.Fori(0, (N - 2) // 2) as pair:
                        n = 2 * pair
                        for k in range(2):
                            a_of(n, k + 1)
                            o_of(n, k)
                    a_of(N - 2, 1)
                    o_of(N - 2, 0)
                    o_of(N - 2, 1)

                @block.scalar
                def _(act):
                    def round_block(n, k, first):
                        for r in range(2):
                            slot = first + r
                            act.wait_ge(loaded[slot].sem, loaded[slot].at(16 * n + (16 * k + 16)))
                            act.activation(ring_hi[:, slot, :], ring[:, slot, :], ACT.Copy)\
                               .then_inc((u_hi if first == 0 else v_hi).sem, 1)

                    def gelu(n, k):
                        for r in range(2):
                            act.wait_ge(pe_a.sem, pe_a.at(2 * n + (2 * k + r + 1)))
                            act.wait_ge(w_ready.sem, w_ready.at(2 * n + 2 * k))
                            act.activation(w[:, r, 0:T].rearrange("p (a b) -> p a b", a=2), ps[:, 2 * r:2 * r + 2, 0:T // 2],
                                           ACT.Gelu_apprx_tanh).then_inc(act_a.sem, 1)

                    round_block(0, 0, 0)
                    round_block(0, 0, 2)
                    gelu(0, 0)
                    round_block(0, 1, 0)
                    with act.Fori(0, (N - 2) // 2) as pair:
                        n = 2 * pair
                        for k in range(2):
                            gelu(n, k + 1)
                            round_block(n, k + 2, 0)
                            round_block(n, k + 1, 2)
                    gelu(N - 2, 1)
                    round_block(N - 2, 1, 2)

                @block.vector
                def _(dve):
                    def rest_of_block(n, k, first, r):
                        hi, done = (u_hi, u_split) if first == 0 else (v_hi, v_split)
                        slot = first + r
                        dve.wait_ge(hi.sem, hi.at(2 * n + (2 * k + r + 1)))
                        dve.tensor_tensor(ring_lo[:, slot, :], ring[:, slot, :], ring_hi[:, slot, :].bitcast(F32), ALU.subtract)\
                           .then_inc(done.sem, 1)

                    def weigh(n, k):
                        dve.wait_ge(gates_in[k % 2].sem, gates_in[k % 2].at(8 * n + (16 * (k // 2) + 16)))
                        for r in range(2):
                            dve.wait_ge(act_a.sem, act_a.at(2 * n + (2 * k + r + 1)))
                            dve.tensor_tensor(w[:, r, 0:T], w[:, r, 0:T], gt[:, k % 2, r, 0:T], ALU.mult)
                        dve.drain()
                        for r in range(2):
                            dve.tensor_copy(w_hi[:, r, 0:T], w[:, r, 0:T])
                        dve.drain()
                        for r in range(2):
                            dve.tensor_tensor(w_lo[:, r, 0:T], w[:, r, 0:T], w_hi[:, r, 0:T].bitcast(F32), ALU.subtract)\
                               .then_inc(w_ready.sem, 1)

                    def gather(n, k, dc):
                        dve.wait_ge(pe_b.sem, pe_b.at(8 * n + (8 * k + dc + 1)))
                        x = acc[:, dc, 0:T].rearrange("p (a b) -> p a b", a=2)
                        b = 4 + 2 * (dc % 2)
                        dve.tensor_tensor(x, x, ps[:, b:b + 2, 0:T // 2], ALU.add).then_inc(dve_c.sem, 1)

                    def step(n, k, more):
                        for dc in range(KC):
                            gather(n, k, dc)
                            if more and dc in (4, 5):
                                rest_of_block(n, k + 2, 0, dc - 4)
                        weigh(n, k + 1)
                        for r in range(2):
                            rest_of_block(n, k + 1, 2, r)

                    dve.memset(acc_flat, 0.0)
                    for first in (0, 2):
                        for r in range(2):
                            rest_of_block(0, 0, first, r)
                    weigh(0, 0)
                    for r in range(2):
                        rest_of_block(0, 1, 0, r)
                    with dve.Fori(0, (N - 2) // 2) as pair:
                        n = 2 * pair
                        for k in range(2):
                            step(n, k, True)
                    step(N - 2, 0, False)
                    for dc in range(KC):
                        gather(N - 2, 1, dc)
                    dve.drain()
                    for s in segs:
                        for kc in range(KC):
                            x = res[s][:, kc, :]
                            dve.scalar_tensor_tensor(x, acc[:, kc, off[s]:off[s] + T_OF[s]], mod[:, 40 + kc, SEG[s]:SEG[s] + 1], x,
                                                     ALU.mult, ALU.add)
            for k in range(4):
                loaded[k].add(16 * N)
            place[0] += 4
            for c in (pe_a, act_a, u_hi, v_hi, u_split, v_split, w_ready):
                c.add(2 * N)
            pe_b.add(8 * N)
            dve_c.add(8 * N)
            for g in gates_in:
                g.add(16 * N // 2)

        def peer(l, segs):
            for s in segs:
                x = ht[:, :, off[s]:off[s] + T_OF[s]]
                stage_norm(s, 1, x, area(small, T_OF[s]))

                def keep(dve, i, k, T=T_OF[s]):
                    return dve.tensor_copy(qp[:, ds(4 * T * i + k * T, T)], ps[:, k, 0:T])

                stage_linear(s, x, keep)
                stage_select(l, s, s == segs[-1])
            T = sum(T_OF[s] for s in segs)
            stage_split(T)
            stage_experts(l, segs)

        for l in range(DEPTH):
            last = l == DEPTH - 1
            stage_ada(l)
            if not last:
                stage_filters(l, "C")
            stage_filters(l, "X")
            if not last:
                mixer(l, "C")
            else:
                m = both["C"]
                stage_norm("C", 0, m["u"], area(m["rest"], CTX))
                stage_project("C", m, False)
            mixer(l, "X")
            peer(l, ("X",) if last else ("X", "C"))
        m = both["X"]
        stage_norm("X", 2, m["u"], area(m["rest"], SEQ))
        with nc.Block() as block:
            @block.sync
            def _(sp):
                sp.dma_start(out, m["u"].rearrange("p a b -> p (a b)")).then_inc(store_done.sem, 16)
                sp.wait_ge(store_done.sem, store_done.at(16))


def _chunks(a):
    a = np.asarray(a)
    return np.swapaxes(a.reshape(a.shape[:-1] + (a.shape[-1] // P, P)), -1, -2)


def _tokens(a):
    return np.ascontiguousarray(np.asarray(a).T.reshape(KC, P, -1).transpose(1, 0, 2).reshape(P, -1))


def _blocks(w):
    w = np.asarray(w)
    n = w.shape[1] // P
    return w.reshape(KC, P, n, P).transpose(2, 1, 0, 3).reshape(n, P, KC * P)


def _constants():
    f = np.float32
    mats = np.zeros((P, 7, P), f)
    mats[:, 0] = np.eye(P)
    for m in range(0, P, 2):
        mats[m + 1, 1, m] = -1.0
        mats[m, 1, m + 1] = 1.0
    mats[:, 2], mats[:, 3], mats[:, 4], mats[:, 5] = 1.0 / D, 1.0 / CW, 1.0 / DV, 1.0
    mats[:, 6] = np.arange(P)
    t = np.arange(SEQ)
    nf = DK // 4
    inv = (10000.0 ** (-np.arange(nf, dtype=f) / f(nf))).astype(f)
    ang = np.concatenate([(t // GRID_W).astype(f)[:, None] * inv, (t % GRID_W).astype(f)[:, None] * inv], 1)
    pair = (np.arange(P) % DK) // 2
    rope = np.stack([np.cos(ang)[:, pair].T, np.sin(ang)[:, pair].T]).astype(f)
    lag = np.arange(896)[None, :] - 384 - np.arange(P)[:, None]
    dec = np.stack([np.maximum(lag, 0), np.maximum(-lag, 0)], 1).astype(f)
    c, p = np.arange(640)[None, :], np.arange(P)[:, None]
    decc = np.stack([c - p + CTX - 128, SEQ + 128 - c + p], 1).astype(f)
    got = dict(mats=mats.reshape(P, -1), rope=rope, dec=dec.reshape(P, -1), decc=decc.reshape(P, -1))
    for s, L in (("x", SEQ), ("c", CTX)):
        tt = np.arange(L, dtype=f)
        tn = tt / f(L - 1)
        w = f(2.0 * math.pi) * tt / f(L)
        bands = np.linspace(1e-4, 15, 16, dtype=f)
        feat = np.concatenate([tn[:, None], np.cos(w[:, None] * bands), -np.sin(w[:, None] * bands)], 1)
        got["feat_" + s] = np.ascontiguousarray(feat.T.astype(f))
        deltas = np.abs(np.linspace(math.log(1e-2) / 1.5, math.log(1e-2) / 0.3, HW, dtype=f))
        win = np.exp(-tn[:, None] * deltas[None, :]).astype(f)
        win2 = np.stack([win, win], 1)
        win2[0, 1] = 0.0
        got["win_" + s] = np.ascontiguousarray(win2.reshape(L // P, P, 2 * HW).transpose(1, 0, 2).reshape(P, -1))
        ph = np.pi * np.outer(np.arange(L), np.arange(L) + 0.5) / L
        tab = np.stack([np.cos(ph), -np.sin(ph)], 1)
        back = np.stack([np.cos(ph).T, -np.sin(ph).T], 1)
        got["dft_" + s] = np.stack([x.reshape(L // P, P, 2 * L).transpose(1, 0, 2).reshape(P, -1) for x in (tab, back)]).astype(f)
    return got


def kernel(x, c, ctx, c_ctx, ada_w, ada_b, norm1_g, norm2_g, w_in, ret_decay_logit, ret_gn_g, w_br_ret, conf_dw_w,
           conf_dw_b, conf_ln_g, conf_ln_b, w_br_conf, hy_short_w, hy_short_b, hy_w1, hy_b1, hy_freq, hy_w2, hy_b2,
           hy_w3, hy_b3, hy_bias, w_br_hy, w_out, peer_wq, peer_keys, peer_u, peer_v, final_g):
    import concourse.bacc as bacc
    from concourse.bass_utils import run_bass_kernel_spmd

    A = np.asarray
    x, c, ctx, c_ctx, w_in = A(x), A(c), A(ctx), A(c_ctx), A(w_in)
    mix, par, keys = [], [], []
    for l in range(DEPTH):
        wb = _blocks(w_in[l])
        ret, conf_hy = _blocks(w_br_ret[l]), _blocks(np.concatenate([A(w_br_conf[l]), A(w_br_hy[l])], 0))
        conf, hy, gate = wb[24:32], wb[32:44], wb[44:68]
        order = list(wb[0:24])
        for n in range(4):
            order += [conf[n], conf[4 + n]]
        order += list(hy)
        for n in range(8):
            order += [gate[n], ret[n]]
        for n in range(8):
            order += [gate[8 + n], gate[16 + n], conf_hy[n]]
        order += list(_blocks(w_out[l])) + list(_blocks(peer_wq[l]))
        mix.append(np.stack(order))
        mlp = np.zeros((P, 3), np.float32)
        mlp[0:HID, 0], mlp[0:HID, 1], mlp[0:HID, 2] = A(hy_b1[l]), A(hy_freq[l]), A(hy_b2[l])
        logit = np.broadcast_to(A(ret_decay_logit[l]).reshape(1, 16), (P, 16))
        cdw = _chunks(conf_dw_w[l]).transpose(1, 2, 0).reshape(P, -1)
        hsw = _chunks(hy_short_w[l]).transpose(1, 0, 2).reshape(P, -1)
        hb = _chunks(hy_bias[l]).transpose(1, 0, 2).reshape(P, -1)
        parts = dict(n1=_chunks(norm1_g[l]), n2=_chunks(norm2_g[l]), ada_b=_chunks(ada_b[l]), gn=_chunks(ret_gn_g[l]),
                     cdw=cdw, cdb=_chunks(conf_dw_b[l]), clg=_chunks(conf_ln_g[l]), clb=_chunks(conf_ln_b[l]),
                     hsw=hsw, hsb=_chunks(hy_short_b[l]), hbias=hb, logit=logit, mlp=mlp)
        par.append(np.concatenate([parts[n] for n in _cols], 1))
        kk = np.zeros((P, 8, 256), np.float32)
        for r in range(2):
            kk[64 * r:64 * r + 64, :, 128 * r:128 * r + 128] = A(peer_keys[l])[:, r].transpose(2, 0, 1)
        keys.append(kk.reshape(P, -1))
    k = _constants()
    arrays = {
        "xT": _tokens(x[0]), "cT": np.stack([_chunks(c[0]), _chunks(c_ctx)], 2).reshape(P, 16),
        "ctxT": _tokens(ctx[0]), "final_g": _chunks(final_g),
        "ada": np.stack([_blocks(ada_w[l]) for l in range(DEPTH)]), "mix": np.stack(mix),
        "peer_u": A(peer_u).reshape(DEPTH, NK, P, KC, P).transpose(0, 1, 4, 3, 2).reshape(DEPTH, NK, P, D),
        "peer_v": A(peer_v).reshape(DEPTH, NK, P, D), "par": np.stack(par),
        "hw1": A(hy_w1), "hw2": A(hy_w2),
        "hw3": np.concatenate([A(hy_w3), A(hy_b3)[:, None, :]], 1), "keys": np.stack(keys),
        "k_mats": k["mats"], "k_rope": k["rope"], "k_dec": k["dec"], "k_decc": k["decc"],
        "k_feat_x": k["feat_x"], "k_feat_c": k["feat_c"], "k_win_x": k["win_x"], "k_win_c": k["win_c"],
        "k_dft_x": k["dft_x"], "k_dft_c": k["dft_c"],
    }
    arrays = {n: np.ascontiguousarray(a) for n, a in arrays.items()}
    nc = bacc.Bacc("TRN2", target_bir_lowering=False, num_devices=1)
    args = {n: nc.dram_tensor("in_" + n, a.shape, mybir.dt.from_np(a.dtype), kind="ExternalInput").ap()
            for n, a in arrays.items()}
    out = nc.dram_tensor("out_0", (P, KC * SEQ), F32, kind="ExternalOutput").ap()
    build(nc, out=out, **args)
    r = run_bass_kernel_spmd(nc, [{"in_" + n: a for n, a in arrays.items()}], core_ids=[0])
    got = np.asarray(r.results[0]["out_0"])
    return np.ascontiguousarray(got.reshape(P, KC, SEQ).transpose(2, 1, 0).reshape(1, SEQ, D))
```

```python
import math
from contextlib import ExitStack

import numpy as np
import concourse.bass as bass
from concourse import mybir

F32 = mybir.dt.float32
U32 = mybir.dt.uint32
F32R = mybir.dt.float32r
ALU = mybir.AluOpType
ACT = mybir.ActivationFunctionType
AX = mybir.AxisListType
ds = bass.ds

P = 128
D = 1024
KC = D // P
SEQ, CTX = 512, 256
DEPTH = 2
EPS = 1e-6
GRID_W = 64
HEADS, DK, DV = 8, 64, 128
TAPS, HALF = 31, 15
CW = HW = 512
CT4 = CW // P
EMB, HID = 33, 64
NK = 128
TOPK = 16
NMIX, NQ = 92, 8
LOW = -3.0e38

_cols = dict(n1=8, n2=8, ada_b=48, gn=8, cdw=CT4 * TAPS, cdb=4, clg=4, clb=4, hsw=36, hsb=12,
             hbias=8, logit=16, mlp=3)
PCOL, _at = {}, 0
for _n, _c in _cols.items():
    PCOL[_n] = (_at, _c)
    _at += _c
NPAR = _at


class Count:

    def __init__(self, nc, stack, name):
        self.sem = stack.enter_context(nc.semaphore(name))
        self.base = 0

    def at(self, n):
        return n + self.base

    def add(self, n):
        self.base += n


def build(nc, xT, cT, ctxT, final_g, ada, mix, peer_u, peer_v, par, hw1, hw2, hw3, keys, k_mats, k_rope,
          k_dec, k_decc, k_feat_x, k_feat_c, k_win_x, k_win_c, k_dft_x, k_dft_c, out):
    stack = ExitStack()
    with stack:
        M0 = -(-(14208 + NPAR + 265) // 8) * 8
        kept = stack.enter_context(nc.sbuf_tensor("kept", [P, M0], F32))
        sb_at = nc.sbuf_base - 4 * M0
        arena = stack.enter_context(nc.sbuf_tensor("arena", [P, 53200 - M0], F32))
        ps = stack.enter_context(nc.psum_tensor("psum", [P, 8, 512], F32))
        spec_d = nc.dram_tensor("spec_scratch", (2, 2, P, 4 * 2 * 512), F32, kind="Internal").ap()
        gate_d = nc.dram_tensor("gate_scratch", (NK, P, SEQ + CTX), F32, kind="Internal").ap()

        def new(name):
            return Count(nc, stack, name)

        loaded = [new(f"weights_loaded_{k}") for k in range(4)]
        blocks_done = new("blocks_done")
        bank_free = new("bank_free")
        gate_ready = new("gate_ready")
        consts_in = new("consts_loaded")
        store_done = new("store_done")
        pe_a, pe_b = new("pe_first"), new("pe_second")
        dve_a, dve_b, dve_c = new("dve_first"), new("dve_second"), new("dve_third")
        act_a, act_b = new("act_first"), new("act_second")
        pool_a = new("pool_first")
        exponents, staged = new("exponents_ready"), new("pair_staged")
        mean_ready, var_ready, squared = new("mean_ready"), new("variance_ready"), new("squares_ready")
        u_hi, v_hi = new("u_rounded"), new("v_rounded")
        u_split, v_split = new("u_split"), new("v_split")
        block_hi, block_lo = new("block_rounded"), new("block_split")
        w_ready = new("w_split")
        rows_out, columns_done = new("ada_rows_out"), new("ada_columns_done")
        root_ready = new("root_ready")
        gates_in = [new("gates_loaded_0"), new("gates_loaded_1")]

        def flat(at, n):
            return kept[:, at:at + n] if at < M0 else arena[:, at - M0:at - M0 + n]

        def area(at, *shape):
            n = int(np.prod(shape))
            v = flat(at, n)
            if len(shape) == 2:
                v = v.rearrange("p (a b) -> p a b", b=shape[1])
            if len(shape) == 3:
                v = v.rearrange("p (a b c) -> p a b c", b=shape[1], c=shape[2])
            return v

        T_OF = {"X": SEQ, "C": CTX}
        res_flat = {"X": area(0, 4096), "C": area(4096, 2048)}
        res = {s: v.rearrange("p (a t) -> p a t", t=T_OF[s]) for s, v in res_flat.items()}
        ctx_k = area(6144, 4, 256)
        ctx_v = area(7168, 2, 1024)
        ring = area(9216, 4, 1024)
        mats = area(13312, 7, 128)
        ident, rotate, mean_d, mean_c, mean_h, ones, iota = (mats[:, n, :] for n in range(7))
        pars = area(14208, NPAR)
        o = 14208 + NPAR
        mod = area(o, 48, 2)
        amp = area(o + 96, 4, 8)
        cs = area(o + 128, 8, 2)
        cs_sig = area(o + 144, 8, 2)
        lg = area(o + 160, 16)
        lt = area(o + 176, 5, 16)
        fin_g = area(o + 256, 8)
        eps = area(o + 264, 1)
        SEG = {"X": 0, "C": 1}

        def par_of(name):
            a, n = PCOL[name]
            return pars[:, a:a + n]

        runs = []
        runs.append(("ada", 0, 0, 48))
        for l in range(DEPTH):
            runs.append(("mix", l, 0, NMIX) if l == 0 else ("mix", l, 4, 12))
            runs.append(("mix", l, 0, NMIX))
            runs.append(("mix", l, NMIX, NQ))
            if l < DEPTH - 1:
                runs += [("ada", l + 1, 0, 48), ("mix", l, NMIX, NQ)]
            runs.append(("peer", l, 0, 4))
        tables = {"ada": ada, "mix": mix}
        order = [(r, l, n + k) for r, l, n, m in runs for k in range(m)]
        place = [0]

        def block_of(entry):
            kind, l, n = entry
            if kind == "peer":
                return (peer_u, peer_v)[n // 2][l, n % 2]
            return tables[kind][l, n]

        def load_ahead(eng, n):
            at, j = place[0] + 4, 0
            ahead = order[at:at + n]
            while j < len(ahead):
                kind, l, first = ahead[j]
                whole = 4
                while ahead[j + whole - 1:j + whole + 1][1:] == [(kind, l, first + whole)]:
                    whole += 4
                if kind != "peer" and whole > 4:
                    with eng.Fori(0, whole // 4) as i:
                        for k in range(4):
                            eng.wait_ge(blocks_done.sem, blocks_done.at(4 * i + (j + k + 1)))
                            eng.dma_start(ring[:, k, :], tables[kind][l, ds(4 * i + (first + k), 1)].rearrange("o p n -> p (o n)"))\
                               .then_inc(loaded[k].sem, 16)
                else:
                    for k in range(whole):
                        eng.wait_ge(blocks_done.sem, blocks_done.at(j + k + 1))
                        eng.dma_start(ring[:, k, :], block_of(ahead[j + k])).then_inc(loaded[k].sem, 16)
                j += whole

        def streamed(n, products):
            place[0] += n
            blocks_done.add(n)
            bank_free.add(products)
            for k in range(4):
                loaded[k].add(16 * n // 4)

        def pe_linear(pe, first, n, act, T):
            with pe.Fori(0, n // 4) as i:
                for k in range(4):
                    pe.wait_ge(loaded[k].sem, loaded[k].at(16 * i + (4 * first + 16)))
                    pe.wait_ge(bank_free.sem, bank_free.at(4 * i + (first + k + 1)))
                    for kc in range(KC):
                        last = pe.matmul(ps[:, k, 0:T], ring[:, k, kc * P:(kc + 1) * P], act[:, kc, :],
                                         start=kc == 0, stop=kc == KC - 1)
                    last.then_inc(blocks_done.sem, 1)

        def split_tensor(name, at, *shape):
            return nc.alloc_sbuf_tensor_at(name, [P] + list(shape), F32R, offset=sb_at + 4 * at)

        ring_lo = split_tensor("ring_lo", 9216, 4, 1024)

        def pe_products(pe, out, lhs, rhs, first, last):
            for j, (x, y) in enumerate(((0, 0), (0, 1), (1, 0))):
                done = pe.matmul(out, lhs[x], rhs[y], start=first and j == 0, stop=last and j == 2)
            return done

        def act_round(act, x, hi):
            for kc in range(x.shape[1]):
                act.activation(hi[:, kc, :], x[:, kc, :], ACT.Copy).then_inc(act_a.sem, 1)

        def dve_rest(dve, x, hi, lo, n):
            for kc in range(x.shape[1]):
                dve.wait_ge(act_a.sem, act_a.at(n + kc + 1))
                last = dve.tensor_tensor(lo[:, kc, :], x[:, kc, :], hi[:, kc, :].bitcast(F32), ALU.subtract)
            last.then_inc(dve_a.sem, 1)

        def act_round_block(act, hi2, j, n, k):
            act.wait_ge(loaded[k % 4].sem, loaded[k % 4].at(4 * j + (16 * (k // 4) + 16)))
            act.wait_ge(blocks_done.sem, blocks_done.at(j + (k - 1)))
            act.activation(hi2[:, k % 2, :], ring[:, k % 4, :], ACT.Copy).then_inc(block_hi.sem, 1)

        def dve_rest_block(dve, hi2, n, k):
            dve.wait_ge(block_hi.sem, block_hi.at(n + (k + 1)))
            dve.tensor_tensor(ring_lo[:, k % 4, :], ring[:, k % 4, :], hi2[:, k % 2, :].bitcast(F32), ALU.subtract)\
               .then_inc(block_lo.sem, 1)

        def skewed(eng, n, prepare, finish, begun, more):
            if not begun:
                prepare(0, 0)
            if n > 4:
                with eng.Fori(0, n // 4 - 1) as i:
                    for k in range(4):
                        prepare(4 * i, k + 1)
                        finish(i, k)
            for k in range(4):
                if k < 3 or more:
                    prepare(n - 4, k + 1)
                finish(n // 4 - 1, k)

        def pe_split_linear(pe, hi2, first, n0, n, x, T):
            with pe.Fori(0, n // 4) as i:
                for k in range(4):
                    pe.wait_ge(block_lo.sem, block_lo.at(4 * i + (n0 + k + 1)))
                    pe.wait_ge(bank_free.sem, bank_free.at(4 * i + (first + k + 1)))
                    for kc in range(KC):
                        c = slice(kc * P, (kc + 1) * P)
                        last = pe_products(pe, ps[:, k, 0:T], (hi2[:, k % 2, c], ring_lo[:, k, c]),
                                           (x[0][:, kc, :], x[1][:, kc, :]), kc == 0, kc == KC - 1)
                    last.then_inc(blocks_done.sem, 1)

        with nc.Block() as block:
            @block.sync
            def _(sp):
                for k in range(4):
                    sp.dma_start(ring[:, k, :], ada[0, k]).then_inc(loaded[k].sem, 16)
                sp.dma_start(res_flat["X"], xT).then_inc(consts_in.sem, 16)
                sp.dma_start(res_flat["C"], ctxT).then_inc(consts_in.sem, 16)
                sp.dma_start(mats.rearrange("p a b -> p (a b)"), k_mats).then_inc(consts_in.sem, 16)
                sp.dma_start(cs.rearrange("p a b -> p (a b)"), cT).then_inc(consts_in.sem, 16)
                sp.dma_start(fin_g, final_g).then_inc(consts_in.sem, 16)
                sp.wait_ge(consts_in.sem, consts_in.at(80))

            @block.scalar
            def _(act):
                act.wait_ge(consts_in.sem, consts_in.at(80))
                act.activation(cs_sig, cs, ACT.Sigmoid).then_inc(act_a.sem, 1)

            @block.vector
            def _(dve):
                dve.memset(eps, EPS)
                dve.memset(lt[:, 0, :], 0.0).then_inc(bank_free.sem, 4)
                dve.wait_ge(act_a.sem, act_a.at(1))
                dve.tensor_tensor(cs, cs, cs_sig, ALU.mult)
        consts_in.add(80)
        act_a.add(1)

        ada_rows = area(6144, 3, 512)
        ada_raw = area(7680, 96)
        ada_columns = ps[:, 4, 384:480]

        def pe_ada(pe, x):
            for c in range(3):
                for k in range(4):
                    pe.wait_ge(loaded[k].sem, loaded[k].at(16 * x + (16 * c + 16)))
                    for kc in range(KC):
                        last = pe.matmul(ps[0:2, 5 + c, k * P:(k + 1) * P], cs[:, kc, :],
                                         ring[:, k, kc * P:(kc + 1) * P], start=kc == 0, stop=kc == KC - 1)
                    last.then_inc(blocks_done.sem, 1)
            for c in range(3):
                pe.wait_ge(rows_out.sem, rows_out.at(x + (c + 1)))
                for k in range(4):
                    last = pe.matmul(ada_columns[:, ds(8 * x + (8 * c + 2 * k), 2)],
                                     ada_rows[0:2, c, k * P:(k + 1) * P], ident[0:2, 0:2], start=True, stop=True)
                last.then_inc(columns_done.sem, 1)

        def act_ada(act, x):
            for c in range(3):
                act.wait_ge(blocks_done.sem, blocks_done.at(4 * x + (4 * c + 4)))
                act.activation(ada_rows[0:2, c, :], ps[0:2, 5 + c, :], ACT.Copy).then_inc(rows_out.sem, 1)

        def dve_ada(dve):
            dve.wait_ge(columns_done.sem, columns_done.at(12))
            dve.tensor_copy(ada_raw, ada_columns)

        def counted_ada():
            rows_out.add(12)
            columns_done.add(12)
            streamed(48, 0)

        def stage_ada():
            with nc.Block() as block:
                @block.sync
                def _(sp):
                    load_ahead(sp, 48)

                @block.tensor
                def _(pe):
                    with pe.Fori(0, 4) as i:
                        pe_ada(pe, 3 * i)

                @block.scalar
                def _(act):
                    with act.Fori(0, 4) as i:
                        act_ada(act, 3 * i)

                @block.vector
                def _(dve):
                    dve_ada(dve)
            counted_ada()

        def stage_modulation(l):
            with nc.Block() as block:
                @block.sync
                def _(sp):
                    sp.dma_start(pars, par[l]).then_inc(consts_in.sem, 16)

                @block.scalar
                def _(act):
                    act.wait_ge(dve_a.sem, dve_a.at(1))
                    act.activation(lt[:, 1, :], lt[:, 0, :], ACT.Exp).then_inc(act_a.sem, 1)

                @block.vector
                def _(dve):
                    x, y, z, z2, r = (lt[:, n, :] for n in range(5))
                    logit = par_of("logit")
                    dve.wait_ge(consts_in.sem, consts_in.at(16))
                    dve.tensor_scalar(x, logit, -1.0, None, ALU.mult)
                    dve.drain()
                    dve.tensor_tensor(x, x, logit, ALU.min).then_inc(dve_a.sem, 1)
                    dve.wait_ge(act_a.sem, act_a.at(1))
                    dve.tensor_scalar(z2, y, 2.0, None, ALU.add)
                    dve.drain()
                    dve.reciprocal(z, z2)
                    dve.drain()
                    dve.tensor_tensor(z, z, y, ALU.mult)
                    dve.memset(r, 0.0)
                    dve.drain()
                    dve.tensor_tensor(z2, z, z, ALU.mult)
                    dve.drain()
                    for n in range(19, 1, -2):
                        dve.scalar_tensor_tensor(r, r, 1.0 / n, z2, ALU.add, ALU.mult)
                        dve.drain()
                    dve.scalar_tensor_tensor(r, r, 1.0, z, ALU.add, ALU.mult)
                    dve.tensor_scalar(x, logit, 0.0, None, ALU.min)
                    dve.drain()
                    dve.scalar_tensor_tensor(lg, r, -2.0, x, ALU.mult, ALU.add)
                    b = par_of("ada_b").unsqueeze(2).broadcast_to([P, 48, 2])
                    dve.tensor_tensor(mod, ada_raw.rearrange("p (a b) -> p a b", b=2), b, ALU.add)
                    dve.drain()
                    for norm in range(2):
                        g = par_of("n1" if norm == 0 else "n2")
                        for s in range(2):
                            j = 8 * (1 + 3 * norm)
                            dve.scalar_tensor_tensor(amp[:, 2 * norm + s, :], mod[:, j:j + 8, s], 1.0, g,
                                                     ALU.add, ALU.mult)
            consts_in.add(16)
            dve_a.add(1)
            act_a.add(1)

        def stage_filters(l, s):
            L = T_OF[s]
            nt = L // P
            a = M0
            feat, h1, h2, rr = area(a, L), area(a + 512, L), area(a + 1024, L), area(a + 1536, L)
            w1, w2, w3 = area(a + 2048, HID), area(a + 2112, HID), area(a + 2176, 2048)
            a += 4224
            win = area(a, nt, 2, 512)
            a += 4096
            ab = flat(a, nt * 2048)
            ab = ab.rearrange("p (n d o c) -> p n d o c", d=2, o=2, c=512)
            a += 8192
            dft = area(a, nt, 2, L)
            a += 4096
            sq = area(a + 11264, 4, 512)
            hb = area(a + 1024, 2, 512)
            inv = area(a + 2048, 2, 512)
            stage = flat(a + 3072, nt * 2048).rearrange("p (o k r c) -> p o k r c", o=2, r=2, c=512)
            k_feat, k_win, k_dft = (k_feat_x, k_win_x, k_dft_x) if s == "X" else (k_feat_c, k_win_c, k_dft_c)
            mlp = par_of("mlp")
            MAGIC, TWO_PI = 12582912.0, 2.0 * math.pi
            HI = float(np.float32(6.28125))
            LO = TWO_PI - HI

            with nc.Block() as block:
                @block.sync
                def _(sp):
                    sp.dma_start(feat[0:EMB, :], k_feat).then_inc(consts_in.sem, 16)
                    sp.dma_start(w1[0:EMB, :], hw1[l]).then_inc(consts_in.sem, 16)
                    sp.dma_start(w2[0:HID, :], hw2[l]).then_inc(consts_in.sem, 16)
                    sp.dma_start(w3[0:HID + 1, :], hw3[l]).then_inc(consts_in.sem, 16)
                    sp.dma_start(win.rearrange("p a b c -> p (a b c)"), k_win).then_inc(gates_in[0].sem, 16)
                    sp.dma_start(dft.rearrange("p a b c -> p (a b c)"), k_dft[0]).then_inc(gates_in[1].sem, 16)
                    sp.wait_ge(dve_b.sem, dve_b.at(2 * nt * 2))
                    for o in range(2):
                        sp.dma_start(spec_d[SEG[s], o, :, 0:nt * 1024],
                                     stage[:, o].rearrange("p k r c -> p (k r c)")).then_inc(store_done.sem, 16)
                    sp.wait_ge(store_done.sem, store_done.at(32))

                @block.tensor
                def _(pe):
                    def energies(n):
                        for o in range(2):
                            for d in range(2):
                                pe.wait_ge(act_b.sem, act_b.at(4 * n + 2 * o + d + 1))
                                pe.matmul(ps[:, 4 + o, :], ones, sq[:, 2 * o + d, :], start=n == d == 0,
                                          stop=(n, d) == (nt - 1, 1)).then_inc(pe_b.sem, 1)

                    pe.wait_ge(consts_in.sem, consts_in.at(64))
                    pe.matmul(ps[0:HID, 4, 0:L], w1[0:EMB, :], feat[0:EMB, :], start=True, stop=True).then_inc(pe_a.sem, 1)
                    pe.wait_ge(act_a.sem, act_a.at(1))
                    pe.matmul(ps[0:HID, 5, 0:L], w2[0:HID, :], h1[0:HID, :], start=True, stop=True).then_inc(pe_a.sem, 1)
                    pe.wait_ge(act_a.sem, act_a.at(2))
                    for n in range(nt):
                        for q in range(4):
                            j = 4 * n + q
                            if j >= 4:
                                pe.wait_ge(dve_a.sem, dve_a.at(2 + j - 3))
                            pe.matmul(ps[:, q, :], h2[0:HID + 1, n * P:(n + 1) * P], w3[0:HID + 1, q * 512:(q + 1) * 512],
                                      start=True, stop=True).then_inc(pe_a.sem, 1)
                        if n > 0:
                            energies(n - 1)
                    energies(nt - 1)
                    pe.wait_ge(gates_in[1].sem, gates_in[1].at(16))
                    j = 0
                    for o in range(2):
                        for kt in range(nt):
                            for r in range(2):
                                if j >= 4:
                                    pe.wait_ge(dve_b.sem, dve_b.at(j - 3))
                                for n in range(nt):
                                    last = pe.matmul(ps[:, j % 4, :], dft[:, n, r, kt * P:(kt + 1) * P],
                                                     ab[:, n, r, o, :], start=n == 0, stop=n == nt - 1)
                                last.then_inc(pe_a.sem, 1)
                                j += 1

                @block.scalar
                def _(act):
                    act.wait_ge(dve_a.sem, dve_a.at(1))
                    act.activation(h1[0:HID, :], h1[0:HID, :], ACT.Sin).then_inc(act_a.sem, 1)
                    act.wait_ge(dve_a.sem, dve_a.at(2))
                    act.activation(h2[0:HID, :], h2[0:HID, :], ACT.Sin).then_inc(act_a.sem, 1)
                    for n in range(nt):
                        act.wait_ge(dve_c.sem, dve_c.at(n + 1))
                        for o in range(2):
                            for d in range(2):
                                if n > 0:
                                    act.wait_ge(pe_b.sem, pe_b.at(4 * n + 2 * o + d - 3))
                                act.activation(sq[:, 2 * o + d, :], ab[:, n, d, o, :], ACT.Square).then_inc(act_b.sem, 1)
                    for o in range(2):
                        act.wait_ge(pe_b.sem, pe_b.at(4 * nt - 2 + 2 * o))
                        act.activation(inv[:, o, :], ps[:, 4 + o, :], ACT.Sqrt, scale=0.5, bias=eps).then_inc(root_ready.sem, 1)

                @block.vector
                def _(dve):
                    dve.memset(h2[64:65, :], 1.0)
                    dve.wait_ge(consts_in.sem, consts_in.at(64))
                    for layer, (bank, h, col) in enumerate(((4, h1, 0), (5, h2, 2))):
                        dve.wait_ge(pe_a.sem, pe_a.at(layer + 1))
                        hh, r = h[0:HID, :], rr[0:HID, :]
                        dve.tensor_scalar(hh, ps[0:HID, bank, 0:L], mlp[0:HID, col:col + 1], mlp[0:HID, 1:2], ALU.add, ALU.mult)
                        dve.drain()
                        dve.tensor_scalar(r, hh, 1.0 / TWO_PI, None, ALU.mult)
                        dve.drain()
                        dve.tensor_scalar(r, r, MAGIC, None, ALU.add)
                        dve.drain()
                        dve.tensor_scalar(r, r, -MAGIC, None, ALU.add)
                        dve.drain()
                        dve.scalar_tensor_tensor(hh, r, -HI, hh, ALU.mult, ALU.add)
                        dve.drain()
                        dve.scalar_tensor_tensor(hh, r, -LO, hh, ALU.mult, ALU.add)
                        dve.drain()
                        dve.tensor_scalar(hh, hh, 3.1415925, -3.1415925, ALU.min, ALU.max).then_inc(dve_a.sem, 1)
                    dve.wait_ge(gates_in[0].sem, gates_in[0].at(16))
                    for n in range(nt):
                        for o in range(2):
                            for d in range(2):
                                j = 4 * n + 2 * o + d
                                dve.wait_ge(pe_a.sem, pe_a.at(2 + j + 1))
                                dve.tensor_tensor(hb[:, d, :], ps[:, 2 * o + d, :], win[:, n, d, :], ALU.mult)\
                                   .then_inc(dve_a.sem, 1)
                            dve.drain()
                            dve.tensor_tensor(ab[:, n, 0, o, :], hb[:, 0, :], hb[:, 1, :], ALU.add)
                            last = dve.tensor_tensor(ab[:, n, 1, o, :], hb[:, 0, :], hb[:, 1, :], ALU.subtract)
                            if o == 1:
                                last.then_inc(dve_c.sem, 1)
                            if n < nt - 1 or o == 0:
                                dve.drain()
                    for o in range(2):
                        dve.wait_ge(root_ready.sem, root_ready.at(o + 1))
                        dve.reciprocal(inv[:, o, :], inv[:, o, :])
                    dve.drain()
                    j = 0
                    for o in range(2):
                        for kt in range(nt):
                            for r in range(2):
                                dve.wait_ge(pe_a.sem, pe_a.at(2 + 4 * nt + j + 1))
                                dve.scalar_tensor_tensor(stage[:, o, kt, r, :], ps[:, j % 4, :], 1.0 / L, inv[:, o, :],
                                                         ALU.mult, ALU.mult).then_inc(dve_b.sem, 1)
                                j += 1
            consts_in.add(64)
            for c in gates_in:
                c.add(16)
            store_done.add(32)
            pe_a.add(2 + 4 * nt + 4 * nt)
            pe_b.add(4 * nt)
            act_a.add(2)
            act_b.add(4 * nt)
            dve_a.add(2 + 4 * nt)
            root_ready.add(2)
            dve_b.add(4 * nt)
            dve_c.add(nt)

        def stage_norm(s, norm, dst, rs):
            T = T_OF[s]
            with nc.Block() as block:
                @block.scalar
                def _(act):
                    for kc in range(KC):
                        act.activation(dst[:, kc, :], res[s][:, kc, :], ACT.Square).then_inc(act_a.sem, 1)
                    act.wait_ge(pe_a.sem, pe_a.at(1))
                    act.activation(rs, ps[:, 7, 0:T], ACT.Sqrt, bias=eps).then_inc(root_ready.sem, 1)
                    for kc in range(KC):
                        act.wait_ge(dve_a.sem, dve_a.at(kc + 1))
                        if norm < 2:
                            act.activation(dst[:, kc, :], dst[:, kc, :], ACT.Identity,
                                           scale=amp[:, 2 * norm + SEG[s], kc:kc + 1],
                                           bias=mod[:, 24 * norm + kc, SEG[s]:SEG[s] + 1])
                        else:
                            act.activation(dst[:, kc, :], dst[:, kc, :], ACT.Copy, scale=fin_g[:, kc:kc + 1])

                @block.tensor
                def _(pe):
                    for kc in range(KC):
                        pe.wait_ge(act_a.sem, act_a.at(kc + 1))
                        last = pe.matmul(ps[:, 7, 0:T], mean_d, dst[:, kc, :], start=kc == 0, stop=kc == KC - 1)
                    last.then_inc(pe_a.sem, 1)

                @block.vector
                def _(dve):
                    dve.wait_ge(root_ready.sem, root_ready.at(1))
                    dve.reciprocal(rs, rs)
                    dve.drain()
                    for kc in range(KC):
                        dve.tensor_tensor(dst[:, kc, :], res[s][:, kc, :], rs, ALU.mult).then_inc(dve_a.sem, 1)
            act_a.add(KC)
            root_ready.add(1)
            pe_a.add(1)
            dve_a.add(KC)

        def places(s):
            T = T_OF[s]
            m = {"T": T, "nt": T // P}
            b = M0
            m["u"] = area(b, 8, T)
            m["qk"] = area(b + 4096, 8 * T)
            m["merged"] = area(b + 4096, 8, T)
            m["v"] = area(b + 8192, m["nt"], 1024)
            m["fwd"] = area(b + 8192, m["nt"], 2, T)
            m["k_dft"] = k_dft_x if s == "X" else k_dft_c
            m["g"] = area(b + 12288, 8 * T)
            m["cp"] = area(b + 16384, 4, T + 2 * HALF)
            m["hc"] = area(b + 18552, 4, T)
            m["hp"] = area(b + 20600, 12, T + 2)
            m["hp_flat"] = flat(b + 20600, 6168)
            m["rest"] = r = b + 26768
            m["ret"] = b + 18552
            m["project_split"] = (split_tensor("pu_hi" + s, r, KC, T), split_tensor("pu_lo" + s, r + 4096, KC, T),
                                  split_tensor("p_ring_hi" + s, r + 8192, 2, 1024))
            m["merge_split"] = (split_tensor("mu_hi" + s, b + 8192, KC, T), split_tensor("mu_lo" + s, b + 12288, KC, T),
                                split_tensor("m_ring_hi" + s, b + 16384, 2, 1024))
            m["branch_split"] = (split_tensor("hc_hi" + s, r + 2048, 4, T), split_tensor("hc_lo" + s, b + 20600, 4, T),
                                 split_tensor("z_hi" + s, r + 4096, 4, T), split_tensor("z_lo" + s, b + 22648, 4, T))
            return m

        both = {s: places(s) for s in ("C", "X")}

        def stage_project(s, m, full):
            T, nt = m["T"], m["nt"]
            n_qk = 8 if full else 4
            total = 44 if full else 12
            off = 0 if full else 4
            tmp = area(m["ret"], 4, T)
            qk, v, g = m["qk"], m["v"], m["g"]
            u_hi, u_lo, hi2 = m["project_split"]

            with nc.Block() as block:
                @block.sync
                def _(sp):
                    load_ahead(sp, total)

                @block.tensor
                def _(pe):
                    pe.wait_ge(dve_a.sem, dve_a.at(1))
                    pe_split_linear(pe, hi2, 0, 0, n_qk, (u_hi, u_lo), T)
                    with pe.Fori(0, 2) as i:
                        for k in range(4):
                            pe.wait_ge(loaded[k].sem, loaded[k].at(16 * i + (4 * n_qk + 16)))
                            pe.wait_ge(bank_free.sem, bank_free.at(4 * i + (n_qk + k + 1)))
                            for tt in range(nt):
                                for kc in range(KC):
                                    last = pe.matmul(ps[:, k, tt * P:(tt + 1) * P], m["u"][:, kc, tt * P:(tt + 1) * P],
                                                     ring[:, k, kc * P:(kc + 1) * P], start=kc == 0, stop=kc == KC - 1)
                            last.then_inc(blocks_done.sem, 1)
                    if full:
                        pe_split_linear(pe, hi2, 16, 8, 28, (u_hi, u_lo), T)

                @block.scalar
                def _(act):
                    def rounder(first, n0):
                        return lambda j, k: act_round_block(act, hi2, j + first, n0, k)

                    def sigmoid(first):
                        def finish(i, k):
                            act.wait_ge(blocks_done.sem, blocks_done.at(4 * i + (first + k + 1)))
                            act.wait_ge(bank_free.sem, bank_free.at(4 * i + (first + k + 1)))
                            act.activation(tmp[:, k, :], ps[:, k, 0:T], ACT.Sigmoid).then_inc(gate_ready.sem, 1)
                        return finish

                    def nothing(i, k):
                        pass

                    act_round(act, m["u"], u_hi)
                    skewed(act, n_qk, rounder(0, 0), nothing, False, False)
                    if full:
                        skewed(act, 8, rounder(16, 8), sigmoid(16), False, True)
                        glu = sigmoid(24)
                        skewed(act, 8, rounder(24, 16), lambda i, k: glu(i, k) if k % 2 else None, True, True)
                        skewed(act, 12, rounder(32, 24), nothing, True, False)

                @block.vector
                def _(dve):
                    def rest(n0):
                        return lambda j, k: dve_rest_block(dve, hi2, j + n0, k)

                    def keep_qk(i, k):
                        dve.wait_ge(blocks_done.sem, blocks_done.at(4 * i + (k + 1)))
                        dve.tensor_copy(qk[:, ds(4 * T * i + (off + k) * T, T)], ps[:, k, 0:T]).then_inc(bank_free.sem, 1)

                    def keep_v(i, k):
                        dve.wait_ge(blocks_done.sem, blocks_done.at(4 * i + (n_qk + k + 1)))
                        dve.tensor_copy(v[:, :, ds(4 * P * i + k * P, P)],
                                        ps[:, k, 0:T].rearrange("p (a b) -> p a b", b=P)).then_inc(bank_free.sem, 1)

                    def keep_g(i, k):
                        dve.wait_ge(gate_ready.sem, gate_ready.at(4 * i + (k + 1)))
                        dve.tensor_tensor(g[:, ds(4 * T * i + k * T, T)], ps[:, k, 0:T], tmp[:, k, :], ALU.mult)\
                           .then_inc(bank_free.sem, 1)

                    cp_flat = m["cp"].rearrange("p a b -> p (a b)")
                    cstep = T + 2 * HALF

                    def keep_glu(i, k):
                        if k % 2:
                            dve.wait_ge(gate_ready.sem, gate_ready.at(2 * i + (8 + (k + 1) // 2)))
                            dve.tensor_tensor(cp_flat[:, ds(2 * cstep * i + (k // 2) * cstep + HALF, T)],
                                              ps[:, k - 1, 0:T], tmp[:, k, :], ALU.mult).then_inc(bank_free.sem, 2)

                    hp_flat = m["hp"].rearrange("p a b -> p (a b)")
                    hstep = T + 2

                    def keep_hp(i, k):
                        dve.wait_ge(blocks_done.sem, blocks_done.at(4 * i + (32 + k + 1)))
                        dve.tensor_copy(hp_flat[:, ds(4 * hstep * i + k * hstep + 1, T)], ps[:, k, 0:T]).then_inc(bank_free.sem, 1)

                    dve_rest(dve, m["u"], u_hi, u_lo, 0)
                    skewed(dve, n_qk, rest(0), keep_qk, False, False)
                    with dve.Fori(0, 2) as i:
                        for k in range(4):
                            keep_v(i, k)
                    if full:
                        dve.memset(m["cp"][:, :, 0:HALF], 0.0)
                        dve.memset(m["cp"][:, :, HALF + T:], 0.0)
                        dve.memset(m["hp"][:, :, 0:1], 0.0)
                        dve.memset(m["hp"][:, :, T + 1:], 0.0)
                        skewed(dve, 8, rest(8), keep_g, False, True)
                        skewed(dve, 8, rest(16), keep_glu, True, True)
                        skewed(dve, 12, rest(24), keep_hp, True, False)
                    if s == "C":
                        dve.drain()
                        dve.tensor_copy(ctx_k, qk[:, 4 * T:8 * T].rearrange("p (a b) -> p a b", b=T))
                        dve.tensor_copy(ctx_v, v)
            if full:
                gate_ready.add(12)
            act_a.add(KC)
            dve_a.add(1)
            block_hi.add(total - 8)
            block_lo.add(total - 8)
            streamed(total, total)

        def stage_rope(m):
            a = m["rest"]
            cos, sin, t = area(a, 512), area(a + 512, 512), area(a + 1024, 2, 512)
            qk = m["qk"]
            with nc.Block() as block:
                @block.sync
                def _(sp):
                    sp.dma_start(cos, k_rope[0]).then_inc(consts_in.sem, 16)
                    sp.dma_start(sin, k_rope[1]).then_inc(consts_in.sem, 16)

                @block.tensor
                def _(pe):
                    for n in range(8):
                        if n >= 2:
                            pe.wait_ge(dve_a.sem, dve_a.at(n - 1))
                        pe.matmul(ps[:, n % 2, :], rotate, qk[:, n * 512:(n + 1) * 512], start=True, stop=True)\
                          .then_inc(pe_a.sem, 1)

                @block.vector
                def _(dve):
                    dve.wait_ge(consts_in.sem, consts_in.at(32))
                    for n in range(8):
                        x = qk[:, n * 512:(n + 1) * 512]
                        dve.wait_ge(pe_a.sem, pe_a.at(n + 1))
                        dve.tensor_tensor(t[:, n % 2, :], ps[:, n % 2, :], sin, ALU.mult).then_inc(dve_a.sem, 1)
                        dve.tensor_tensor(x, x, cos, ALU.mult)
                        dve.drain()
                        dve.tensor_tensor(x, x, t[:, n % 2, :], ALU.add)
            consts_in.add(32)
            pe_a.add(8)
            dve_a.add(8)

        def stage_retention(s, m):
            T, nt = m["T"], m["nt"]
            own = [("own", j) for j in range(nt)]
            tiles = own + ([("ctx", j) for j in range(2)] if s == "X" else [])
            NJ = len(tiles)
            BANKS = (0, 1, 6)
            a = m["rest"]
            lag = area(a, 896)
            a += 896
            decc = area(a, 2, 640)
            a += 1280
            back = area(a, 896)
            a += 896
            ec = area(a, 2, 640)
            a += 1280
            tables = [area(a + 1536 * n, 896) for n in range(2)]
            tables_c = [area(a + 1536 * n + 896, 640) for n in range(2)]
            a += 3072
            q_s, k_s = area(a, T), area(a + 512, T)
            a += 1024
            v_s = area(a, 6, 256)
            a += 1536
            prob = area(a, 3, 512)
            o_s, o_c, rs = (area(m["ret"] + 512 * n, T) for n in range(3))
            kc_s = area(m["ret"] + 1536, 256)
            qk, v, g = m["qk"], m["v"], m["g"]
            SC = DK ** -0.5
            gn = par_of("gn")

            def over_heads(eng, step):
                step(0, 0)
                step(0, 1)
                with eng.Fori(0, 2) as i:
                    step(2 * i, 2)
                    step(2 * i, 3)
                step(0, 6)
                step(0, 7)

            with nc.Block() as block:
                @block.sync
                def _(sp):
                    sp.dma_start(lag, k_dec).then_inc(consts_in.sem, 16)
                    sp.dma_start(decc.rearrange("p a b -> p (a b)"), k_decc).then_inc(consts_in.sem, 16)

                @block.scalar
                def _(act):
                    def exponentials(x, c):
                        act.wait_ge(exponents.sem, exponents.at(x + (c + 1)))
                        table = tables[c % 2]
                        last = act.activation(table, table, ACT.Exp)
                        if s == "X":
                            for d in range(2):
                                last = act.activation(ec[:, d, :], decc[:, d, :], ACT.Exp, scale=lg[:, ds(x + (8 * d + c), 1)])
                        last.then_inc(act_a.sem, 1)

                    def square(x, c):
                        act.wait_ge(dve_b.sem, dve_b.at(x + (c + 1)))
                        act.activation(o_s, o_c, ACT.Square).then_inc(squared.sem, 1)

                    def root(x, c):
                        act.wait_ge(var_ready.sem, var_ready.at(x + (c + 1)))
                        act.activation(rs, ps[:, 4, 0:T], ACT.Sqrt, bias=eps).then_inc(root_ready.sem, 1)

                    def step(x, c):
                        if c > 0:
                            square(x, c - 1)
                        if c < 7:
                            exponentials(x, c + 1)
                        if c > 0:
                            root(x, c - 1)
                        act.wait_ge(pe_b.sem, pe_b.at(x + (c + 1)))
                        act.activation(o_s, ps[:, 2 + 3 * (c % 2), 0:T], ACT.Copy).then_inc(act_b.sem, 1)

                    act.wait_ge(consts_in.sem, consts_in.at(32))
                    exponentials(0, 0)
                    over_heads(act, step)
                    square(0, 7)
                    root(0, 7)

                @block.tensor
                def _(pe):
                    def mean(x, c):
                        pe.wait_ge(act_b.sem, act_b.at(x + (c + 1)))
                        pe.matmul(ps[:, 3, 0:T], mean_h, o_s, start=True, stop=True).then_inc(mean_ready.sem, 1)

                    def variance(x, c):
                        pe.wait_ge(squared.sem, squared.at(x + (c + 1)))
                        pe.matmul(ps[:, 4, 0:T], mean_h, o_s, start=True, stop=True).then_inc(var_ready.sem, 1)

                    def step(x, c):
                        h = c % 2
                        b = h * DK
                        if h == 0:
                            pe.wait_ge(staged.sem, staged.at(x + (c + 1)))

                        def score(j):
                            kind, jt = tiles[j]
                            k = k_s if kind == "own" else kc_s
                            pe.matmul(ps[:, BANKS[j % 3], 0:T], k[b:b + DK, jt * P:(jt + 1) * P], q_s[b:b + DK, :],
                                      start=True, stop=True).then_inc(pe_a.sem, 1)

                        score(0)
                        score(1)
                        for j in range(NJ):
                            if j + 2 < NJ:
                                score(j + 2)
                            if c > 0 and j == 0:
                                mean(x, c - 1)
                            if c > 0 and j == min(2, NJ - 1):
                                variance(x, c - 1)
                            pe.wait_ge(dve_c.sem, dve_c.at(NJ * x + (NJ * c + j + 1)))
                            last = pe.matmul(ps[:, 2 + 3 * h, 0:T], v_s[:, j, h * P:(h + 1) * P], prob[:, j % 3, 0:T],
                                             start=j == 0, stop=j == NJ - 1)
                        last.then_inc(pe_b.sem, 1)

                    over_heads(pe, step)
                    mean(0, 7)
                    variance(0, 7)

                @block.vector
                def _(dve):
                    def stage_pair(x, c):
                        if c > 0:
                            dve.wait_ge(pe_b.sem, pe_b.at(x + c))
                        at = (T // 2) * x + T * (c // 2)
                        at_v = 128 * x + 128 * c
                        dve.tensor_copy(q_s, qk[:, ds(at, T)])
                        dve.tensor_copy(k_s, qk[:, ds(at + 4 * T, T)])
                        last = dve.tensor_copy(v_s[:, 0:nt, :], v[:, :, ds(at_v, 256)])
                        if s == "X":
                            dve.tensor_copy(kc_s, ctx_k.rearrange("p a b -> p (a b)")[:, ds(at_v, 256)])
                            last = dve.tensor_copy(v_s[:, nt:nt + 2, :], ctx_v[:, :, ds(at_v, 256)])
                        last.then_inc(staged.sem, 2)

                    def centre(x, c):
                        dve.wait_ge(mean_ready.sem, mean_ready.at(x + (c + 1)))
                        dve.tensor_tensor(o_c, o_s, ps[:, 3, 0:T], ALU.subtract).then_inc(dve_b.sem, 1)

                    def end(x, c):
                        dve.wait_ge(root_ready.sem, root_ready.at(x + (c + 1)))
                        dve.reciprocal(rs, rs)
                        dve.drain()
                        dve.tensor_tensor(o_c, o_c, rs, ALU.mult)
                        dve.drain()
                        gh = g[:, ds(T * x + T * c, T)]
                        dve.scalar_tensor_tensor(gh, o_c, gn[:, ds(x + c, 1)], gh, ALU.mult, ALU.mult)
                        dve.drain()

                    def make_exponents(x, c):
                        dve.tensor_scalar(back, lag, lg[:, ds(x + (8 + c), 1)], -1.0, ALU.mult, ALU.mult)
                        dve.drain()
                        dve.scalar_tensor_tensor(tables[c % 2], lag, lg[:, ds(x + c, 1)], back, ALU.mult, ALU.min)\
                           .then_inc(exponents.sem, 1)

                    def complete(x, c):
                        dve.wait_ge(act_a.sem, act_a.at(x + (c + 1)))
                        diagonal = tables[c % 2][:, 384:512]
                        dve.tensor_tensor(diagonal, diagonal, ident, ALU.add)
                        if s == "X":
                            dve.tensor_tensor(tables_c[c % 2], ec[:, 0, :], ec[:, 1, :], ALU.add)
                        dve.drain()

                    def step(x, c):
                        if c % 2 == 0:
                            stage_pair(x, c)
                        table, table_c = tables[c % 2], tables_c[c % 2]
                        for j, (kind, jt) in enumerate(tiles):
                            dve.wait_ge(pe_a.sem, pe_a.at(NJ * x + (NJ * c + j + 1)))
                            if kind == "own":
                                w = table[:, 384 - 128 * jt:384 - 128 * jt + T]
                            else:
                                w = table_c[:, 128 - 128 * jt:128 - 128 * jt + T]
                            dve.scalar_tensor_tensor(prob[:, j % 3, 0:T], ps[:, BANKS[j % 3], 0:T], SC, w, ALU.mult, ALU.mult)\
                               .then_inc(dve_c.sem, 1)
                            if c > 1 and j == 1:
                                end(x, c - 2)
                            if c > 0 and j == 1:
                                centre(x, c - 1)
                            if c < 7 and j == min(2, NJ - 1):
                                make_exponents(x, c + 1)
                        if c < 7:
                            complete(x, c + 1)

                    dve.wait_ge(consts_in.sem, consts_in.at(32))
                    make_exponents(0, 0)
                    complete(0, 0)
                    over_heads(dve, step)
                    end(0, 6)
                    centre(0, 7)
                    end(0, 7)
            consts_in.add(32)
            for c in (act_a, act_b, root_ready, pe_b, dve_b, mean_ready, var_ready, squared, exponents, staged):
                c.add(HEADS)
            pe_a.add(8 * NJ)
            dve_c.add(8 * NJ)

        def stage_conformer(s, m):
            T = m["T"]
            a = m["rest"]
            hs = area(a, 12, T)
            tmp, sq, rs = area(a + 6144, 4, T), area(a + 8192, 4, T), area(a + 10240, T)
            sg = sq
            part = area(a + 10752, T)
            g = m["g"].rearrange("p (a t) -> p a t", t=T)
            mg = m["merged"].rearrange("p a t -> p (a t)")
            hc = m["hc"]
            cp_flat = m["cp"].rearrange("p a b -> p (a b)")
            step = T + 2 * HALF
            w, b = par_of("cdw"), par_of("cdb")
            lng, lnb = par_of("clg"), par_of("clb")

            with nc.Block() as block:
                @block.sync
                def _(sp):
                    sp.dma_start(m["fwd"].rearrange("p a b c -> p (a b c)"), m["k_dft"][0]).then_inc(consts_in.sem, 16)
                    load_ahead(sp, 16)

                @block.tensor
                def _(pe):
                    def merge_block(i, k):
                        pe.wait_ge(loaded[k].sem, loaded[k].at(16 * i + 16))
                        pe.wait_ge(bank_free.sem, bank_free.at(4 * i + (k + 1)))
                        x = m["u"] if k % 2 == 0 else g
                        for kc in range(KC):
                            last = pe.matmul(ps[:, k, 0:T], ring[:, k, kc * P:(kc + 1) * P], x[:, kc, :],
                                             start=kc == 0, stop=kc == KC - 1)
                        last.then_inc(blocks_done.sem, 1)

                    def mean_of(bank, x):
                        for c in range(CT4):
                            last = pe.matmul(ps[:, bank, 0:T], mean_c, x[:, c, :], start=c == 0, stop=c == CT4 - 1)
                        last.then_inc(pe_a.sem, 1)

                    with pe.Fori(0, 3) as i:
                        for k in range(4):
                            merge_block(i, k)
                    merge_block(3, 0)
                    merge_block(3, 1)
                    pe.wait_ge(dve_a.sem, dve_a.at(1))
                    mean_of(4, hc)
                    merge_block(3, 2)
                    pe.wait_ge(act_a.sem, act_a.at(1))
                    mean_of(5, sq)
                    merge_block(3, 3)

                @block.scalar
                def _(act):
                    def gate(i, k):
                        act.wait_ge(blocks_done.sem, blocks_done.at(4 * i + (k + 1)))
                        act.wait_ge(bank_free.sem, bank_free.at(4 * i + (k + 1)))
                        act.activation(tmp[:, k, :], ps[:, k, 0:T], ACT.Sigmoid).then_inc(gate_ready.sem, 1)

                    with act.Fori(0, 3) as i:
                        for k in (0, 2):
                            gate(i, k)
                    gate(3, 0)
                    act.wait_ge(dve_a.sem, dve_a.at(2))
                    act.activation(sq, hc, ACT.Square).then_inc(act_a.sem, 1)
                    act.wait_ge(pe_a.sem, pe_a.at(2))
                    act.activation(rs, ps[:, 5, 0:T], ACT.Sqrt, bias=eps).then_inc(root_ready.sem, 1)
                    gate(3, 2)
                    act.wait_ge(dve_a.sem, dve_a.at(3))
                    act.activation(sg, hc, ACT.Sigmoid).then_inc(act_a.sem, 1)

                @block.vector
                def _(dve):
                    def merge(i, k):
                        dve.wait_ge(blocks_done.sem, blocks_done.at(4 * i + (k + 1)))
                        dve.wait_ge(gate_ready.sem, gate_ready.at(2 * i + (k + 1) // 2))
                        dve.tensor_tensor(mg[:, ds(2 * T * i + (k // 2) * T, T)], ps[:, k, 0:T], tmp[:, k - 1, :], ALU.mult)\
                           .then_inc(bank_free.sem, 2)

                    def taps(first, n):
                        for tap in range(n):
                            dve.drain()
                            for c in range(CT4):
                                dve.scalar_tensor_tensor(hc[:, c, :], cp_flat[:, ds(first + (tap + c * step), T)],
                                                         w[:, ds(first + (tap + c * TAPS), 1)], hc[:, c, :], ALU.mult, ALU.add)

                    for c in range(CT4):
                        dve.tensor_scalar(hc[:, c, :], m["cp"][:, c, 0:T], w[:, c * TAPS:c * TAPS + 1], b[:, c:c + 1], ALU.mult, ALU.add)
                    taps(1, 3)
                    with dve.Fori(0, 3) as i:
                        taps(9 * i + 4, 5)
                        merge(i, 1)
                        taps(9 * i + 9, 4)
                        merge(i, 3)
                    dve.drain().then_inc(dve_a.sem, 1)
                    merge(3, 1)
                    dve.wait_ge(pe_a.sem, pe_a.at(1))
                    dve.tensor_tensor(hc, hc, ps[:, 4, 0:T].unsqueeze(1).broadcast_to([P, 4, T]), ALU.subtract).then_inc(dve_a.sem, 1)
                    dve.wait_ge(root_ready.sem, root_ready.at(1))
                    dve.reciprocal(rs, rs)
                    dve.drain()
                    dve.tensor_tensor(hc, hc, rs.unsqueeze(1).broadcast_to([P, 4, T]), ALU.mult)
                    dve.drain()
                    for c in range(CT4):
                        last = dve.tensor_scalar(hc[:, c, :], hc[:, c, :], lng[:, c:c + 1], lnb[:, c:c + 1], ALU.mult, ALU.add)
                    last.then_inc(dve_a.sem, 1)
                    merge(3, 3)
                    dve.wait_ge(act_a.sem, act_a.at(2))
                    dve.tensor_tensor(hc, hc, sg, ALU.mult)

                @block.gpsimd
                def _(pool):
                    w, b = par_of("hsw"), par_of("hsb")
                    for c in range(12):
                        pool.tensor_scalar(hs[:, c, :], m["hp"][:, c, 0:T], w[:, c:c + 1], b[:, c:c + 1], ALU.mult, ALU.add)
                    for tap in (1, 2):
                        for c in range(12):
                            pool.drain()
                            pool.tensor_scalar(part, m["hp"][:, c, tap:tap + T], w[:, tap * 12 + c:tap * 12 + c + 1], None, ALU.mult)
                            pool.drain()
                            pool.tensor_tensor(hs[:, c, :], hs[:, c, :], part, ALU.add)
            consts_in.add(16)
            pe_a.add(2)
            root_ready.add(1)
            act_a.add(2)
            dve_a.add(3)
            gate_ready.add(8)
            streamed(16, 16)

        def stage_hyena(s, m):
            T, nt = m["T"], m["nt"]
            a = m["rest"]
            hs = area(a, 12, T)
            hs_flat = area(a, 12 * T)
            y = area(a + 6144, nt, 2, 512)
            tmp = area(a + 10240, 2, 512)
            spec = m["hp_flat"][:, 0:nt * 1024].rearrange("p (k r c) -> p k r c", r=2, c=512)
            ztm = m["hp_flat"][:, 4096:4096 + nt * 512].rearrange("p (a b) -> p a b", b=512)
            fwd, k_dft = m["fwd"], m["k_dft"]
            inv = area(M0 + 12288, nt, 2, T)
            bias = par_of("hbias")
            z = hs[:, 0:4, :]
            with nc.Block() as block:
                @block.sync
                def _(sp):
                    sp.dma_start(inv.rearrange("p a b c -> p (a b c)"), k_dft[1]).then_inc(consts_in.sem, 16)
                    for o in range(2):
                        if o == 1:
                            sp.wait_ge(dve_a.sem, dve_a.at(1))
                        sp.dma_start(spec.rearrange("p k r c -> p (k r c)"), spec_d[SEG[s], o, :, 0:nt * 1024])\
                          .then_inc(gates_in[0].sem, 16)

                @block.vector
                def _(dve):
                    with dve.Fori(0, 2) as o:
                        for n in range(nt):
                            dve.wait_ge(pe_a.sem, pe_a.at(nt * o + (n + 1)))
                            dve.tensor_copy(ztm[:, n, :], ps[:, n % 4, :]).then_inc(dve_b.sem, 1)
                        dve.wait_ge(gates_in[0].sem, gates_in[0].at(16 * o + 16))
                        for k in range(nt):
                            dve.wait_ge(pe_b.sem, pe_b.at((nt + 4) * o + (k + 1)))
                            zr, zi = ps[:, 4 + 2 * (k % 2), :], ps[:, 5 + 2 * (k % 2), :]
                            dve.tensor_tensor(y[:, k, 0, :], zr, spec[:, k, 0, :], ALU.mult)
                            dve.tensor_tensor(tmp[:, 0, :], zi, spec[:, k, 1, :], ALU.mult)
                            dve.tensor_tensor(y[:, k, 1, :], zr, spec[:, k, 1, :], ALU.mult)
                            dve.tensor_tensor(tmp[:, 1, :], zi, spec[:, k, 0, :], ALU.mult)
                            dve.drain()
                            dve.tensor_tensor(y[:, k, 0, :], y[:, k, 0, :], tmp[:, 0, :], ALU.subtract)
                            last = dve.tensor_tensor(y[:, k, 1, :], y[:, k, 1, :], tmp[:, 1, :], ALU.add)
                            last.then_inc(dve_b.sem, 1)
                            dve.drain()
                        dve.drain().then_inc(dve_a.sem, 1)
                        for c in range(4):
                            dve.wait_ge(pe_b.sem, pe_b.at((nt + 4) * o + (nt + c + 1)))
                            zc = z[:, c, :]
                            dve.scalar_tensor_tensor(zc, zc, bias[:, ds(4 * o + c, 1)], ps[:, c, 0:T], ALU.mult, ALU.add)
                            dve.drain()
                            dve.tensor_tensor(zc, zc, hs_flat[:, ds(4 * T * o + (4 + c) * T, T)], ALU.mult).then_inc(dve_c.sem, 1)

                @block.tensor
                def _(pe):
                    pe.wait_ge(consts_in.sem, consts_in.at(0))
                    with pe.Fori(0, 2) as o:
                        pe.wait_ge(dve_c.sem, dve_c.at(4 * o))
                        for n in range(nt):
                            for c in range(4):
                                last = pe.transpose(ps[:, n % 4, c * P:(c + 1) * P], z[:, c, n * P:(n + 1) * P], ident)
                            last.then_inc(pe_a.sem, 1)
                        pe.wait_ge(dve_b.sem, dve_b.at(2 * nt * o + nt))
                        for k in range(nt):
                            if k >= 2:
                                pe.wait_ge(dve_b.sem, dve_b.at(2 * nt * o + (nt + k - 1)))
                            for r in range(2):
                                for n in range(nt):
                                    last = pe.matmul(ps[:, 4 + 2 * (k % 2) + r, :], fwd[:, n, r, k * P:(k + 1) * P], ztm[:, n, :],
                                                     start=n == 0, stop=n == nt - 1)
                            last.then_inc(pe_b.sem, 1)
                        pe.wait_ge(consts_in.sem, consts_in.at(16))
                        pe.wait_ge(dve_b.sem, dve_b.at(2 * nt * o + 2 * nt))
                        for c in range(4):
                            for k in range(nt):
                                for r in range(2):
                                    last = pe.matmul(ps[:, c, 0:T], y[:, k, r, c * P:(c + 1) * P], inv[:, k, r, :],
                                                     start=k == r == 0, stop=(k, r) == (nt - 1, 1))
                            last.then_inc(pe_b.sem, 1)
            consts_in.add(16)
            gates_in[0].add(32)
            pe_a.add(2 * nt)
            pe_b.add(2 * (nt + 4))
            dve_a.add(2)
            dve_b.add(4 * nt)
            dve_c.add(8)

        def stage_merge_others(s, m):
            T = m["T"]
            z = area(m["rest"], 12, T)[:, 0:4, :]
            tmp = area(m["rest"] + 6144, 4, T)
            part = area(m["rest"] + 8192, 4, T)
            mg = m["merged"].rearrange("p a t -> p (a t)")
            u_hi, u_lo, hi2 = m["merge_split"]
            hc_hi, hc_lo, z_hi, z_lo = m["branch_split"]
            with nc.Block() as block:
                @block.sync
                def _(sp):
                    load_ahead(sp, 24)

                @block.tensor
                def _(pe):
                    def merge_block(i, n):
                        k, c, kind = n % 4, n // 3, n % 3
                        pe.wait_ge(block_lo.sem, block_lo.at(12 * i + (n + 1)))
                        w = (hi2[:, k % 2, :], ring_lo[:, k, :])

                        def product(bank, x, first):
                            for j in range(len(x[0])):
                                at = slice((first + j) * P, (first + j + 1) * P)
                                last = pe_products(pe, ps[:, bank, 0:T], [v[:, at] for v in w], [v[j] for v in x],
                                                   j == 0, j == len(x[0]) - 1)
                            return last

                        def chunks(hi, lo):
                            return [[v[:, j, :] for j in range(v.shape[1])] for v in (hi, lo)]

                        if kind < 2:
                            pe.wait_ge(bank_free.sem, bank_free.at(12 * i + (3 * c + 1)))
                            last = product(2 * (c % 2) + kind, chunks(u_hi, u_lo), 0)
                        else:
                            if c == 0 and n == 2:
                                pe.wait_ge(dve_a.sem, dve_a.at(3))
                            product(4 + 2 * (c % 2), chunks(hc_hi, hc_lo), 0)
                            last = product(5 + 2 * (c % 2), chunks(z_hi, z_lo), 4)
                        last.then_inc(blocks_done.sem, 1)

                    pe.wait_ge(dve_a.sem, dve_a.at(1))
                    with pe.Fori(0, 2) as i:
                        for n in range(12):
                            merge_block(i, n)

                @block.scalar
                def _(act):
                    def gate(i, n):
                        if n % 3 < 2:
                            c, kind = n // 3, n % 3
                            act.wait_ge(blocks_done.sem, blocks_done.at(12 * i + (n + 1)))
                            act.activation(tmp[:, 2 * (c % 2) + kind, :], ps[:, 2 * (c % 2) + kind, 0:T], ACT.Sigmoid)\
                               .then_inc(gate_ready.sem, 1)

                    act_round(act, m["u"], u_hi)
                    act_round_block(act, hi2, 0, 0, 0)
                    act_round(act, m["hc"], hc_hi)
                    act_round(act, z, z_hi)
                    for i in range(2):
                        for n in range(12):
                            if 12 * i + n < 23:
                                act_round_block(act, hi2, 12 * i, 0, n + 1)
                            gate(i, n)

                @block.vector
                def _(dve):
                    def merge(i, c):
                        dve.wait_ge(gate_ready.sem, gate_ready.at(8 * i + (2 * c + 2)))
                        dve.wait_ge(blocks_done.sem, blocks_done.at(12 * i + (3 * c + 3)))
                        for r in range(2):
                            dve.tensor_tensor(part[:, 2 * (c % 2) + r, :], ps[:, 4 + 2 * (c % 2) + r, 0:T], tmp[:, 2 * (c % 2) + r, :], ALU.mult)
                        dve.drain()
                        dve.tensor_tensor(part[:, 2 * (c % 2), :], part[:, 2 * (c % 2), :], part[:, 2 * (c % 2) + 1, :], ALU.add)
                        dve.drain()
                        x = mg[:, ds(4 * T * i + c * T, T)]
                        dve.tensor_tensor(x, x, part[:, 2 * (c % 2), :], ALU.add).then_inc(bank_free.sem, 3)

                    dve_rest(dve, m["u"], u_hi, u_lo, 0)
                    dve_rest_block(dve, hi2, 0, 0)
                    dve_rest(dve, m["hc"], hc_hi, hc_lo, 8)
                    dve_rest(dve, z, z_hi, z_lo, 12)
                    for i in range(2):
                        for n in range(12):
                            if 12 * i + n < 23:
                                dve_rest_block(dve, hi2, 12 * i, n + 1)
                            if n % 3 == 2:
                                merge(i, n // 3)
            gate_ready.add(16)
            act_a.add(16)
            dve_a.add(3)
            block_hi.add(24)
            block_lo.add(24)
            streamed(24, 24)

        def stage_linear(s, x, split, evacuate):
            T = T_OF[s]
            x_hi, x_lo, hi2 = split
            with nc.Block() as block:
                @block.sync
                def _(sp):
                    load_ahead(sp, 8)

                @block.tensor
                def _(pe):
                    pe.wait_ge(dve_a.sem, dve_a.at(1))
                    pe_split_linear(pe, hi2, 0, 0, 8, (x_hi, x_lo), T)

                @block.scalar
                def _(act):
                    act_round(act, x, x_hi)
                    skewed(act, 8, lambda j, k: act_round_block(act, hi2, j, 0, k), lambda i, k: None, False, False)

                @block.vector
                def _(dve):
                    def keep(i, k):
                        dve.wait_ge(blocks_done.sem, blocks_done.at(4 * i + (k + 1)))
                        evacuate(dve, i, k).then_inc(bank_free.sem, 1)

                    dve_rest(dve, x, x_hi, x_lo, 0)
                    skewed(dve, 8, lambda j, k: dve_rest_block(dve, hi2, j, k), keep, False, False)
            act_a.add(KC)
            dve_a.add(1)
            block_hi.add(8)
            block_lo.add(8)
            streamed(8, 8)

        mod_flat = mod.rearrange("p a b -> p (a b)")

        def stage_out(s, m):
            T = T_OF[s]

            def add(dve, i, k):
                x = res_flat[s][:, ds(4 * T * i + k * T, T)]
                gate = mod_flat[:, ds(8 * i + (2 * (16 + k) + SEG[s]), 1)]
                return dve.scalar_tensor_tensor(x, ps[:, k, 0:T], gate, x, ALU.mult, ALU.add)

            stage_linear(s, m["merged"], m["merge_split"], add)

        def mixer(l, s):
            m = both[s]
            stage_norm(s, 0, m["u"], area(m["rest"], T_OF[s]))
            stage_project(s, m, True)
            if s == "X":
                stage_rope(m)
            stage_retention(s, m)
            stage_conformer(s, m)
            stage_hyena(s, m)
            stage_merge_others(s, m)
            stage_out(s, m)

        TOK = SEQ + CTX
        off = {"X": 0, "C": SEQ}
        ht = area(M0, KC, TOK)
        acc = area(M0 + 6144, KC, TOK)
        acc_flat = area(M0 + 6144, KC * TOK)
        gate_block = area(M0 + 12288, NK, P)
        qp = area(M0 + 28672, 8 * SEQ)
        keys_sb = area(M0 + 32768, 8, 256)
        small = M0 + 34816

        def stage_select(l, s, with_ada):
            T = T_OF[s]
            nt = T // P
            q_s = area(small, 8, P)
            top = area(small + 1024, 8, 2, TOPK)
            top_i = area(small + 1280, 8, 2, TOPK)
            top_u = top_i.bitcast(U32)
            top_f = area(small + 1536, 8, 2, TOPK)
            best = area(small + 1792, 8, TOPK)
            best_u = area(small + 1920, 8, TOPK).bitcast(U32)
            half_u = area(small + 2048, 2, 128).bitcast(U32)
            half_f = area(small + 2304, 2, 8, TOPK)
            picked = area(small + 2560, 3, 128)
            picked_t = area(small + 2944, 3, 128)
            total = area(small + 3328, 8)
            a = M0 + 6144
            sc, sc2, cand = area(a, 8, 2, NK), area(a + 2048, 8, 2, NK), area(a + 4096, 8, 256)
            cand2 = area(M0 + 12288, 8, 256)
            hot_i, hot_j = (area(a + 2048 * n, 2, 8 * NK) for n in range(2))
            hot_i, hot_j = (v.rearrange("p g (t n) -> p g t n", n=NK) for v in (hot_i, hot_j))
            match = area(a, 8, TOPK, TOPK)
            q3 = qp[:, 0:8 * T].rearrange("p (h t) -> p h t", t=T)
            iota16 = iota[:, 0:TOPK].unsqueeze(1).unsqueeze(1).broadcast_to([P, 8, TOPK, TOPK])

            with nc.Block() as block:
                @block.sync
                def _(sp):
                    sp.dma_start(keys_sb.rearrange("p a b -> p (a b)"), keys[l]).then_inc(consts_in.sem, 16)

                    def store(tt):
                        sp.wait_ge(act_b.sem, act_b.at(32 * tt + 32))
                        sp.dma_start(gate_d[:, :, ds(P * tt + off[s], P)].rearrange("i p t -> p i t"), gate_block)\
                          .then_inc(store_done.sem, 16)

                    def load(tt, n, source):
                        sp.wait_ge(blocks_done.sem, blocks_done.at(12 * tt + (n + 1)))
                        sp.dma_start(ring[:, n % 4, :], source).then_inc(loaded[n % 4].sem, 16)

                    if with_ada:
                        with sp.Fori(0, nt - 1) as tt:
                            for n in range(12):
                                load(tt, n, ada[l + 1, ds(12 * tt + (n + 4), 1)].rearrange("o p n -> p (o n)"))
                            store(tt)
                        for n in range(12):
                            load(nt - 1, n, block_of(order[place[0] + 4 + 12 * (nt - 1) + n]))
                        store(nt - 1)
                    else:
                        with sp.Fori(0, nt) as tt:
                            store(tt)

                @block.tensor
                def _(pe):
                    pe.wait_ge(consts_in.sem, consts_in.at(16))
                    with pe.Fori(0, nt) as tt:
                        pe.wait_ge(dve_a.sem, dve_a.at(2 * tt + 1))
                        pe.wait_ge(act_b.sem, act_b.at(32 * tt))
                        for h in range(8):
                            last = pe.matmul(ps[:, h // 2, (h % 2) * 256:(h % 2) * 256 + 256], q_s[:, h, :], keys_sb[:, h, :],
                                             start=True, stop=True)
                        last.then_inc(pe_a.sem, 1)
                        if with_ada:
                            pe_ada(pe, 3 * tt)
                        pe.wait_ge(dve_a.sem, dve_a.at(2 * tt + 2))
                        for n in range(3):
                            last = pe.transpose(ps[:, 4, n * P:(n + 1) * P], picked[:, n, :], ident)
                        last.then_inc(pe_a.sem, 1)
                        with pe.Fori(0, P // 16) as pair:
                            for g in range(2):
                                pe.wait_ge(dve_b.sem, dve_b.at(32 * tt + 4 * pair + (2 * g + 2)))
                                pe.wait_ge(pool_a.sem, pool_a.at(16 * tt + 2 * pair + (g + 1)))
                                for q in range(8):
                                    if q % 4 == 0:
                                        pe.wait_ge(act_b.sem, act_b.at(32 * tt + 4 * pair + (2 * g + q // 4 - 3)))
                                    pe.matmul(ps[:, 2 * g + q // 4, (q % 4) * P:(q % 4 + 1) * P], hot_j[:, g, q, :],
                                              hot_i[:, g, q, :], start=True, stop=True).then_inc(pe_b.sem, 1)

                @block.scalar
                def _(act):
                    with act.Fori(0, nt) as tt:
                        act.wait_ge(pe_a.sem, pe_a.at(2 * tt + 1))
                        act.activation(sc.rearrange("p a b c -> p (a b c)"), ps[:, 0:4, :].rearrange("p a b -> p (a b)"), ACT.Copy)\
                           .then_inc(act_a.sem, 1)
                        if with_ada:
                            act_ada(act, 3 * tt)
                        act.wait_ge(dve_c.sem, dve_c.at(tt + 1))
                        act.activation(best, best, ACT.Exp).then_inc(act_a.sem, 1)
                        act.wait_ge(store_done.sem, store_done.at(16 * tt))
                        with act.Fori(0, P // 16) as pair:
                            for q in range(4):
                                act.wait_ge(pe_b.sem, pe_b.at(P * tt + 16 * pair + (4 * q + 4)))
                                act.activation(gate_block[:, :, ds(16 * pair + 4 * q, 4)],
                                               ps[:, q, :].rearrange("p (t i) -> p i t", t=4), ACT.Copy).then_inc(act_b.sem, 1)

                @block.vector
                def _(dve):
                    with dve.Fori(0, nt) as tt:
                        dve.tensor_copy(q_s, q3[:, :, ds(P * tt, P)]).then_inc(dve_a.sem, 1)
                        dve.wait_ge(act_a.sem, act_a.at(2 * tt + 1))
                        dve.memset(total, 0.0)
                        for h in range(8):
                            for r in range(2):
                                dve.max(top[:, h, r, 0:8], sc[:, h, r, :])
                        dve.drain()
                        for h in range(8):
                            for r in range(2):
                                dve.match_replace(sc2[:, h, r, :], top[:, h, r, 0:8], sc[:, h, r, :], LOW)
                                dve.max_index(top_u[:, h, r, 0:8], top[:, h, r, 0:8], sc[:, h, r, :])
                        dve.drain()
                        for h in range(8):
                            for r in range(2):
                                dve.max(top[:, h, r, 8:16], sc2[:, h, r, :])
                        dve.drain()
                        for h in range(8):
                            for r in range(2):
                                dve.max_index(top_u[:, h, r, 8:16], top[:, h, r, 8:16], sc2[:, h, r, :])
                        dve.tensor_tensor(cand.rearrange("p h (a b) -> p h a b", b=TOPK),
                                          top[:, :, 0, :].unsqueeze(3).broadcast_to([P, 8, TOPK, TOPK]),
                                          top[:, :, 1, :].unsqueeze(2).broadcast_to([P, 8, TOPK, TOPK]), ALU.add)
                        dve.drain()
                        dve.wait_ge(store_done.sem, store_done.at(16 * tt))
                        dve.tensor_copy(top_f, top_u)
                        for h in range(8):
                            dve.max(best[:, h, 0:8], cand[:, h, :])
                        dve.drain()
                        for h in range(8):
                            dve.match_replace(cand2[:, h, :], best[:, h, 0:8], cand[:, h, :], LOW)
                            dve.max_index(best_u[:, h, 0:8], best[:, h, 0:8], cand[:, h, :])
                        dve.drain()
                        for h in range(8):
                            dve.max(best[:, h, 8:16], cand2[:, h, :])
                        dve.drain()
                        for h in range(8):
                            dve.max_index(best_u[:, h, 8:16], best[:, h, 8:16], cand2[:, h, :])
                        dve.tensor_copy(total, best[:, :, 0])
                        dve.drain()
                        dve.tensor_tensor(best, best, total.unsqueeze(2).broadcast_to([P, 8, TOPK]), ALU.subtract)\
                           .then_inc(dve_c.sem, 1)
                        flat_u = best_u.rearrange("p h k -> p (h k)")
                        dve.tensor_scalar(half_u[:, 0, :], flat_u, 4, None, ALU.logical_shift_right)
                        dve.tensor_scalar(half_u[:, 1, :], flat_u, 15, None, ALU.bitwise_and)
                        dve.drain()
                        dve.tensor_copy(half_f.rearrange("p r h k -> p r (h k)"), half_u)
                        dve.drain()
                        for r in range(2):
                            dve.tensor_tensor(match, half_f[:, r].unsqueeze(3).broadcast_to([P, 8, TOPK, TOPK]), iota16, ALU.is_equal)
                            dve.drain()
                            dve.tensor_tensor(match, match, top_f[:, :, r, :].unsqueeze(2).broadcast_to([P, 8, TOPK, TOPK]), ALU.mult)
                            dve.drain()
                            dve.tensor_reduce(picked[:, r, :].rearrange("p (h k) -> p h k", k=TOPK), match, AX.X, ALU.add)
                            dve.drain()
                        dve.wait_ge(act_a.sem, act_a.at(2 * tt + 2))
                        dve.tensor_reduce(total, best, AX.X, ALU.add)
                        dve.drain()
                        dve.reciprocal(total, total)
                        dve.drain()
                        dve.tensor_tensor(picked[:, 2, :].rearrange("p (h k) -> p h k", k=TOPK), best,
                                          total.unsqueeze(2).broadcast_to([P, 8, TOPK]), ALU.mult).then_inc(dve_a.sem, 1)
                        dve.wait_ge(pe_a.sem, pe_a.at(2 * tt + 2))
                        dve.tensor_copy(picked_t.rearrange("p a b -> p (a b)"), ps[:, 4, 0:384])
                        dve.drain()
                        pick_i, pick_j, pick_g = (picked_t[:, n, :] for n in range(3))
                        iota8 = iota.unsqueeze(1).broadcast_to([P, 8, NK])
                        with dve.Fori(0, P // 16) as pair:
                            for g in range(2):
                                dve.wait_ge(pe_b.sem, pe_b.at(P * tt + 16 * pair + (8 * g - 8)))
                                for hot, pick in ((hot_i, pick_i), (hot_j, pick_j)):
                                    dve.tensor_tensor(hot[:, g], iota8, pick[:, ds(16 * pair + 8 * g, 8)].unsqueeze(2).broadcast_to([P, 8, NK]),
                                                      ALU.is_equal).then_inc(dve_b.sem, 1)
                        dve.wait_ge(pe_b.sem, pe_b.at(P * tt + P))
                    if with_ada:
                        dve_ada(dve)

                @block.gpsimd
                def _(pool):
                    with pool.Fori(0, nt) as tt:
                        with pool.Fori(0, P // 16) as pair:
                            for g in range(2):
                                pool.wait_ge(dve_b.sem, dve_b.at(32 * tt + 4 * pair + (2 * g + 1)))
                                pool.tensor_tensor(hot_i[:, g], hot_i[:, g],
                                                   picked_t[:, 2, ds(16 * pair + 8 * g, 8)].unsqueeze(2).broadcast_to([P, 8, NK]),
                                                   ALU.mult).then_inc(pool_a.sem, 1)
            consts_in.add(16)
            store_done.add(16 * nt)
            pe_a.add(2 * nt)
            pe_b.add(P * nt)
            act_a.add(2 * nt)
            act_b.add(32 * nt)
            dve_a.add(2 * nt)
            dve_b.add(32 * nt)
            pool_a.add(16 * nt)
            if with_ada:
                counted_ada()
            dve_c.add(nt)

        h_hi = split_tensor("h_hi", M0 + 28672, KC, TOK)
        h_lo = split_tensor("h_lo", M0, KC, TOK)
        u_ring_hi = split_tensor("u_ring_hi", M0 + 34816, 2, 1024)
        v_ring_hi = split_tensor("v_ring_hi", M0 + 12288, 2, 1024)
        w_hi = split_tensor("w_hi", M0 + 14336, 2, TOK)
        w_lo = split_tensor("w_lo", M0 + 15872, 2, TOK)

        query_split = {s: (split_tensor("q_hi" + s, M0 + 6144, KC, T_OF[s]), split_tensor("q_lo" + s, at, KC, T_OF[s]),
                           split_tensor("q_ring_hi" + s, M0 + 10240, 2, 1024)) for s, at in (("X", M0 + 12288), ("C", M0 + 8192))}

        def ring_hi(slot):
            return (u_ring_hi, v_ring_hi)[slot // 2][:, slot % 2, :]

        def stage_split(T):
            with nc.Block() as block:
                @block.scalar
                def _(act):
                    for kc in range(KC):
                        act.activation(h_hi[:, kc, 0:T], ht[:, kc, 0:T], ACT.Copy).then_inc(act_a.sem, 1)

                @block.vector
                def _(dve):
                    for kc in range(KC):
                        dve.wait_ge(act_a.sem, act_a.at(kc + 1))
                        dve.tensor_tensor(h_lo[:, kc, 0:T], ht[:, kc, 0:T], h_hi[:, kc, 0:T].bitcast(F32), ALU.subtract)
            act_a.add(KC)

        def stage_experts(l, segs):
            T = sum(T_OF[s] for s in segs)
            halves = [(0, T // 2), (T // 2, T // 2)]
            gt = area(M0 + 17408, 2, 2, TOK)
            w = area(M0 + 20480, 2, TOK)
            N = NK // 2
            kinds = order[place[0] + 4:place[0] + 8]

            with nc.Block() as block:
                @block.sync
                def _(sp):
                    def load_u(n, k):
                        for r in range(2):
                            sp.wait_ge(pe_a.sem, pe_a.at(2 * n + (2 * k + r - 1)))
                            sp.dma_start(ring[:, r, :], peer_u[l, ds(2 * n + (2 * k + r), 1)].rearrange("o p n -> p (o n)"))\
                              .then_inc(loaded[r].sem, 16)

                    def load_v(n, k):
                        sp.wait_ge(pe_b.sem, pe_b.at(8 * n + 8 * k))
                        for r in range(2):
                            sp.dma_start(ring[:, 2 + r, :], peer_v[l, ds(2 * n + (2 * k + r), 1)].rearrange("o p n -> p (o n)"))\
                              .then_inc(loaded[2 + r].sem, 16)

                    def load_gates(n, k):
                        sp.dma_start(gt[:, k % 2, :, 0:T], gate_d[ds(2 * n + 2 * k, 2), :, 0:T].rearrange("i p t -> p i t"))\
                          .then_inc(gates_in[k % 2].sem, 16)

                    sp.wait_ge(store_done.sem, store_done.at(0))
                    load_gates(0, 0)
                    load_gates(0, 1)
                    load_u(0, 1)
                    with sp.Fori(0, (N - 2) // 2) as pair:
                        n = 2 * pair
                        for k in range(2):
                            load_u(n, k + 2)
                            sp.wait_ge(w_ready.sem, w_ready.at(2 * n + (2 * k + 2)))
                            load_gates(n, k + 2)
                            load_v(n, k + 1)
                    load_v(N - 2, 1)
                    for k, entry in enumerate(kinds):
                        if k < 2:
                            sp.wait_ge(pe_a.sem, pe_a.at(2 * N - 1 + k))
                        else:
                            sp.wait_ge(pe_b.sem, pe_b.at(8 * N))
                        sp.dma_start(ring[:, k, :], block_of(entry)).then_inc(loaded[k].sem, 16)

                @block.tensor
                def _(pe):
                    def a_of(n, k):
                        for r in range(2):
                            pe.wait_ge(u_split.sem, u_split.at(2 * n + (2 * k + r + 1)))
                            pe.wait_ge(act_a.sem, act_a.at(2 * n + (2 * k + r - 1)))
                            for p, (t0, t) in enumerate(halves):
                                for kc in range(KC):
                                    c = slice(kc * P, (kc + 1) * P)
                                    last = pe_products(pe, ps[:, 2 * r + p, 0:t], (ring_hi(r)[:, c], ring_lo[:, r, c]),
                                                    (h_hi[:, kc, t0:t0 + t], h_lo[:, kc, t0:t0 + t]), kc == 0, kc == KC - 1)
                            last.then_inc(pe_a.sem, 1)

                    def o_of(n, k):
                        pe.wait_ge(v_split.sem, v_split.at(2 * n + (2 * k + 2)))
                        pe.wait_ge(w_ready.sem, w_ready.at(2 * n + (2 * k + 2)))
                        for dc in range(KC):
                            pe.wait_ge(dve_c.sem, dve_c.at(8 * n + (8 * k + dc - 1)))
                            c = slice(dc * P, (dc + 1) * P)
                            for p, (t0, t) in enumerate(halves):
                                for r in range(2):
                                    last = pe_products(pe, ps[:, 4 + 2 * (dc % 2) + p, 0:t], (ring_hi(2 + r)[:, c], ring_lo[:, 2 + r, c]),
                                                    (w_hi[:, r, t0:t0 + t], w_lo[:, r, t0:t0 + t]), r == 0, r == 1)
                            last.then_inc(pe_b.sem, 1)

                    a_of(0, 0)
                    with pe.Fori(0, (N - 2) // 2) as pair:
                        n = 2 * pair
                        for k in range(2):
                            a_of(n, k + 1)
                            o_of(n, k)
                    a_of(N - 2, 1)
                    o_of(N - 2, 0)
                    o_of(N - 2, 1)

                @block.scalar
                def _(act):
                    def round_block(n, k, first):
                        for r in range(2):
                            slot = first + r
                            act.wait_ge(loaded[slot].sem, loaded[slot].at(16 * n + (16 * k + 16)))
                            act.activation(ring_hi(slot), ring[:, slot, :], ACT.Copy)\
                               .then_inc((u_hi if first == 0 else v_hi).sem, 1)

                    def gelu(n, k):
                        for r in range(2):
                            act.wait_ge(pe_a.sem, pe_a.at(2 * n + (2 * k + r + 1)))
                            act.wait_ge(w_ready.sem, w_ready.at(2 * n + 2 * k))
                            act.activation(w[:, r, 0:T].rearrange("p (a b) -> p a b", a=2), ps[:, 2 * r:2 * r + 2, 0:T // 2],
                                           ACT.Gelu_apprx_tanh).then_inc(act_a.sem, 1)

                    round_block(0, 0, 0)
                    act.wait_ge(store_done.sem, store_done.at(0))
                    round_block(0, 0, 2)
                    gelu(0, 0)
                    round_block(0, 1, 0)
                    with act.Fori(0, (N - 2) // 2) as pair:
                        n = 2 * pair
                        for k in range(2):
                            gelu(n, k + 1)
                            round_block(n, k + 2, 0)
                            round_block(n, k + 1, 2)
                    gelu(N - 2, 1)
                    round_block(N - 2, 1, 2)

                @block.vector
                def _(dve):
                    def rest_of_block(n, k, first, r):
                        hi, done = (u_hi, u_split) if first == 0 else (v_hi, v_split)
                        slot = first + r
                        dve.wait_ge(hi.sem, hi.at(2 * n + (2 * k + r + 1)))
                        dve.tensor_tensor(ring_lo[:, slot, :], ring[:, slot, :], ring_hi(slot).bitcast(F32), ALU.subtract)\
                           .then_inc(done.sem, 1)

                    def weigh(n, k):
                        dve.wait_ge(gates_in[k % 2].sem, gates_in[k % 2].at(8 * n + (16 * (k // 2) + 16)))
                        for r in range(2):
                            dve.wait_ge(act_a.sem, act_a.at(2 * n + (2 * k + r + 1)))
                            dve.tensor_tensor(w[:, r, 0:T], w[:, r, 0:T], gt[:, k % 2, r, 0:T], ALU.mult)
                        dve.drain()
                        for r in range(2):
                            dve.tensor_copy(w_hi[:, r, 0:T], w[:, r, 0:T])
                        dve.drain()
                        for r in range(2):
                            dve.tensor_tensor(w_lo[:, r, 0:T], w[:, r, 0:T], w_hi[:, r, 0:T].bitcast(F32), ALU.subtract)\
                               .then_inc(w_ready.sem, 1)

                    def gather(n, k, dc):
                        dve.wait_ge(pe_b.sem, pe_b.at(8 * n + (8 * k + dc + 1)))
                        x = acc[:, dc, 0:T].rearrange("p (a b) -> p a b", a=2)
                        b = 4 + 2 * (dc % 2)
                        dve.tensor_tensor(x, x, ps[:, b:b + 2, 0:T // 2], ALU.add).then_inc(dve_c.sem, 1)

                    def step(n, k, more):
                        for dc in range(KC):
                            gather(n, k, dc)
                            if more and dc in (4, 5):
                                rest_of_block(n, k + 2, 0, dc - 4)
                        weigh(n, k + 1)
                        for r in range(2):
                            rest_of_block(n, k + 1, 2, r)

                    dve.memset(acc_flat, 0.0)
                    for first in (0, 2):
                        for r in range(2):
                            rest_of_block(0, 0, first, r)
                    weigh(0, 0)
                    for r in range(2):
                        rest_of_block(0, 1, 0, r)
                    with dve.Fori(0, (N - 2) // 2) as pair:
                        n = 2 * pair
                        for k in range(2):
                            step(n, k, True)
                    step(N - 2, 0, False)
                    for dc in range(KC):
                        gather(N - 2, 1, dc)
                    dve.drain()
                    for s in segs:
                        for kc in range(KC):
                            x = res[s][:, kc, :]
                            dve.scalar_tensor_tensor(x, acc[:, kc, off[s]:off[s] + T_OF[s]], mod[:, 40 + kc, SEG[s]:SEG[s] + 1], x,
                                                     ALU.mult, ALU.add)
            for k in range(4):
                loaded[k].add(16 * N)
            place[0] += 4
            for c in (pe_a, act_a, u_hi, v_hi, u_split, v_split, w_ready):
                c.add(2 * N)
            pe_b.add(8 * N)
            dve_c.add(8 * N)
            for g in gates_in:
                g.add(16 * N // 2)

        def peer(l, segs):
            for s in segs:
                x = ht[:, :, off[s]:off[s] + T_OF[s]]
                stage_norm(s, 1, x, area(small, T_OF[s]))

                def keep(dve, i, k, T=T_OF[s]):
                    return dve.tensor_copy(qp[:, ds(4 * T * i + k * T, T)], ps[:, k, 0:T])

                stage_linear(s, x, query_split[s], keep)
                stage_select(l, s, l < DEPTH - 1 and s == "X")
            T = sum(T_OF[s] for s in segs)
            stage_split(T)
            stage_experts(l, segs)

        stage_ada()
        for l in range(DEPTH):
            last = l == DEPTH - 1
            stage_modulation(l)
            if not last:
                stage_filters(l, "C")
            stage_filters(l, "X")
            if not last:
                mixer(l, "C")
            else:
                m = both["C"]
                stage_norm("C", 0, m["u"], area(m["rest"], CTX))
                stage_project("C", m, False)
            mixer(l, "X")
            peer(l, ("X",) if last else ("X", "C"))
        m = both["X"]
        stage_norm("X", 2, m["u"], area(m["rest"], SEQ))
        with nc.Block() as block:
            @block.sync
            def _(sp):
                sp.dma_start(out, m["u"].rearrange("p a b -> p (a b)")).then_inc(store_done.sem, 16)
                sp.wait_ge(store_done.sem, store_done.at(16))


def _chunks(a):
    a = np.asarray(a)
    return np.swapaxes(a.reshape(a.shape[:-1] + (a.shape[-1] // P, P)), -1, -2)


def _tokens(a):
    return np.ascontiguousarray(np.asarray(a).T.reshape(KC, P, -1).transpose(1, 0, 2).reshape(P, -1))


def _blocks(w):
    w = np.asarray(w)
    n = w.shape[1] // P
    return w.reshape(KC, P, n, P).transpose(2, 1, 0, 3).reshape(n, P, KC * P)


def _constants():
    f = np.float32
    mats = np.zeros((P, 7, P), f)
    mats[:, 0] = np.eye(P)
    for m in range(0, P, 2):
        mats[m + 1, 1, m] = -1.0
        mats[m, 1, m + 1] = 1.0
    mats[:, 2], mats[:, 3], mats[:, 4], mats[:, 5] = 1.0 / D, 1.0 / CW, 1.0 / DV, 1.0
    mats[:, 6] = np.arange(P)
    t = np.arange(SEQ)
    nf = DK // 4
    inv = (10000.0 ** (-np.arange(nf, dtype=f) / f(nf))).astype(f)
    ang = np.concatenate([(t // GRID_W).astype(f)[:, None] * inv, (t % GRID_W).astype(f)[:, None] * inv], 1)
    pair = (np.arange(P) % DK) // 2
    rope = np.stack([np.cos(ang)[:, pair].T, np.sin(ang)[:, pair].T]).astype(f)
    lag = np.arange(896)[None, :] - 384 - np.arange(P)[:, None]
    c, p = np.arange(640)[None, :], np.arange(P)[:, None]
    decc = np.stack([c - p + CTX - 128, SEQ + 128 - c + p], 1).astype(f)
    got = dict(mats=mats.reshape(P, -1), rope=rope, dec=lag.astype(f), decc=decc.reshape(P, -1))
    for s, L in (("x", SEQ), ("c", CTX)):
        tt = np.arange(L, dtype=f)
        tn = tt / f(L - 1)
        w = f(2.0 * math.pi) * tt / f(L)
        bands = np.linspace(1e-4, 15, 16, dtype=f)
        feat = np.concatenate([tn[:, None], np.cos(w[:, None] * bands), -np.sin(w[:, None] * bands)], 1)
        got["feat_" + s] = np.ascontiguousarray(feat.T.astype(f))
        deltas = np.abs(np.linspace(math.log(1e-2) / 1.5, math.log(1e-2) / 0.3, HW, dtype=f))
        win = np.exp(-tn[:, None] * deltas[None, :]).astype(f)
        win2 = np.stack([win, win], 1)
        win2[0, 1] = 0.0
        got["win_" + s] = np.ascontiguousarray(win2.reshape(L // P, P, 2 * HW).transpose(1, 0, 2).reshape(P, -1))
        ph = np.pi * np.outer(np.arange(L), np.arange(L) + 0.5) / L
        tab = np.stack([np.cos(ph), -np.sin(ph)], 1)
        back = np.stack([np.cos(ph).T, -np.sin(ph).T], 1)
        got["dft_" + s] = np.stack([x.reshape(L // P, P, 2 * L).transpose(1, 0, 2).reshape(P, -1) for x in (tab, back)]).astype(f)
    return got


def kernel(x, c, ctx, c_ctx, ada_w, ada_b, norm1_g, norm2_g, w_in, ret_decay_logit, ret_gn_g, w_br_ret, conf_dw_w,
           conf_dw_b, conf_ln_g, conf_ln_b, w_br_conf, hy_short_w, hy_short_b, hy_w1, hy_b1, hy_freq, hy_w2, hy_b2,
           hy_w3, hy_b3, hy_bias, w_br_hy, w_out, peer_wq, peer_keys, peer_u, peer_v, final_g):
    import concourse.bacc as bacc
    from concourse.bass_utils import run_bass_kernel_spmd

    A = np.asarray
    x, c, ctx, c_ctx, w_in = A(x), A(c), A(ctx), A(c_ctx), A(w_in)
    mix, par, keys = [], [], []
    for l in range(DEPTH):
        wb = _blocks(w_in[l])
        ret, conf_hy = _blocks(w_br_ret[l]), _blocks(np.concatenate([A(w_br_conf[l]), A(w_br_hy[l])], 0))
        conf, hy, gate = wb[24:32], wb[32:44], wb[44:68]
        order = list(wb[0:24])
        for n in range(4):
            order += [conf[n], conf[4 + n]]
        order += list(hy)
        for n in range(8):
            order += [gate[n], ret[n]]
        for n in range(8):
            order += [gate[8 + n], gate[16 + n], conf_hy[n]]
        order += list(_blocks(w_out[l])) + list(_blocks(peer_wq[l]))
        mix.append(np.stack(order))
        mlp = np.zeros((P, 3), np.float32)
        mlp[0:HID, 0], mlp[0:HID, 1], mlp[0:HID, 2] = A(hy_b1[l]), A(hy_freq[l]), A(hy_b2[l])
        logit = np.broadcast_to(A(ret_decay_logit[l]).reshape(1, 16), (P, 16))
        cdw = _chunks(conf_dw_w[l]).transpose(1, 2, 0).reshape(P, -1)
        hsw = _chunks(hy_short_w[l]).transpose(1, 0, 2).reshape(P, -1)
        hb = _chunks(hy_bias[l]).transpose(1, 0, 2).reshape(P, -1)
        parts = dict(n1=_chunks(norm1_g[l]), n2=_chunks(norm2_g[l]), ada_b=_chunks(ada_b[l]), gn=_chunks(ret_gn_g[l]),
                     cdw=cdw, cdb=_chunks(conf_dw_b[l]), clg=_chunks(conf_ln_g[l]), clb=_chunks(conf_ln_b[l]),
                     hsw=hsw, hsb=_chunks(hy_short_b[l]), hbias=hb, logit=logit, mlp=mlp)
        par.append(np.concatenate([parts[n] for n in _cols], 1))
        kk = np.zeros((P, 8, 256), np.float32)
        for r in range(2):
            kk[64 * r:64 * r + 64, :, 128 * r:128 * r + 128] = A(peer_keys[l])[:, r].transpose(2, 0, 1)
        keys.append(kk.reshape(P, -1))
    k = _constants()
    arrays = {
        "xT": _tokens(x[0]), "cT": np.stack([_chunks(c[0]), _chunks(c_ctx)], 2).reshape(P, 16),
        "ctxT": _tokens(ctx[0]), "final_g": _chunks(final_g),
        "ada": np.stack([_blocks(ada_w[l]) for l in range(DEPTH)]), "mix": np.stack(mix),
        "peer_u": A(peer_u).reshape(DEPTH, NK, P, KC, P).transpose(0, 1, 4, 3, 2).reshape(DEPTH, NK, P, D),
        "peer_v": A(peer_v).reshape(DEPTH, NK, P, D), "par": np.stack(par),
        "hw1": A(hy_w1), "hw2": A(hy_w2),
        "hw3": np.concatenate([A(hy_w3), A(hy_b3)[:, None, :]], 1), "keys": np.stack(keys),
        "k_mats": k["mats"], "k_rope": k["rope"], "k_dec": k["dec"], "k_decc": k["decc"],
        "k_feat_x": k["feat_x"], "k_feat_c": k["feat_c"], "k_win_x": k["win_x"], "k_win_c": k["win_c"],
        "k_dft_x": k["dft_x"], "k_dft_c": k["dft_c"],
    }
    arrays = {n: np.ascontiguousarray(a) for n, a in arrays.items()}
    nc = bacc.Bacc("TRN2", target_bir_lowering=False, num_devices=1)
    args = {n: nc.dram_tensor("in_" + n, a.shape, mybir.dt.from_np(a.dtype), kind="ExternalInput").ap()
            for n, a in arrays.items()}
    out = nc.dram_tensor("out_0", (P, KC * SEQ), F32, kind="ExternalOutput").ap()
    build(nc, out=out, **args)
    r = run_bass_kernel_spmd(nc, [{"in_" + n: a for n, a in arrays.items()}], core_ids=[0])
    got = np.asarray(r.results[0]["out_0"])
    return np.ascontiguousarray(got.reshape(P, KC, SEQ).transpose(2, 1, 0).reshape(1, SEQ, D))
```
